# Optimizing a Trainium2 kernel written in Bass

```python
import math
import jax, jax.numpy as jnp
from jax import lax
import numpy as np

D_MODEL = 1024
BATCH = 1
SEQ = 256
DEPTH = 1

HEAD_DIM = 64
ROPE_THETA = 10000.0
EPS = 1e-6
NEG_INF = -1e30

DIL_GROUPS = ((128, 1), (512, 4), (2048, 16))
N_DIL_GROUPS = 3
DIL_HEADS_PER_GROUP = 4
DIL_HEADS = N_DIL_GROUPS * DIL_HEADS_PER_GROUP
DIL_WIDTH = DIL_HEADS * HEAD_DIM
DIL_OUT = DIL_HEADS_PER_GROUP * HEAD_DIM

DIFF_HEADS = D_MODEL // (2 * HEAD_DIM)
DIFF_QK_WIDTH = DIFF_HEADS * 2 * HEAD_DIM
DIFF_V_WIDTH = DIFF_HEADS * 2 * HEAD_DIM
DIFF_Q_BLOCK = 128

N_BRANCHES = 2
GATE_WIDTH = N_BRANCHES * D_MODEL
IN_WIDTH = 3 * DIL_WIDTH + 2 * DIFF_QK_WIDTH + DIFF_V_WIDTH + GATE_WIDTH
IN_SPLITS = (DIL_WIDTH, 2 * DIL_WIDTH, 3 * DIL_WIDTH,
             3 * DIL_WIDTH + DIFF_QK_WIDTH,
             3 * DIL_WIDTH + 2 * DIFF_QK_WIDTH,
             3 * DIL_WIDTH + 2 * DIFF_QK_WIDTH + DIFF_V_WIDTH)

PEER_HEADS = 8
PEER_N_KEYS = 128
PEER_N_EXPERTS = PEER_N_KEYS * PEER_N_KEYS
PEER_TOPK = 16
PEER_QUERY_DIM = 256
PEER_HALF = PEER_QUERY_DIM // 2
PEER_CHUNK = 128


def rms_norm(x, g):
    xf = x.astype(jnp.float32)
    y = xf * lax.rsqrt(jnp.mean(xf * xf, axis=-1, keepdims=True) + EPS)
    return (y * g.astype(jnp.float32)).astype(x.dtype)

def rope(x, positions):
    hd = x.shape[-1]
    inv_freq = 1.0 / (ROPE_THETA ** (jnp.arange(0, hd, 2, dtype=jnp.float32) / hd))
    ang = positions.astype(jnp.float32)[:, :, None, None] * inv_freq
    cos, sin = jnp.cos(ang), jnp.sin(ang)
    xf = x.astype(jnp.float32)
    x1, x2 = xf[..., : hd // 2], xf[..., hd // 2:]
    return jnp.concatenate([x1 * cos - x2 * sin, x2 * cos + x1 * sin], axis=-1).astype(x.dtype)

def dilated_window_attention(q, k, v, window, dilation):
    b, s, h, hd = q.shape
    m = window // (2 * dilation)
    blk = m
    L = s // dilation
    nb = -(-L // blk)
    Lp = nb * blk

    def to_res(t):
        return t.reshape(b, L, dilation, h, hd).transpose(0, 2, 3, 1, 4)

    qr = jnp.pad(to_res(q), ((0, 0), (0, 0), (0, 0), (0, Lp - L), (0, 0)))
    kpad = ((0, 0), (0, 0), (0, 0), (blk, Lp - L + blk), (0, 0))
    kp = jnp.pad(to_res(k), kpad)
    vp = jnp.pad(to_res(v), kpad)
    qb = qr.reshape(b, dilation, h, nb, blk, hd)

    def band(t):
        tb = t.reshape(b, dilation, h, nb + 2, blk, hd)
        return jnp.concatenate([tb[:, :, :, :-2], tb[:, :, :, 1:-1], tb[:, :, :, 2:]], axis=4)

    kb, vb = band(kp), band(vp)
    scores = jnp.einsum('brhnqc,brhnkc->brhnqk', qb, kb).astype(jnp.float32) * (hd ** -0.5)
    qi = jnp.arange(nb)[:, None, None] * blk + jnp.arange(blk)[None, :, None]
    ki = jnp.arange(nb)[:, None, None] * blk - blk + jnp.arange(3 * blk)[None, None, :]
    mask = (jnp.abs(ki - qi) <= m) & (ki >= 0) & (ki < L)
    scores = jnp.where(mask, scores, NEG_INF)
    lse = jax.nn.logsumexp(scores, axis=-1)
    p = jnp.exp(scores - lse[..., None])
    out = jnp.einsum('brhnqk,brhnkc->brhnqc', p.astype(v.dtype), vb)
    out = out.reshape(b, dilation, h, Lp, hd)[:, :, :, :L]
    out = out.transpose(0, 3, 1, 2, 4).reshape(b, s, h, hd)
    lse = lse.reshape(b, dilation, h, Lp)[..., :L].transpose(0, 3, 1, 2).reshape(b, s, h)
    return out, lse

def differential_attention(q1, q2, k1, k2, v, lam):
    b, s, h, hd = q1.shape
    nqb = s // DIFF_Q_BLOCK
    scale = hd ** -0.5

    def blockify(t):
        return t.reshape(b, nqb, DIFF_Q_BLOCK, h, hd).transpose(1, 0, 2, 3, 4)

    def one_block(qs):
        qa, qb = qs
        s1 = jnp.einsum('bqhc,bkhc->bhqk', qa, k1).astype(jnp.float32) * scale
        s2 = jnp.einsum('bqhc,bkhc->bhqk', qb, k2).astype(jnp.float32) * scale
        a = jax.nn.softmax(s1, axis=-1) - lam * jax.nn.softmax(s2, axis=-1)
        return jnp.einsum('bhqk,bkhc->bqhc', a.astype(v.dtype), v)

    out = lax.map(one_block, (blockify(q1), blockify(q2)))
    return out.transpose(1, 0, 2, 3, 4).reshape(b, s, h, 2 * hd)

def peer_ffn(h, w_query, sub_keys, expert_u, expert_v):
    b, s, d = h.shape
    tokens = h.reshape((b * s) // PEER_CHUNK, PEER_CHUNK, d)

    def chunk(xc):
        q = (xc @ w_query).reshape(PEER_CHUNK, PEER_HEADS, 2, PEER_HALF)
        s1 = jnp.einsum('thc,hnc->thn', q[:, :, 0], sub_keys[:, 0]).astype(jnp.float32)
        s2 = jnp.einsum('thc,hnc->thn', q[:, :, 1], sub_keys[:, 1]).astype(jnp.float32)
        v1, i1 = lax.top_k(s1, PEER_TOPK)
        v2, i2 = lax.top_k(s2, PEER_TOPK)
        cand = (v1[..., :, None] + v2[..., None, :]).reshape(PEER_CHUNK, PEER_HEADS, PEER_TOPK * PEER_TOPK)
        top, ci = lax.top_k(cand, PEER_TOPK)
        e1 = jnp.take_along_axis(i1, ci // PEER_TOPK, axis=-1)
        e2 = jnp.take_along_axis(i2, ci % PEER_TOPK, axis=-1)
        eidx = e1 * PEER_N_KEYS + e2
        gate = jax.nn.softmax(top, axis=-1)
        u = expert_u[eidx]
        vv = expert_v[eidx]
        act = jax.nn.gelu(jnp.einsum('td,thkd->thk', xc, u).astype(jnp.float32), approximate=False)
        wts = (gate * act).astype(xc.dtype)
        return jnp.einsum('thk,thkd->td', wts, vv)

    return lax.map(chunk, tokens).reshape(b, s, d)

def hybrid_layer(x, c, positions, lam_init, w_ada, b_ada, norm1_g, w_in, b_gate,
                 qn_a, kn_a, w_proj_a, qn_b, kn_b, lam_q1, lam_k1, lam_q2, lam_k2,
                 subln_g, w_proj_b, w_out, norm2_g, w_query, sub_keys, expert_u, expert_v):
    b, s, d = x.shape
    mod = jax.nn.silu(c) @ w_ada + b_ada
    sh1, sc1, g1, sh2, sc2, g2 = [m[:, None, :] for m in jnp.split(mod, 6, axis=-1)]

    h = rms_norm(x, norm1_g) * (1 + sc1) + sh1
    proj = h @ w_in
    qa, ka, va, qb, kb, vb, gl = jnp.split(proj, IN_SPLITS, axis=-1)

    qa = rope(rms_norm(qa.reshape(b, s, DIL_HEADS, HEAD_DIM), qn_a), positions)
    ka = rope(rms_norm(ka.reshape(b, s, DIL_HEADS, HEAD_DIM), kn_a), positions)
    va = va.reshape(b, s, DIL_HEADS, HEAD_DIM)
    outs, lses = [], []
    for gi, (win, dil) in enumerate(DIL_GROUPS):
        sl = slice(gi * DIL_HEADS_PER_GROUP, (gi + 1) * DIL_HEADS_PER_GROUP)
        o, l = dilated_window_attention(qa[:, :, sl], ka[:, :, sl], va[:, :, sl], win, dil)
        outs.append(o)
        lses.append(l)
    wg = jax.nn.softmax(jnp.stack(lses), axis=0)
    oa = jnp.sum(wg[..., None] * jnp.stack(outs).astype(jnp.float32), axis=0).astype(x.dtype)
    branch_a = oa.reshape(b, s, DIL_OUT) @ w_proj_a

    qb = rms_norm(qb.reshape(b, s, DIFF_HEADS, 2, HEAD_DIM), qn_b)
    kb = rms_norm(kb.reshape(b, s, DIFF_HEADS, 2, HEAD_DIM), kn_b)
    q1, q2 = rope(qb[:, :, :, 0], positions), rope(qb[:, :, :, 1], positions)
    k1, k2 = rope(kb[:, :, :, 0], positions), rope(kb[:, :, :, 1], positions)
    f32 = jnp.float32
    lam = (jnp.exp(jnp.sum(lam_q1.astype(f32) * lam_k1.astype(f32)))
           - jnp.exp(jnp.sum(lam_q2.astype(f32) * lam_k2.astype(f32))) + lam_init)
    ob = differential_attention(q1, q2, k1, k2, vb.reshape(b, s, DIFF_HEADS, 2 * HEAD_DIM), lam)
    ob = rms_norm(ob, subln_g) * (1.0 - lam_init)
    branch_b = ob.reshape(b, s, DIFF_V_WIDTH) @ w_proj_b

    gates = jax.nn.sigmoid((gl + b_gate).astype(f32)).astype(x.dtype).reshape(b, s, N_BRANCHES, d)
    mixed = gates[:, :, 0] * branch_a + gates[:, :, 1] * branch_b
    x = x + g1 * (mixed @ w_out)

    h2 = rms_norm(x, norm2_g) * (1 + sc2) + sh2
    x = x + g2 * peer_ffn(h2, w_query, sub_keys, expert_u, expert_v)
    return x

def first_inputs(seed: int = 0) -> dict:
    key = jax.random.key(seed)
    ks = jax.random.split(key, 32)
    f32 = jnp.float32

    def nrm(k, shape, scale):
        return jax.random.normal(k, shape, f32) * scale

    def gain(k, shape):
        return 1.0 + 0.02 * jax.random.normal(k, shape, f32)

    L = DEPTH
    D = D_MODEL
    return {
        "x": jax.random.normal(ks[0], (BATCH, SEQ, D), f32),
        "c": jax.random.normal(ks[1], (BATCH, D), f32),
        "positions": jnp.broadcast_to(jnp.arange(SEQ, dtype=jnp.int32), (BATCH, SEQ)),
        "w_ada": nrm(ks[2], (L, D, 6 * D), 0.5 * D ** -0.5),
        "b_ada": nrm(ks[3], (L, 6 * D), 0.02),
        "norm1_g": gain(ks[4], (L, D)),
        "w_in": nrm(ks[5], (L, D, IN_WIDTH), D ** -0.5),
        "b_gate": nrm(ks[6], (L, GATE_WIDTH), 0.02),
        "qn_a": gain(ks[7], (L, HEAD_DIM)),
        "kn_a": gain(ks[8], (L, HEAD_DIM)),
        "w_proj_a": nrm(ks[9], (L, DIL_OUT, D), DIL_OUT ** -0.5),
        "qn_b": gain(ks[10], (L, HEAD_DIM)),
        "kn_b": gain(ks[11], (L, HEAD_DIM)),
        "lam_q1": nrm(ks[12], (L, HEAD_DIM), 0.1),
        "lam_k1": nrm(ks[13], (L, HEAD_DIM), 0.1),
        "lam_q2": nrm(ks[14], (L, HEAD_DIM), 0.1),
        "lam_k2": nrm(ks[15], (L, HEAD_DIM), 0.1),
        "subln_g": gain(ks[16], (L, 2 * HEAD_DIM)),
        "w_proj_b": nrm(ks[17], (L, DIFF_V_WIDTH, D), DIFF_V_WIDTH ** -0.5),
        "w_out": nrm(ks[18], (L, D, D), D ** -0.5),
        "norm2_g": gain(ks[19], (L, D)),
        "w_query": nrm(ks[20], (L, D, PEER_HEADS * PEER_QUERY_DIM), D ** -0.5),
        "sub_keys": nrm(ks[21], (L, PEER_HEADS, 2, PEER_N_KEYS, PEER_HALF), PEER_HALF ** -0.5),
        "expert_u": nrm(ks[22], (L, PEER_N_EXPERTS, D), D ** -0.5),
        "expert_v": nrm(ks[23], (L, PEER_N_EXPERTS, D), PEER_HEADS ** -0.5),
    }

def first_block(x, c, positions, w_ada, b_ada, norm1_g, w_in, b_gate, qn_a, kn_a, w_proj_a,
              qn_b, kn_b, lam_q1, lam_k1, lam_q2, lam_k2, subln_g, w_proj_b, w_out,
              norm2_g, w_query, sub_keys, expert_u, expert_v):
    for l in range(DEPTH):
        lam_init = 0.8 - 0.6 * math.exp(-0.3 * l)
        x = hybrid_layer(x, c, positions, lam_init, w_ada[l], b_ada[l], norm1_g[l], w_in[l],
                         b_gate[l], qn_a[l], kn_a[l], w_proj_a[l], qn_b[l], kn_b[l],
                         lam_q1[l], lam_k1[l], lam_q2[l], lam_k2[l], subln_g[l], w_proj_b[l],
                         w_out[l], norm2_g[l], w_query[l], sub_keys[l], expert_u[l], expert_v[l])
    return x


CHUNK = 64
D_MIX = D_MODEL
CONV_WIDTH = D_MIX // 2
CONV_GROUPS = 8
CONV_K = 3
HGRN_WIDTH = D_MIX - CONV_WIDTH
HGRN_HEADS = 4
HGRN_DK = HGRN_WIDTH // HGRN_HEADS
HGRN_DV = HGRN_WIDTH // HGRN_HEADS
N_PROJ_SLOTS = 7
PROJ_WIDTH = 3 * CONV_WIDTH + 4 * HGRN_WIDTH
MEM_LEN = 256
XATTN_HEADS = 4
XATTN_HEAD_DIM = D_MODEL // XATTN_HEADS
N_GROUPS = 4
EXPERTS_PER_GROUP = 4
N_EXPERTS = N_GROUPS * EXPERTS_PER_GROUP
TOPK_IN_GROUP = 2
D_EXPERT = D_MODEL // 2


def rms_norm_2(x, g):
    xf = x.astype(jnp.float32)
    y = xf * lax.rsqrt(jnp.mean(xf * xf, axis=-1, keepdims=True) + EPS)
    return (y * g.astype(jnp.float32)).astype(x.dtype)

def hgrn2_chunkwise(q, k, v, log_f):
    bsz, seq, heads, dk = q.shape
    dv = v.shape[-1]
    n_chunks = seq // CHUNK

    def to_chunks(t):
        return t.reshape(bsz, n_chunks, CHUNK, heads, t.shape[-1]).transpose(1, 0, 3, 2, 4)

    tri = jnp.tril(jnp.ones((CHUNK, CHUNK), dtype=bool))

    def step(state, inp):
        qc, kc, vc, ac = inp
        b = jnp.cumsum(ac, axis=2)
        diff = b[:, :, :, None, :] - b[:, :, None, :, :]
        decay = jnp.exp(jnp.where(tri[None, None, :, :, None], diff, -jnp.inf))
        scores = jnp.einsum('bhtsk,bhsk->bhts', qc[:, :, :, None, :] * decay, kc)
        o = (jnp.einsum('bhts,bhsv->bhtv', scores, vc)
             + jnp.einsum('bhtk,bhkv->bhtv', qc * jnp.exp(b), state))
        b_last = b[:, :, -1:, :]
        state = (jnp.exp(b_last[:, :, 0, :])[..., None] * state
                 + jnp.einsum('bhsk,bhsv->bhkv', kc * jnp.exp(b_last - b), vc))
        return state, o

    s0 = jnp.zeros((bsz, heads, dk, dv), jnp.float32)
    _, o = lax.scan(step, s0, (to_chunks(q), to_chunks(k), to_chunks(v), to_chunks(log_f)))
    return o.transpose(1, 0, 3, 2, 4).reshape(bsz, seq, heads, dv)

def parallel_mixer(h, w_in, conv_w, lb, hgrn_norm, w_out):
    bsz, seq, _ = h.shape
    proj = jnp.einsum('bsd,dp->bsp', h, w_in)
    cb, cc, cx, hq, hf, hi, hg = jnp.split(proj, N_PROJ_SLOTS, axis=-1)
    u = jnp.pad(cc * cx, ((0, 0), (CONV_K - 1, 0), (0, 0)))
    conv = sum(u[:, j:j + seq] * conv_w[j] for j in range(CONV_K))
    y_a = cb * conv
    z = hf.astype(jnp.float32).reshape(bsz, seq, HGRN_HEADS, HGRN_DK)
    lbh = lb.astype(jnp.float32).reshape(HGRN_HEADS, HGRN_DK)
    log_f = jnp.log(lbh + (1.0 - lbh) * jax.nn.sigmoid(z))
    k = (1.0 - lbh) * jax.nn.sigmoid(-z)
    q = hq.astype(jnp.float32).reshape(bsz, seq, HGRN_HEADS, HGRN_DK)
    v = hi.astype(jnp.float32).reshape(bsz, seq, HGRN_HEADS, HGRN_DV)
    o = hgrn2_chunkwise(q, k, v, log_f)
    o = o * lax.rsqrt(jnp.mean(o * o, axis=-1, keepdims=True) + EPS)
    o = o * hgrn_norm.astype(jnp.float32).reshape(HGRN_HEADS, HGRN_DV)
    g = hg.astype(jnp.float32).reshape(bsz, seq, HGRN_HEADS, HGRN_DV)
    y_b = (o * jax.nn.silu(g)).reshape(bsz, seq, HGRN_WIDTH).astype(h.dtype)
    y = jnp.concatenate([y_a, y_b], axis=-1)
    return jnp.einsum('bsm,md->bsd', y, w_out)

def memory_cross_attention(h, m, w_q, w_kv, w_o):
    bsz, seq, _ = h.shape
    q = jnp.einsum('bsd,de->bse', h, w_q).reshape(bsz, seq, XATTN_HEADS, XATTN_HEAD_DIM)
    kv = jnp.einsum('bmd,de->bme', m, w_kv)
    k, v = jnp.split(kv, 2, axis=-1)
    k = k.reshape(bsz, m.shape[1], XATTN_HEADS, XATTN_HEAD_DIM)
    v = v.reshape(bsz, m.shape[1], XATTN_HEADS, XATTN_HEAD_DIM)
    s = jnp.einsum('bshd,bmhd->bhsm', q, k).astype(jnp.float32) * (XATTN_HEAD_DIM ** -0.5)
    p = jax.nn.softmax(s, axis=-1).astype(v.dtype)
    o = jnp.einsum('bhsm,bmhd->bshd', p, v).reshape(bsz, seq, D_MODEL)
    return jnp.einsum('bse,ed->bsd', o, w_o)

def hierarchical_moe(h, w_group, b_group, w_expert, b_expert, w_gate, w_up, w_down):
    bsz, seq, d = h.shape
    t = h.reshape(-1, d)
    g_prob = jax.nn.softmax((t @ w_group + b_group).astype(jnp.float32), axis=-1)
    g_p, g_idx = lax.top_k(g_prob, 1)
    e_logits = (t @ w_expert + b_expert).astype(jnp.float32).reshape(-1, N_GROUPS, EXPERTS_PER_GROUP)
    e_logits = jnp.take_along_axis(e_logits, g_idx[:, :, None], axis=1)[:, 0]
    e_prob = jax.nn.softmax(e_logits, axis=-1)
    e_p, e_idx = lax.top_k(e_prob, TOPK_IN_GROUP)
    weights = g_p * e_p / jnp.sum(e_p, axis=-1, keepdims=True)
    expert_id = g_idx * EXPERTS_PER_GROUP + e_idx
    combine = jnp.sum(jax.nn.one_hot(expert_id, N_EXPERTS, dtype=jnp.float32) * weights[..., None], axis=1)
    out = jnp.zeros(t.shape, jnp.float32)
    for e in range(N_EXPERTS):
        hid = jax.nn.silu(t @ w_gate[e]) * (t @ w_up[e])
        out = out + combine[:, e:e + 1] * (hid @ w_down[e])
    return out.astype(h.dtype).reshape(bsz, seq, d)

def second_inputs(seed: int = 0) -> dict:
    key = jax.random.key(seed)
    ks = jax.random.split(key, 24)
    f32 = jnp.float32

    def nrm(k, shape, scale):
        return jax.random.normal(k, shape, f32) * scale

    def gain(k, shape):
        return 1.0 + 0.02 * jax.random.normal(k, shape, f32)

    return {
        "x": jax.random.normal(ks[0], (BATCH, SEQ, D_MODEL), f32),
        "mem": jax.random.normal(ks[1], (BATCH, MEM_LEN, D_MODEL), f32),
        "mix_norm": gain(ks[2], (DEPTH, D_MODEL)),
        "w_in": nrm(ks[3], (DEPTH, D_MODEL, PROJ_WIDTH), D_MODEL ** -0.5),
        "conv_w": nrm(ks[4], (DEPTH, CONV_K, CONV_WIDTH), CONV_K ** -0.5),
        "hgrn_lb": jax.random.normal(ks[5], (DEPTH + 1, HGRN_WIDTH), f32),
        "hgrn_norm": gain(ks[6], (DEPTH, HGRN_WIDTH)),
        "w_out": nrm(ks[7], (DEPTH, D_MIX, D_MODEL), D_MIX ** -0.5),
        "xattn_norm": gain(ks[8], (DEPTH, D_MODEL)),
        "mem_norm": gain(ks[9], (DEPTH, D_MODEL)),
        "w_q": nrm(ks[10], (DEPTH, D_MODEL, D_MODEL), D_MODEL ** -0.5),
        "w_kv": nrm(ks[11], (DEPTH, D_MODEL, 2 * D_MODEL), D_MODEL ** -0.5),
        "w_o": nrm(ks[12], (DEPTH, D_MODEL, D_MODEL), D_MODEL ** -0.5),
        "ffn_norm": gain(ks[13], (DEPTH, D_MODEL)),
        "w_group": nrm(ks[14], (DEPTH, D_MODEL, N_GROUPS), D_MODEL ** -0.5),
        "b_group": nrm(ks[15], (DEPTH, N_GROUPS), 0.01),
        "w_expert": nrm(ks[16], (DEPTH, D_MODEL, N_EXPERTS), D_MODEL ** -0.5),
        "b_expert": nrm(ks[17], (DEPTH, N_EXPERTS), 0.01),
        "w_gate": nrm(ks[18], (DEPTH, N_EXPERTS, D_MODEL, D_EXPERT), D_MODEL ** -0.5),
        "w_up": nrm(ks[19], (DEPTH, N_EXPERTS, D_MODEL, D_EXPERT), D_MODEL ** -0.5),
        "w_down": nrm(ks[20], (DEPTH, N_EXPERTS, D_EXPERT, D_MODEL), D_EXPERT ** -0.5),
        "final_norm": gain(ks[21], (D_MODEL,)),
    }

def second_block(x, mem, mix_norm, w_in, conv_w, hgrn_lb, hgrn_norm, w_out,
              xattn_norm, mem_norm, w_q, w_kv, w_o,
              ffn_norm, w_group, b_group, w_expert, b_expert, w_gate, w_up, w_down,
              final_norm):
    lb_all = jnp.cumsum(jax.nn.softmax(hgrn_lb.astype(jnp.float32), axis=0), axis=0)
    for l in range(DEPTH):
        x = x + parallel_mixer(rms_norm_2(x, mix_norm[l]), w_in[l], conv_w[l], lb_all[l],
                               hgrn_norm[l], w_out[l])
        x = x + memory_cross_attention(rms_norm_2(x, xattn_norm[l]), rms_norm_2(mem, mem_norm[l]),
                                       w_q[l], w_kv[l], w_o[l])
        x = x + hierarchical_moe(rms_norm_2(x, ffn_norm[l]), w_group[l], b_group[l], w_expert[l],
                                 b_expert[l], w_gate[l], w_up[l], w_down[l])
    return rms_norm_2(x, final_norm)


def setup_inputs(seed=0):
    out = dict(first_inputs(seed))
    for name, value in second_inputs(seed + 1).items():
        if name != "x":
            out[name + "_2"] = value
    return out


def reference(
    x, c, positions, w_ada, b_ada, norm1_g, w_in, b_gate, qn_a, kn_a, w_proj_a, qn_b, kn_b,
    lam_q1, lam_k1, lam_q2, lam_k2, subln_g, w_proj_b, w_out, norm2_g, w_query, sub_keys,
    expert_u, expert_v, mem_2, mix_norm_2, w_in_2, conv_w_2, hgrn_lb_2, hgrn_norm_2, w_out_2,
    xattn_norm_2, mem_norm_2, w_q_2, w_kv_2, w_o_2, ffn_norm_2, w_group_2, b_group_2,
    w_expert_2, b_expert_2, w_gate_2, w_up_2, w_down_2, final_norm_2,
):
    x = first_block(
        x, c, positions, w_ada, b_ada, norm1_g, w_in, b_gate, qn_a, kn_a, w_proj_a, qn_b, kn_b,
        lam_q1, lam_k1, lam_q2, lam_k2, subln_g, w_proj_b, w_out, norm2_g, w_query, sub_keys,
        expert_u, expert_v,
    )
    return second_block(
        x, mem_2, mix_norm_2, w_in_2, conv_w_2, hgrn_lb_2, hgrn_norm_2, w_out_2, xattn_norm_2,
        mem_norm_2, w_q_2, w_kv_2, w_o_2, ffn_norm_2, w_group_2, b_group_2, w_expert_2,
        b_expert_2, w_gate_2, w_up_2, w_down_2, final_norm_2,
    )


_drawn_inputs = setup_inputs


def setup_inputs(seed=0):
    import zlib

    import numpy as np

    out = dict(_drawn_inputs(seed))
    spreads = {}
    factors = {'norm1_g': 4.375,
     'b_gate': 6.56,
     'qn_a': 7.009,
     'kn_a': 8.0,
     'qn_b': 7.135,
     'kn_b': 8.0,
     'lam_q1': 2.89,
     'lam_q2': 8.0,
     'lam_k2': 4.349,
     'subln_g': 4.967,
     'norm2_g': 2.798,
     'hgrn_norm_2': 3.943,
     'xattn_norm_2': 7.337,
     'mem_norm_2': 3.67,
     'b_group_2': 23.988,
     'b_expert_2': 45.721,
     'final_norm_2': 8.021,
     'ffn_norm_2': 7.932}
    for name, (base, spread) in spreads.items():
        noise = np.random.default_rng([zlib.crc32(name.encode()), seed]).standard_normal(out[name].shape)
        drawn = base * np.exp(spread * noise) if base else spread * noise
        out[name] = __import__('jax').numpy.asarray(drawn.astype(out[name].dtype))
    for name, factor in factors.items():
        out[name] = (out[name] * factor).astype(out[name].dtype)
    return out
```

```python
import concourse.bass as bass
from concourse import mybir
from contextlib import ExitStack
import math

P = 128
S = 256
TT = S // P
D = 1024
DC = D // P
HD = 64
A_SLOTS, A_GROUPS = 4, 3
A_HEADS = A_SLOTS * A_GROUPS
A_DIL = (1, 4, 16)
A_REACH = 64
A_W = A_HEADS * HD
B_HEADS = 8
QK_W = 2 * A_W + 2 * D
GL_W = 2 * D
V_W = A_W + D
IN_W = QK_W + GL_W + V_W
NQK = QK_W // P
QK_HEADS = QK_W // HD
EPS = 1e-6
NEG = -1e30
LAM_INIT = 0.8 - 0.6 * math.exp(0.0)
N_KEYS, PH, TOPK = 128, 8, 16
NHH = 2 * PH
CW = 512
RH = 4
SEG = 64
LEVELS = 7
XH, XD = 4, 256
N_EXP, N_GRP, PER_GRP = 16, 4, 4
FE = 512
UW = 2048
HALF = N_KEYS // 2
NI = HALF // 2

ADA_GROUPS = 6 * D // UW
U_IN = ADA_GROUPS * DC
IN_BLOCKS = IN_W // 512
U_PA = U_IN + 2 * IN_BLOCKS + 1
U_PB = U_PA + 1
U_WO = U_PB + 4
U_WQ = U_WO + 4
U_PEER = U_WQ + 8
U_MIX = U_PEER + 2 * HALF
MIX_T = 5 * CW // 256
U_WO2 = U_MIX + MIX_T + 4
U_KV = U_WO2 + 4
U_XQ = U_KV + 8
U_XO = U_XQ + 4
U_MOE = U_XO + 4
NU = U_MOE + 6 * N_EXP

T_H1, T_OA, T_OB, T_MIXED, T_H2, T_MIX, T_YB, T_MEM, T_HX, T_HF = range(10)
ROWS = {t: n + 1 for n, t in enumerate(t for t in range(10) if t != T_OA)}
T_GROUPS = [4, 1, 4, 4, 4, 4, 2, 4, 4, 4]
T_BASE = [sum(T_GROUPS[:k]) for k in range(11)]
NORM_USE = [T_H1, T_H2, T_MIX, T_MEM, T_HX, T_HF]


def hybrid_block_then_mixer_memory_moe_kernel(nc, io):
    f32, f32r = mybir.dt.float32, mybir.dt.float32r
    i32, u32 = mybir.dt.int32, mybir.dt.uint32
    ALU, ACT, AX = mybir.AluOpType, mybir.ActivationFunctionType, mybir.AxisListType

    ctx = ExitStack()
    with ctx:
        def sb(name, shape, dt=f32):
            return ctx.enter_context(nc.sbuf_tensor(name, shape, dt))

        def sem(name):
            return ctx.enter_context(nc.semaphore(name))

        raw = sb("raw", [P, 2, UW])
        whi = sb("whi", [P, 2, UW], f32r)
        wlo = sb("wlo", [P, 2, UW], f32r)
        X = sb("X", [P, TT, D])
        H = sb("H", [P, TT, D])
        thi = sb("thi", [P, DC, S], f32r)
        tlo = sb("tlo", [P, DC, S], f32r)
        MOD = sb("MOD", [P, 6 * D])
        BIG = sb("BIG", [P, 16384])
        MID = sb("MID", [P, 7168])
        phi = sb("phi", [P, 2, 512], f32r)
        plo = sb("plo", [P, 2, 512], f32r)
        ident = sb("ident", [P, P])
        iota = sb("iota", [P, S])
        SM = sb("SM", [P, 264])
        ps = ctx.enter_context(nc.psum_tensor("ps", [P, 8, 512], f32))

        used_cols = [0]

        def col(n):
            used_cols[0] += n
            return SM[:, used_cols[0] - n:used_cols[0]]

        pidx = col(1)
        pidx_i = col(1).bitcast(i32)
        cT, siluc = col(DC), col(DC)
        sumsq, meansq, std, rstd = col(TT), col(TT), col(TT), col(TT)
        pos_i, pos = col(TT).bitcast(i32), col(TT)
        lam2, lam = col(2), col(1)
        a_max, a_nmax, a_sum, a_rec = col(2), col(2), col(2), col(2)
        b_max, b_sum, b_rec = col(4), col(4), col(4)
        qk_stat = col(2 * QK_HEADS)
        ob_stat = col(TT * B_HEADS)
        conv_w = col(12)
        lb2, lb, omlb = col(2 * RH), col(RH), col(RH)

        x_max, x_sum, x_rec = col(2), col(2), col(2)
        r_stat = col(8 * TT)

        big = BIG[:, :]
        mid = MID[:, :]
        mod = MOD[:, :].rearrange("p (m d) -> p m d", m=6)
        sh1, sc1, g1, sh2, sc2, g2 = (mod[:, m, :] for m in range(6))
        ada_acc = [big[:, g * UW:(g + 1) * UW] for g in range(ADA_GROUPS)]
        b_ada_row = big[0:1, 8192:8192 + 6 * D]
        ones = big[:, 14336:14336 + P]
        proj = big[:, 0:TT * IN_W].rearrange("p (t n) -> p t n", t=TT)
        lam_vec = big[:, 14848:15104].rearrange("p (k d) -> p k d", k=4)
        qk_gain = big[:, 15104:15360].rearrange("p (k d) -> p k d", k=4)
        subln = big[:, 15360:15488]
        inv_freq = big[:, 15488:15520]
        oa = big[:, 15520:15520 + TT * 256].rearrange("p (t n) -> p t n", t=TT)
        b_gate = mid[:, 4096:4096 + GL_W]
        gain = mid[:, 6144:7168]
        masks = MOD[:, 0:1024]
        rope_c = MOD[:, 1024:1536].rearrange("p (t k d) -> p t k d", t=TT, k=4)
        rope_s = MOD[:, 1536:2048].rearrange("p (t k d) -> p t k d", t=TT, k=4)
        rot = mid[:, 0:QK_W]
        ang = mid[:, 6144:6208].rearrange("p (t d) -> p t d", t=TT)
        cos = mid[:, 6208:6272].rearrange("p (t d) -> p t d", t=TT)
        sin = mid[:, 6272:6336].rearrange("p (t d) -> p t d", t=TT)
        atmp = mid[:, 6336:6400].rearrange("p (t d) -> p t d", t=TT)
        key_i = mid[:, 6400:6656].bitcast(i32)
        mtmp_i = mid[:, 6656:6912].bitcast(i32)
        qkT = mid[:, 0:NQK * S].rearrange("p (b t) -> p b t", b=NQK)
        a_s = [big[:, i * 768:(i + 1) * 768] for i in range(2)]
        a_pT = [big[:, 1536 + i * 768:1536 + (i + 1) * 768] for i in range(2)]
        b_p = [big[:, IN_W + i * 512:IN_W + (i + 1) * 512] for i in range(2)]
        b_pT = [big[:, IN_W + 1024 + i * 256:IN_W + 1024 + (i + 1) * 256] for i in range(2)]
        b_a1 = big[:, IN_W + 1536:IN_W + 1792]
        ob_sq = big[:, 0:2048]
        mixed = big[:, 0:2048].rearrange("p (t n) -> p t n", t=TT)
        lin_tmp = mid[:, 0:512]
        qT = big[:, 0:NHH * S].rearrange("p (b t) -> p b t", b=NHH)
        keysT = big[:, 4096:4096 + NHH * N_KEYS].rearrange("p (b n) -> p b n", b=NHH)
        score = [mid[:, t * 2048:(t + 1) * 2048] for t in range(TT)]
        cand = mid[:, 4096:6144]
        top_v = MOD[:, 2048:2304].rearrange("p (b k) -> p b k", b=NHH)
        top_i = MOD[:, 2304:2560].bitcast(u32).rearrange("p (b k) -> p b k", b=NHH)
        top_f = MOD[:, 2560:2816].rearrange("p (h s k) -> p h s k", h=PH, s=2)
        best_v = MOD[:, 2816:2944].rearrange("p (h k) -> p h k", h=PH)
        best_i = MOD[:, 2944:3072].bitcast(u32).rearrange("p (h k) -> p h k", h=PH)
        half_i = MOD[:, 3072:3200].bitcast(u32)
        half_f = [MOD[:, 3200:3328], MOD[:, 3328:3456]]
        gate_e = MOD[:, 3456:3584].rearrange("p (h k) -> p h k", h=PH)
        gate_s, gate_r = MOD[:, 3584:3592], MOD[:, 3592:3600]
        route = MOD[:, 0:768].rearrange("p (t q k) -> p t q k", t=TT, q=3)
        routeT = MOD[:, 1024:1792].rearrange("p (q t) -> p q t", q=3)
        G = big
        one_a = [mid[:, i * 1024:(i + 1) * 1024].rearrange("p (t n) -> p t n", t=8) for i in range(2)]
        one_b = [mid[:, 2048 + i * 512:2048 + (i + 1) * 512].rearrange("p (t n) -> p t n", t=8) for i in range(2)]
        act_s = [mid[:, 3072 + i * 512:3072 + (i + 1) * 512] for i in range(2)]
        act_w = [mid[:, 4096 + i * 512:4096 + (i + 1) * 512] for i in range(2)]
        mixT = big[:, 0:20 * S].rearrange("p (b t) -> p b t", b=20)
        cb, cc, cx, hq, hz = (mixT[:, 4 * k:4 * k + 4, :] for k in range(5))
        hv = big[:, 5120:6144].rearrange("p (t n) -> p t n", t=TT)
        hg = big[:, 6144:7168].rearrange("p (t n) -> p t n", t=TT)
        conv_u = big[:, 7168:8192].rearrange("p (b t) -> p b t", b=4)
        conv_y = big[:, 8192:9216].rearrange("p (b t) -> p b t", b=4)
        sig = big[:, 9216:10240].rearrange("p (b t) -> p b t", b=4)
        dec = big[:, 10240:11264].rearrange("p (b t) -> p b t", b=4)
        rk = big[:, 11264:12288].rearrange("p (b t) -> p b t", b=4)
        lev_e = [big[:, 12288 + i * 1024:13312 + i * 1024].rearrange("p (b t) -> p b t", b=4) for i in range(2)]
        lev_q = big[:, 14336:15360].rearrange("p (b t) -> p b t", b=4)
        lev_k = big[:, 15360:16384].rearrange("p (b t) -> p b t", b=4)
        lmask = mid[:, 0:1024].rearrange("p (l t) -> p l t", l=8)
        lev_t = mid[:, 1024:2048].rearrange("p (t h n) -> p t h n", t=TT, h=RH)
        rsc = mid[:, 2048:3072].rearrange("p (t h n) -> p t h n", t=TT, h=RH)
        rsc_x = mid[:, 3072:3584].rearrange("p (h n) -> p h n", h=RH)
        keep = mid[:, 3584:3840]
        lint = mid[:, 3840:3968].bitcast(i32)
        lsh = mid[:, 3968:4096].bitcast(i32)
        lup = mid[:, 4096:4224]
        hnorm = mid[:, 4608:5120]
        ro = mid[:, 5120:6144].rearrange("p (t n) -> p t n", t=TT)
        mem = MOD[:, 0:2048].rearrange("p (t n) -> p t n", t=TT)
        kT = MOD[:, 2048:4096].rearrange("p (b t) -> p b t", b=DC)
        vm = MOD[:, 4096:6144].rearrange("p (t n) -> p t n", t=TT)
        xqT = big[:, 0:2048].rearrange("p (b t) -> p b t", b=DC)
        x_p = [big[:, 2048 + i * 256:2304 + i * 256] for i in range(2)]
        x_pT = [big[:, 2560 + i * 512:3072 + i * 512].rearrange("p (k t) -> p k t", k=TT) for i in range(2)]
        wr = big[:, 8192:8192 + DC * 20].rearrange("p (c n) -> p c n", c=DC)
        r_bias = big[:, 8400:8420]
        r_log = big[:, 8448:8488].rearrange("p (t n) -> p t n", t=TT)
        r_prob = big[:, 8512:8552].rearrange("p (t n) -> p t n", t=TT)
        r_cmp = big[:, 8576:8576 + TT * 80].rearrange("p (t g a b) -> p t g a b", t=TT, g=5, a=4)
        r_tie = big[:, 8768:8768 + TT * 80].rearrange("p (t g a b) -> p t g a b", t=TT, g=5, a=4)
        r_rank = big[:, 8960:9000].rearrange("p (t n) -> p t n", t=TT)
        r_sel = big[:, 9024:9064].rearrange("p (t n) -> p t n", t=TT)
        r_low = big[:, 9088:9104].rearrange("p (a b) -> p a b", a=4)
        comb = big[:, 9152:9152 + TT * N_EXP].rearrange("p (t n) -> p t n", t=TT)
        silu_g = [big[:, i * 512:(i + 1) * 512] for i in range(2)]
        hid = [big[:, 1024 + i * 512:1536 + i * 512] for i in range(2)]
        wrhi = sb("wrhi", [P, DC, 20], f32r)
        wrlo = sb("wrlo", [P, DC, 20], f32r)

        raw_loaded = [sem("raw_loaded0"), sem("raw_loaded1")]
        unit_hi, unit_split, unit_used = sem("unit_hi"), sem("unit_split"), sem("unit_used")
        x_loaded, c_loaded, rows_loaded, gain_loaded = (
            sem("x_loaded"), sem("c_loaded"), sem("rows_loaded"), sem("gain_loaded"))
        keys_loaded, mix_loaded, mem_loaded, router_loaded = (
            sem("keys_loaded"), sem("mix_loaded"), sem("mem_loaded"), sem("router_loaded"))
        pool_chain, consts_ready = sem("pool_chain"), sem("consts_ready")
        dve_chain, act_chain = sem("dve_chain"), sem("act_chain")
        siluc_ready, ones_ready = sem("siluc_ready"), sem("ones_ready")
        ada_full, ada_free = sem("ada_full"), sem("ada_free")
        x_ready, norm_ss, norm_ms, norm_std = sem("x_ready"), sem("norm_ss"), sem("norm_ms"), sem("norm_std")
        rows_ready, tr_done, tr_hi, tr_lo = sem("rows_ready"), sem("tr_done"), sem("tr_hi"), sem("tr_lo")
        acc_free, keys_scored = sem("acc_free"), sem("keys_scored")
        angles_ready, sincos_ready, lam_dots, lam_exp = (
            sem("angles_ready"), sem("sincos_ready"), sem("lam_dots"), sem("lam_exp"))
        qk_sq, qk_summed, qk_ms, qk_std, rope_done = (
            sem("qk_sq"), sem("qk_summed"), sem("qk_ms"), sem("qk_std"), sem("rope_done"))
        gate_biased, gate_ready = sem("gate_biased"), sem("gate_ready")
        qkT_done, qkT_even, qkT_odd = sem("qkT_done"), sem("qkT_even"), sem("qkT_odd")
        a_scored, a_masked, a_prob, a_tr, a_trT, a_pv, a_out = (
            sem("a_scored"), sem("a_masked"), sem("a_prob"), sem("a_tr"), sem("a_trT"), sem("a_pv"), sem("a_out"))
        b_scored, b_bias, b_prob, b_mix, b_tr, b_trT, b_pv, b_out = (
            sem("b_scored"), sem("b_bias"), sem("b_prob"), sem("b_mix"), sem("b_tr"), sem("b_trT"),
            sem("b_pv"), sem("b_out"))
        ob_sqd, ob_ms, ob_std = sem("ob_sqd"), sem("ob_ms"), sem("ob_std")
        gate_shift, gate_exp, routed, route_tr, route_in = (
            sem("gate_shift"), sem("gate_exp"), sem("routed"), sem("route_tr"), sem("route_in"))
        oh_ready, g_full, g_free = sem("oh_ready"), sem("g_full"), sem("g_free")
        gelu_done, w_done, w_hi, w_lo = sem("gelu_done"), sem("w_done"), sem("w_hi"), sem("w_lo")
        lb_diff, lb_exp, z_exp, f_ready, f_log, lev_d, lev_exp, lev_qk, lev_full, lev_free = (
            sem("lb_diff"), sem("lb_exp"), sem("z_exp"), sem("f_ready"), sem("f_log"), sem("lev_d"), sem("lev_exp"), sem("lev_qk"),
            sem("lev_full"), sem("lev_free"))
        conv_ready, conv_hi, conv_lo, sc_ready, ro_full, ro_copied, ro_sq, ro_ms, ro_std = (
            sem("conv_ready"), sem("conv_hi"), sem("conv_lo"), sem("sc_ready"), sem("ro_full"),
            sem("ro_copied"), sem("ro_sq"), sem("ro_ms"), sem("ro_std"))
        x_scored, x_bias, x_prob, x_norm, x_tr, x_trT, xo_full, xo_hi, xo_lo = (
            sem("x_scored"), sem("x_bias"), sem("x_prob"), sem("x_norm"), sem("x_tr"), sem("x_trT"),
            sem("xo_full"), sem("xo_hi"), sem("xo_lo"))
        wr_hi, wr_lo, r_full, r_ready, r_exp = (
            sem("wr_hi"), sem("wr_lo"), sem("r_full"), sem("r_ready"), sem("r_exp"))
        m_silu, m_hid, m_hi, m_lo, d_free = sem("m_silu"), sem("m_hid"), sem("m_hi"), sem("m_lo"), sem("d_free")
        out_ready, out_stored = sem("out_ready"), sem("out_stored")

        N_IN = 0
        N_PA = N_IN + 2 * (IN_BLOCKS + 1)
        N_PB = N_PA + 4
        N_WO = N_PB + 4
        N_WQ = N_WO + 4
        N_SC = N_WQ + 8
        N_MT = N_SC + 8
        N_MV = N_MT + MIX_T
        N_W2 = N_MV + 4
        N_K = N_W2 + 4
        N_V = N_K + 4
        N_XQ = N_V + 4
        N_XO = N_XQ + 4
        SPLIT_U = U_IN

        GL0, V0 = QK_W, QK_W + GL_W

        block = ctx.enter_context(nc.Block())

        @block.sync
        def _(sp):
            stream = io["stream"]
            for k in range(2):
                sp.dma_start(raw[:, k, :], stream[k, :, :]).then_inc(raw_loaded[k], 16)
            with sp.Fori(1, NU // 2) as i:
                for k in range(2):
                    sp.wait_ge(unit_split, 2 * i + (k - 1))
                    sp.dma_start(raw[:, k, :], stream[bass.ds(2 * i + k, 1), :, :].rearrange("a p n -> (a p) n")
                                 ).then_inc(raw_loaded[k], 16)
            sp.wait_ge(out_ready, 1)
            sp.dma_start(io["out"].rearrange("(t p) d -> p t d", p=P), H[:, :, :]).then_inc(out_stored, 16)
            sp.wait_ge(out_stored, 16)

        @block.gpsimd
        def _(pool):
            nc.gpsimd.iota(iota[:, :], [[1, S]], base=0, channel_multiplier=0,
                           allow_small_or_imprecise_dtypes=True).then_inc(consts_ready, 1)
            nc.gpsimd.iota(pidx, [[0, 1]], base=0, channel_multiplier=1,
                           allow_small_or_imprecise_dtypes=True).then_inc(consts_ready, 1)
            nc.gpsimd.memset(ident[:, :], 0.0).then_inc(pool_chain, 1)
            pool.wait_ge(pool_chain, 1)
            nc.gpsimd.affine_select(out=ident[:, :], in_=ident[:, :], compare_op=ALU.not_equal, fill=1.0, base=0,
                                    pattern=[[-1, P]], channel_multiplier=1).then_inc(consts_ready, 1)

            def load_gain(j):
                pool.dma_start(gain, io["gains"][j, :].partition_broadcast(P)).then_inc(gain_loaded, 16)

            load_gain(0)
            pool.wait_ge(rope_done, TT)
            pool.wait_ge(rows_ready, ROWS[T_OB])
            load_gain(1)
            pool.wait_ge(rows_ready, ROWS[T_MIXED])
            pool.dma_start(keysT, io["keysT"].rearrange("p (b n) -> p b n", b=NHH)).then_inc(keys_loaded, 16)
            pool.wait_ge(rows_ready, ROWS[T_H2])
            load_gain(2)
            pool.wait_ge(x_ready, 2)
            pool.dma_start(conv_w, io["conv_w"]).then_inc(mix_loaded, 16)
            pool.dma_start(lb2, io["hgrn_lb"]).then_inc(mix_loaded, 16)
            pool.dma_start(hnorm, io["hgrn_norm"].partition_broadcast(P)).then_inc(mix_loaded, 16)
            pool.dma_start(mem, io["mem"].rearrange("(t p) d -> p t d", p=P)).then_inc(mem_loaded, 16)
            pool.wait_ge(rows_ready, ROWS[T_MIX])
            load_gain(3)
            pool.wait_ge(rows_ready, ROWS[T_MEM])
            load_gain(4)
            pool.wait_ge(rows_ready, ROWS[T_HX])
            load_gain(5)
            pool.dma_start(wr[:, :, :], io["router"].rearrange("p (c n) -> p c n", c=DC)).then_inc(router_loaded, 16)
            pool.dma_start(r_bias, io["router_b"].partition_broadcast(P)).then_inc(router_loaded, 16)
            pool.wait_ge(rows_ready, ROWS[T_HF])
            load_gain(6)

        @block.scalar
        def _(act):
            chain = [0]

            def mark(ins):
                chain[0] += 1
                ins.then_inc(act_chain, 1)

            def settle():
                act.wait_ge(act_chain, chain[0])

            def hi(u, off=0):
                s = u - SPLIT_U
                act.wait_ge(raw_loaded[u % 2], 16 * (u // 2 + 1) + 8 * off)
                if s >= 2:
                    act.wait_ge(unit_used, s - 1 + off)
                nc.scalar.activation(whi[:, u % 2, :], raw[:, u % 2, :], ACT.Copy).then_inc(unit_hi, 1)

            def used(u, off=0):
                act.wait_ge(unit_used, u - SPLIT_U + 1 + off)

            def evac(n, u, out, func=ACT.Copy, uoff=0, width=512):
                used(u, uoff)
                nc.scalar.activation(out, ps[:, n % 4, 0:width], func).then_inc(acc_free, 1)

            def norm(j, src, ready):
                act.wait_ge(*ready)
                for t in range(TT):
                    nc.scalar.activation(H[:, t, :], src[:, t, :], ACT.Square,
                                         accum_out=sumsq[:, t:t + 1]).then_inc(norm_ss, 1)
                act.wait_ge(norm_ms, j + 1)
                nc.scalar.activation(std, meansq, ACT.Sqrt).then_inc(norm_std, 1)

            def tr_high(t, first=0, skip=0):
                for k in range(T_GROUPS[t]):
                    g = T_BASE[t] + k
                    act.wait_ge(tr_done, g + 1)
                    nc.scalar.activation(thi[:, first + 2 * k:first + 2 * k + 2, :].rearrange("p c t -> p (c t)"),
                                         ps[:, 4 + g % 2, :], ACT.Copy).then_inc(tr_hi, 1)

            act.dma_start(cT, io["c"]).then_inc(c_loaded, 16)
            act.dma_start(X[:, :, :], io["x"].rearrange("(t p) d -> p t d", p=P)).then_inc(x_loaded, 16)
            act.dma_start(b_ada_row, io["b_ada"].rearrange("(a n) -> a n", a=1)).then_inc(rows_loaded, 16)
            act.dma_start(lam_vec, io["lam"].partition_broadcast(P)).then_inc(rows_loaded, 16)
            act.dma_start(qk_gain, io["qk_gain"].partition_broadcast(P)).then_inc(rows_loaded, 16)
            act.dma_start(subln, io["subln"].partition_broadcast(P)).then_inc(rows_loaded, 16)
            act.dma_start(inv_freq, io["inv_freq"].partition_broadcast(P)).then_inc(rows_loaded, 16)
            act.dma_start(b_gate, io["b_gate"].partition_broadcast(P)).then_inc(rows_loaded, 16)
            act.dma_start(pos_i, io["positions"]).then_inc(rows_loaded, 16)

            act.wait_ge(c_loaded, 16)
            nc.scalar.activation(siluc, cT, ACT.Silu).then_inc(siluc_ready, 1)
            norm(0, X, (x_loaded, 16))
            hi(U_IN)
            hi(U_IN + 1)
            tr_high(T_H1)

            with act.Fori(0, 4) as i:
                for b in range(2):
                    hi(U_IN + 2 * b + 2, 4 * i)
                    hi(U_IN + 2 * b + 3, 4 * i)
                    for t in range(TT):
                        evac(2 * b + t, U_IN + 2 * b + 1, proj[:, t, bass.ds(1024 * i + 512 * b, 512)], uoff=4 * i)

            def in_block(b):
                hi(U_IN + 2 * b + 2)
                if b < IN_BLOCKS:
                    hi(U_IN + 2 * b + 3)
                w = 512 if b < IN_BLOCKS else 256
                for t in range(TT):
                    evac(2 * b + t, min(U_IN + 2 * b + 1, U_PA - 1), proj[:, t, 512 * b:512 * b + w], width=w)

            in_block(8)
            act.wait_ge(angles_ready, 1)
            nc.scalar.activation(sin, ang, ACT.Sin).then_inc(sincos_ready, 1)
            nc.scalar.activation(cos, atmp, ACT.Sin).then_inc(sincos_ready, 1)
            act.wait_ge(lam_dots, 1)
            nc.scalar.activation(lam2, lam2, ACT.Exp).then_inc(lam_exp, 1)
            in_block(9)
            act.wait_ge(acc_free, 2 * (QK_W // 512))
            for t in range(TT):
                if t:
                    act.wait_ge(rope_done, t)
                nc.scalar.activation(rot, proj[:, t, 0:QK_W], ACT.Square).then_inc(qk_sq, 1)
                act.wait_ge(qk_ms, t + 1)
                nc.scalar.activation(qk_stat[:, t * QK_HEADS:(t + 1) * QK_HEADS],
                                     qk_stat[:, t * QK_HEADS:(t + 1) * QK_HEADS], ACT.Sqrt).then_inc(qk_std, 1)
                in_block(10 + 2 * t)
                in_block(11 + 2 * t)
            in_block(14)
            act.wait_ge(gate_biased, 1)
            for t in range(TT):
                nc.scalar.activation(proj[:, t, GL0:GL0 + GL_W], proj[:, t, GL0:GL0 + GL_W],
                                     ACT.Sigmoid).then_inc(gate_ready, 1)

            for g in range(0, NQK // 4 * TT, 2):
                act.wait_ge(qkT_done, g + 1)
                t, b4 = g % TT, g // TT
                nc.scalar.activation(qkT[:, 4 * b4:4 * b4 + 4, t * P:(t + 1) * P],
                                     ps[:, 4, :].rearrange("p (b t) -> p b t", b=4), ACT.Copy).then_inc(qkT_even, 1)

            for i in range(A_SLOTS * TT):
                act.wait_ge(a_masked, i + 1)
                nc.scalar.activation(a_s[i % 2], a_s[i % 2], ACT.Exp, bias=a_nmax[:, i % 2:i % 2 + 1],
                                     accum_out=a_sum[:, i % 2:i % 2 + 1]).then_inc(a_prob, 1)

            def b_copy(i):
                act.wait_ge(b_tr, i + 1)
                nc.scalar.activation(b_pT[i % 2], ps[:, 4 + i % 2, 0:S], ACT.Copy).then_inc(b_trT, 1)

            for i in range(B_HEADS * TT):
                act.wait_ge(b_bias, i + 1)
                for m in range(2):
                    nc.scalar.activation(b_p[i % 2][:, m * S:(m + 1) * S], ps[:, 2 * (i % 2) + m, 0:S], ACT.Exp,
                                         bias=b_max[:, 2 * (i % 2) + m:2 * (i % 2) + m + 1], scale=HD ** -0.5,
                                         accum_out=b_sum[:, 2 * (i % 2) + m:2 * (i % 2) + m + 1]).then_inc(b_prob, 1)
                if i:
                    b_copy(i - 1)
            b_copy(B_HEADS * TT - 1)
            act.wait_ge(b_out, B_HEADS * TT)
            nc.scalar.activation(ob_sq, H[:, :, :].rearrange("p t n -> p (t n)"), ACT.Square).then_inc(ob_sqd, 1)
            act.wait_ge(ob_ms, 1)
            nc.scalar.activation(ob_stat, ob_stat, ACT.Sqrt).then_inc(ob_std, 1)

            tr_high(T_OA)
            hi(U_PA + 2)
            tr_high(T_OB)
            for u in range(U_PB, U_WO):
                hi(u + 2)
            tr_high(T_MIXED)
            for u in range(U_WO, U_WQ):
                hi(u + 2)

            norm(1, X, (x_ready, 1))
            tr_high(T_H2)
            for u in range(8):
                hi(U_WQ + u + 2)
                evac(N_WQ + u, U_WQ + u, qT[:, 2 * u:2 * u + 2, :].rearrange("p b t -> p (b t)"))
            for n in range(8):
                act.wait_ge(keys_scored, n + 1)
                nc.scalar.activation(score[n // 4][:, (n % 4) * 512:(n % 4 + 1) * 512], ps[:, (N_SC + n) % 4, :],
                                     ACT.Copy).then_inc(acc_free, 1)
            for t in range(TT):
                act.wait_ge(gate_shift, t + 1)
                nc.scalar.activation(gate_e, gate_e, ACT.Exp).then_inc(gate_exp, 1)
            for q in range(3):
                act.wait_ge(route_tr, q + 1)
                nc.scalar.activation(routeT[:, q, :], ps[:, 4 + q % 2, 0:S], ACT.Copy).then_inc(route_in, 1)

            for hf in range(2):
                with act.Fori(0, S // 16) as i:
                    for k in range(2):
                        act.wait_ge(g_full, hf * (S // 8) + 2 * i + (k + 1))
                        nc.scalar.activation(G[:, bass.ds(1024 * i + 512 * k, 512)], ps[:, 6 + k, :],
                                             ACT.Copy).then_inc(g_free, 1)
                u0 = U_PEER + hf * 2 * NI
                base = hf * NI

                def expert_act(i, off=0):
                    used(u0 if i == 0 else u0 + 2 * i - 1, 2 * off)
                    nc.scalar.activation(act_s[i % 2], ps[:, 4 + i % 2, :], ACT.Gelu).then_inc(gelu_done, 1)
                    act.wait_ge(w_done, base + i + 1 + off)
                    nc.scalar.activation(phi[:, i % 2, :], act_w[i % 2], ACT.Copy).then_inc(w_hi, 1)

                hi(u0 + 2)
                expert_act(0)
                hi(u0 + 3)
                expert_act(1)
                hi(u0 + 4)
                with act.Fori(0, (NI - 2) // 2) as r:
                    for k in (1, 2):
                        hi(u0 + 2 * k + 3, 4 * r)
                        expert_act(k + 1, 2 * r)
                        hi(u0 + 2 * k + 4, 4 * r)
                hi(u0 + 2 * NI + 1)

            norm(2, X, (x_ready, 2))
            tr_high(T_MIX)
            for u in range(MIX_T):
                hi(U_MIX + u + 2)
                evac(N_MT + u, U_MIX + u, mixT[:, 2 * u:2 * u + 2, :].rearrange("p b t -> p (b t)"))
            for b in range(2):
                hi(U_MIX + MIX_T + 2 * b + 2)
                hi(U_MIX + MIX_T + 2 * b + 3)
                for t in range(TT):
                    if b == 0:
                        evac(N_MV + t, U_MIX + MIX_T + 1, hv[:, t, :])
                    else:
                        evac(N_MV + 2 + t, U_MIX + MIX_T + 3, hg[:, t, :], ACT.Silu)
            act.wait_ge(lb_diff, 1)
            nc.scalar.activation(lb, lb, ACT.Exp).then_inc(lb_exp, 1)
            act.wait_ge(acc_free, N_MT + MIX_T)
            nc.scalar.activation(sig, hz, ACT.Exp, scale=-1.0).then_inc(z_exp, 1)
            nc.scalar.activation(rk, hz, ACT.Exp).then_inc(z_exp, 1)
            act.wait_ge(f_ready, 1)
            nc.scalar.activation(dec, sig, ACT.Ln).then_inc(f_log, 1)
            act.wait_ge(conv_ready, 1)
            used(U_WO2 - 1)
            nc.scalar.activation(thi[:, 0:4, :], conv_y, ACT.Copy).then_inc(conv_hi, 1)
            for l in range(1, LEVELS + 2):
                act.wait_ge(lev_d, l)
                nc.scalar.activation(lev_e[l % 2], lev_e[l % 2], ACT.Exp, scale=-1.0).then_inc(lev_exp, 1)
            for t in range(TT):
                act.wait_ge(ro_full, t + 1)
                nc.scalar.activation(ro[:, t, :], ps[:, t, :], ACT.Copy).then_inc(ro_copied, 1)
            act.wait_ge(ro_copied, TT)
            nc.scalar.activation(lev_q.rearrange("p b t -> p (b t)"), ro.rearrange("p t n -> p (t n)"),
                                 ACT.Square).then_inc(ro_sq, 1)
            act.wait_ge(ro_ms, 1)
            nc.scalar.activation(r_stat[:, 0:TT * RH], r_stat[:, 0:TT * RH], ACT.Sqrt).then_inc(ro_std, 1)
            tr_high(T_YB, 4)
            for u in range(U_WO2, U_KV):
                hi(u + 2)

            norm(3, mem, (mem_loaded, 16))
            tr_high(T_MEM)
            for u in range(4):
                hi(U_KV + u + 2)
                evac(N_K + u, U_KV + u, kT[:, 2 * u:2 * u + 2, :].rearrange("p b t -> p (b t)"))
            for b in range(2):
                hi(U_KV + 4 + 2 * b + 2)
                hi(U_KV + 4 + 2 * b + 3)
                for t in range(TT):
                    evac(N_V + 2 * b + t, U_KV + 4 + 2 * b + 1, vm[:, t, 512 * b:512 * (b + 1)])
            norm(4, X, (acc_free, N_W2 + 4))
            tr_high(T_HX)
            for u in range(4):
                hi(U_XQ + u + 2)
                evac(N_XQ + u, U_XQ + u, xqT[:, 2 * u:2 * u + 2, :].rearrange("p b t -> p (b t)"))
            for i in range(XH * TT):
                act.wait_ge(x_bias, i + 1)
                nc.scalar.activation(x_p[i % 2], ps[:, i % 2, 0:S], ACT.Exp, bias=x_max[:, i % 2:i % 2 + 1],
                                     scale=XD ** -0.5, accum_out=x_sum[:, i % 2:i % 2 + 1]).then_inc(x_prob, 1)
                act.wait_ge(x_tr, i + 1)
                h, t = i // TT, i % TT
                nc.scalar.activation(x_pT[h % 2][:, :, t * P:(t + 1) * P],
                                     ps[:, 4 + i % 2, 0:S].rearrange("p (k t) -> p k t", k=TT),
                                     ACT.Copy).then_inc(x_trT, 1)
                if t == TT - 1:
                    act.wait_ge(xo_full, h + 1)
                    nc.scalar.activation(thi[:, 2 * h:2 * h + 2, :].rearrange("p c t -> p (c t)"),
                                         ps[:, 6 + h % 2, :], ACT.Copy).then_inc(xo_hi, 1)
            for u in range(U_XO, U_MOE):
                hi(u + 2)

            act.wait_ge(router_loaded, 32)
            nc.scalar.activation(wrhi[:, :, :], wr, ACT.Copy).then_inc(wr_hi, 1)
            norm(5, X, (acc_free, N_XO + 4))
            tr_high(T_HF)
            act.wait_ge(r_ready, 1)
            nc.scalar.activation(r_prob, r_log, ACT.Exp).then_inc(r_exp, 1)

            def expert(u, off, uoff, last):
                for j in range(2):
                    hi(u + 2 * j + 2, uoff)
                    hi(u + 2 * j + 3, uoff)
                    used(u + 2 * j, uoff)
                    nc.scalar.activation(silu_g[j], ps[:, 4 + 2 * j, :], ACT.Silu).then_inc(m_silu, 1)
                    act.wait_ge(m_hid, j + 1 + 2 * off)
                    nc.scalar.activation(phi[:, j, :], hid[j], ACT.Copy).then_inc(m_hi, 1)
                if not last:
                    hi(u + 6, uoff)
                    hi(u + 7, uoff)

            with act.Fori(0, N_EXP - 1) as e:
                expert(U_MOE, e, 6 * e, False)
            expert(U_MOE + 6 * (N_EXP - 1), N_EXP - 1, 0, True)
            norm(6, X, (d_free, 4 * N_EXP))

        @block.vector
        def _(dve):
            chain = [0]

            def mark(ins):
                chain[0] += 1
                ins.then_inc(dve_chain, 1)

            def settle():
                dve.wait_ge(dve_chain, chain[0])

            def lo(u, off=0):
                s = u - SPLIT_U
                dve.wait_ge(unit_hi, s + 1 + off)
                nc.vector.tensor_tensor(wlo[:, u % 2, :], raw[:, u % 2, :], whi[:, u % 2, :].bitcast(f32),
                                        ALU.subtract).then_inc(unit_split, 1)

            def used(u, off=0):
                dve.wait_ge(unit_used, u - SPLIT_U + 1 + off)

            def tr_low(t, first=0):
                for k in range(T_GROUPS[t]):
                    g = T_BASE[t] + k
                    dve.wait_ge(tr_hi, g + 1)
                    c = first + 2 * k
                    nc.vector.tensor_tensor(tlo[:, c:c + 2, :], ps[:, 4 + g % 2, :].rearrange("p (c t) -> p c t", c=2),
                                            thi[:, c:c + 2, :].bitcast(f32), ALU.subtract).then_inc(tr_lo, 1)

            def norm(j, src, out_sem, scale=None, shift=None):
                dve.wait_ge(norm_ss, TT * (j + 1))
                nc.vector.tensor_scalar(meansq, sumsq, 1.0 / D, EPS, ALU.mult, ALU.add).then_inc(norm_ms, 1)
                dve.wait_ge(norm_std, j + 1)
                mark(nc.vector.reciprocal(rstd, std))
                dve.wait_ge(gain_loaded, 16 * (j + 1))
                settle()
                for t in range(TT):
                    last = nc.vector.scalar_tensor_tensor(H[:, t, :], src[:, t, :], rstd[:, t:t + 1], gain,
                                                          ALU.mult, ALU.mult)
                    if scale is None and t == TT - 1:
                        last.then_inc(out_sem, 1)
                    else:
                        mark(last)
                if scale is not None:
                    settle()
                    for t in range(TT):
                        mark(nc.vector.tensor_tensor(H[:, t, :], H[:, t, :], scale, ALU.mult))
                    settle()
                    for t in range(TT):
                        last = nc.vector.tensor_tensor(H[:, t, :], H[:, t, :], shift, ALU.add)
                        if t == TT - 1:
                            last.then_inc(out_sem, 1)
                        else:
                            mark(last)

            def root_mean(stat, width, ready, ms, rooted, count):
                dve.wait_ge(*ready)
                nc.vector.tensor_scalar(stat, stat, 1.0 / width, EPS, ALU.mult, ALU.add).then_inc(ms, 1)
                dve.wait_ge(rooted, count)
                mark(nc.vector.reciprocal(stat, stat))
                settle()

            nc.vector.memset(ones, 1.0).then_inc(ones_ready, 1)
            dve.wait_ge(siluc_ready, 1)

            def ada_rows(g):
                for m in range(4):
                    row = 4 * g + m
                    dve.wait_ge(ada_full, g + 1)
                    plus = 1.0 if row // 2 in (1, 4) else 0.0
                    nc.vector.tensor_scalar(MOD[:, row * 512:(row + 1) * 512], ps[:, (4 * g + m) % 8, :], plus, None,
                                            ALU.add).then_inc(ada_free, 1)

            for u in range(U_IN):
                g, c = u // DC, u % DC
                dve.wait_ge(raw_loaded[u % 2], 16 * (u // 2 + 1))
                if c == 0:
                    last = nc.vector.tensor_scalar(ada_acc[g], raw[:, u % 2, :], siluc[:, 0:1], None, ALU.mult)
                else:
                    dve.wait_ge(unit_split, u)
                    last = nc.vector.scalar_tensor_tensor(ada_acc[g], raw[:, u % 2, :], siluc[:, c:c + 1], ada_acc[g],
                                                          ALU.mult, ALU.add)
                last.then_inc(unit_split, 1)
                if c == 3 and g:
                    ada_rows(g - 1)
            ada_rows(ADA_GROUPS - 1)

            dve.wait_ge(ada_free, 4 * ADA_GROUPS)
            norm(0, X, rows_ready, sc1, sh1)
            lo(U_IN)
            lo(U_IN + 1)
            tr_low(T_H1)

            with dve.Fori(0, 4) as i:
                for k in range(4):
                    lo(U_IN + 2 + k, 4 * i)

            def in_block(b):
                lo(U_IN + 2 * b + 2)
                if b < IN_BLOCKS:
                    lo(U_IN + 2 * b + 3)

            in_block(8)
            dve.wait_ge(rows_loaded, 16 * 7)
            dve.wait_ge(rows_ready, ROWS[T_H1])
            dve.wait_ge(consts_ready, 3)
            mark(nc.vector.tensor_copy(pos, pos_i))
            mark(nc.vector.tensor_copy(pidx_i, pidx))
            mark(nc.vector.tensor_copy(key_i, iota[:, :]))
            settle()
            for t in range(TT):
                mark(nc.vector.tensor_scalar(ang[:, t, :], inv_freq, pos[:, t:t + 1], None, ALU.mult))
            settle()
            magic = 1.5 * 2.0 ** 23
            mark(nc.vector.tensor_scalar(atmp, ang, 1.0 / (2.0 * math.pi), magic, ALU.mult, ALU.add))
            settle()
            mark(nc.vector.tensor_scalar(atmp, atmp, magic, None, ALU.subtract))
            for part in (6.28125, 1.9350051879882812e-3, 3.0199159819566e-7):
                settle()
                mark(nc.vector.scalar_tensor_tensor(ang, atmp, -part, ang, ALU.mult, ALU.add))
            settle()
            mark(nc.vector.tensor_scalar(ang, ang, 3.1415925, -3.1415925, ALU.min, ALU.max))
            settle()
            mark(nc.vector.scalar_tensor_tensor(atmp, ang, -1.0, ang, ALU.mult, ALU.max))
            settle()
            nc.vector.tensor_scalar(atmp, atmp, -1.0, math.pi / 2, ALU.mult, ALU.add).then_inc(angles_ready, 1)
            lam_prod = mid[:, 6912:7040].rearrange("p (a d) -> p a d", a=2)
            mark(nc.vector.tensor_tensor(lam_prod, lam_vec[:, 0:4:2, :], lam_vec[:, 1:4:2, :], ALU.mult))
            settle()
            nc.vector.tensor_reduce(lam2, lam_prod, axis=AX.X, op=ALU.add).then_inc(lam_dots, 1)
            for t, at in ((0, 0), (1, 768)):
                band = masks[:, at:at + S]
                mark(nc.vector.tensor_scalar(band, iota[:, :], pidx, float(t * P), ALU.subtract, ALU.subtract))
                settle()
                mark(nc.vector.scalar_tensor_tensor(band, band, -1.0, band, ALU.mult, ALU.max))
                settle()
                mark(nc.vector.tensor_scalar(band, band, float(A_REACH), NEG, ALU.is_gt, ALU.mult))
            for g in (1, 2):
                mark(nc.vector.tensor_scalar(mtmp_i, key_i, pidx_i, A_DIL[g] - 1, ALU.bitwise_xor, ALU.bitwise_and))
                settle()
                mark(nc.vector.tensor_scalar(masks[:, g * S:(g + 1) * S], mtmp_i, 0.0, NEG, ALU.not_equal, ALU.mult))
                settle()
            in_block(9)
            dve.wait_ge(sincos_ready, 2)
            hf32 = HD // 2
            for t in range(TT):
                for k in range(4):
                    g_lo, g_hi = qk_gain[:, k, 0:hf32], qk_gain[:, k, hf32:HD]
                    mark(nc.vector.tensor_tensor(rope_c[:, t, k, 0:hf32], cos[:, t, :], g_lo, ALU.mult))
                    mark(nc.vector.tensor_tensor(rope_c[:, t, k, hf32:HD], cos[:, t, :], g_hi, ALU.mult))
                    mark(nc.vector.scalar_tensor_tensor(rope_s[:, t, k, 0:hf32], sin[:, t, :], -1.0, g_hi,
                                                        ALU.mult, ALU.mult))
                    mark(nc.vector.tensor_tensor(rope_s[:, t, k, hf32:HD], sin[:, t, :], g_lo, ALU.mult))
            dve.wait_ge(lam_exp, 1)
            mark(nc.vector.tensor_scalar(lam, lam2[:, 0:1], lam2[:, 1:2], LAM_INIT, ALU.subtract, ALU.add))
            settle()
            mark(nc.vector.tensor_scalar(lam, lam, -1.0, None, ALU.mult))
            mark(nc.vector.tensor_scalar(subln, subln, 1.0 - LAM_INIT, None, ALU.mult))
            settle()
            kinds = ((0, 12), (12, 24), (24, 40), (40, 56))
            for t in range(TT):
                stat = qk_stat[:, t * QK_HEADS:(t + 1) * QK_HEADS]
                rows = proj[:, t, 0:QK_W].rearrange("p (h d) -> p h d", d=HD)
                rots = rot.rearrange("p (h d) -> p h d", d=HD)
                dve.wait_ge(qk_sq, t + 1)
                nc.vector.tensor_reduce(stat, rots, axis=AX.X, op=ALU.add).then_inc(qk_summed, 1)
                root_mean(stat, HD, (qk_summed, t + 1), qk_ms, qk_std, t + 1)
                mark(nc.vector.tensor_tensor(rows, rows, stat.unsqueeze(2).broadcast_to([P, QK_HEADS, HD]), ALU.mult))
                in_block(10 + 2 * t)
                settle()
                for k, (a, b) in enumerate(kinds):
                    for out_h, in_h in ((0, hf32), (hf32, 0)):
                        table = rope_s[:, t, k, out_h:out_h + hf32].unsqueeze(1).broadcast_to([P, b - a, hf32])
                        mark(nc.vector.tensor_tensor(rots[:, a:b, out_h:out_h + hf32], rows[:, a:b, in_h:in_h + hf32],
                                                     table, ALU.mult))
                settle()
                for k, (a, b) in enumerate(kinds):
                    table = rope_c[:, t, k, :].unsqueeze(1).broadcast_to([P, b - a, HD])
                    mark(nc.vector.tensor_tensor(rows[:, a:b, :], rows[:, a:b, :], table, ALU.mult))
                in_block(11 + 2 * t)
                settle()
                nc.vector.tensor_tensor(rows, rows, rots, ALU.add).then_inc(rope_done, 1)
            in_block(14)
            dve.wait_ge(acc_free, N_PA)
            for t in range(TT):
                last = nc.vector.tensor_tensor(proj[:, t, GL0:GL0 + GL_W], proj[:, t, GL0:GL0 + GL_W], b_gate, ALU.add)
            last.then_inc(gate_biased, 1)

            for g in range(1, NQK // 4 * TT, 2):
                dve.wait_ge(qkT_done, g + 1)
                t, b4 = g % TT, g // TT
                nc.vector.tensor_copy(qkT[:, 4 * b4:4 * b4 + 4, t * P:(t + 1) * P],
                                      ps[:, 5, :].rearrange("p (b t) -> p b t", b=4)).then_inc(qkT_odd, 1)

            def a_mask(i):
                t, b = i // A_SLOTS, i % 2
                sc = ps[:, 2 * b:2 * b + 2, :].rearrange("p a n -> p (a n)")[:, 0:768]
                dve.wait_ge(a_scored, i + 1)
                mark(nc.vector.scalar_tensor_tensor(a_s[b], sc, HD ** -0.5, masks[:, t * S:t * S + 768],
                                                    ALU.mult, ALU.add))
                settle()
                mark(nc.vector.tensor_reduce(a_max[:, b:b + 1], a_s[b], axis=AX.X, op=ALU.max))
                settle()
                nc.vector.tensor_scalar(a_nmax[:, b:b + 1], a_max[:, b:b + 1], -1.0, None,
                                        ALU.mult).then_inc(a_masked, 1)

            def a_finish(i):
                t, h, b = i // A_SLOTS, i % A_SLOTS, i % 2
                dve.wait_ge(a_tr, i + 1)
                mark(nc.vector.reciprocal(a_rec[:, b:b + 1], a_sum[:, b:b + 1]))
                nc.vector.tensor_copy(a_pT[b], ps[:, 4:6, :].rearrange("p a n -> p (a n)")[:, 0:768]
                                      ).then_inc(a_trT, 1)
                dve.wait_ge(a_pv, i + 1)
                settle()
                nc.vector.tensor_scalar(oa[:, t, h * HD:(h + 1) * HD], ps[:, 6 + b, 0:HD], a_rec[:, b:b + 1], None,
                                        ALU.mult).then_inc(a_out, 1)

            n_a = A_SLOTS * TT
            a_mask(0)
            for i in range(n_a):
                if i + 1 < n_a:
                    a_mask(i + 1)
                a_finish(i)

            def b_maxima(i):
                b = 2 * (i % 2)
                dve.wait_ge(b_scored, i + 1)
                mark(nc.vector.tensor_reduce(b_max[:, b:b + 2], ps[:, b:b + 2, 0:S],
                                             axis=AX.X, op=ALU.max))
                settle()
                nc.vector.tensor_scalar(b_max[:, b:b + 2], b_max[:, b:b + 2], -(HD ** -0.5), None,
                                        ALU.mult).then_inc(b_bias, 1)

            def b_weights(i):
                b = 2 * (i % 2)
                dve.wait_ge(b_prob, 2 * i + 2)
                mark(nc.vector.reciprocal(b_rec[:, b:b + 2], b_sum[:, b:b + 2]))
                settle()
                mark(nc.vector.tensor_scalar(b_rec[:, b + 1:b + 2], b_rec[:, b + 1:b + 2], lam, None, ALU.mult))
                mark(nc.vector.tensor_scalar(b_a1, b_p[i % 2][:, 0:S], b_rec[:, b:b + 1], None, ALU.mult))
                settle()
                nc.vector.scalar_tensor_tensor(b_p[i % 2][:, 0:S], b_p[i % 2][:, S:2 * S], b_rec[:, b + 1:b + 2], b_a1,
                                               ALU.mult, ALU.add).then_inc(b_mix, 1)

            def b_rows(i):
                t, h = i // B_HEADS, i % B_HEADS
                dve.wait_ge(b_pv, i + 1)
                nc.vector.tensor_copy(H[:, t, h * P:(h + 1) * P], ps[:, 6 + i % 2, 0:P]).then_inc(b_out, 1)

            n_b = B_HEADS * TT
            b_maxima(0)
            for i in range(n_b):
                if i + 1 < n_b:
                    b_maxima(i + 1)
                b_weights(i)
                if i:
                    b_rows(i - 1)
            b_rows(n_b - 1)
            dve.wait_ge(ob_sqd, 1)
            mark(nc.vector.tensor_reduce(ob_stat, ob_sq.rearrange("p (h d) -> p h d", d=P), axis=AX.X, op=ALU.add))
            root_mean(ob_stat, P, (dve_chain, chain[0]), ob_ms, ob_std, 1)
            obv = H[:, :, :].rearrange("p t (h d) -> p (t h) d", d=P)
            mark(nc.vector.tensor_tensor(obv, obv, ob_stat.unsqueeze(2).broadcast_to([P, TT * B_HEADS, P]), ALU.mult))
            settle()
            nc.vector.tensor_tensor(obv, obv, subln.unsqueeze(1).broadcast_to([P, TT * B_HEADS, P]),
                                    ALU.mult).then_inc(rows_ready, 1)

            def group(n, u, t, h, mul, out, first, last_sem):
                used(u)
                cols = slice(h * 512, (h + 1) * 512)
                if first:
                    ins = nc.vector.tensor_tensor(out[:, t, cols], ps[:, n % 4, :], mul, ALU.mult)
                    ins.then_inc(acc_free, 1)
                    return
                settle()
                nc.vector.tensor_tensor(lin_tmp, ps[:, n % 4, :], mul, ALU.mult).then_inc(acc_free, 1)
                dve.wait_ge(acc_free, n + 1)
                ins = nc.vector.tensor_tensor(out[:, t, cols], out[:, t, cols], lin_tmp, ALU.add)
                if last_sem is None:
                    mark(ins)
                else:
                    ins.then_inc(last_sem, 1)

            tr_low(T_OA)
            lo(U_PA + 2)
            dve.wait_ge(gate_ready, TT)
            for n in range(4):
                t, h = n // 2, n % 2
                group(N_PA + n, U_PA, t, h, proj[:, t, GL0 + h * 512:GL0 + (h + 1) * 512], mixed, True, None)
            tr_low(T_OB)
            for b in range(2):
                lo(U_PB + 2 * b + 2)
                lo(U_PB + 2 * b + 3)
                for t in range(TT):
                    group(N_PB + 2 * b + t, U_PB + 2 * b + 1, t, b, proj[:, t, GL0 + D + b * 512:GL0 + D + (b + 1) * 512],
                          mixed, False, None)
            settle()
            mark(nc.vector.tensor_copy(H[:, 0, :], mixed[:, 0, :]))
            nc.vector.tensor_copy(H[:, 1, :], mixed[:, 1, :]).then_inc(rows_ready, 1)
            tr_low(T_MIXED)
            for b in range(2):
                lo(U_WO + 2 * b + 2)
                lo(U_WO + 2 * b + 3)
                for t in range(TT):
                    end = b == 1 and t == 1
                    group(N_WO + 2 * b + t, U_WO + 2 * b + 1, t, b, g1[:, b * 512:(b + 1) * 512], X, False, x_ready if end else None)

            settle()
            dve.wait_ge(x_ready, 1)
            norm(1, X, rows_ready, sc2, sh2)
            tr_low(T_H2)
            for u in range(8):
                lo(U_WQ + u + 2)

            low = -3.0e38
            for t in range(TT):
                dve.wait_ge(acc_free, N_SC + 4 * t + 4)
                sc = score[t].rearrange("p (b n) -> p b n", b=NHH)
                cd = cand.rearrange("p (h n) -> p h n", h=PH)
                for rows, vals, idx, n in ((sc, top_v, top_i, NHH), (cd, best_v, best_i, PH)):
                    if n == PH:
                        v4 = top_v.rearrange("p (h s) k -> p h s k", s=2)
                        settle()
                        mark(nc.vector.tensor_tensor(
                            cand.rearrange("p (h a b) -> p h a b", h=PH, a=TOPK),
                            v4[:, :, 0, :].unsqueeze(3).broadcast_to([P, PH, TOPK, TOPK]),
                            v4[:, :, 1, :].unsqueeze(2).broadcast_to([P, PH, TOPK, TOPK]), ALU.add))
                        settle()
                    for half in range(2):
                        k8 = slice(8 * half, 8 * half + 8)
                        for b in range(n):
                            mark(nc.vector.max(vals[:, b, k8], rows[:, b, :]))
                        settle()
                        for b in range(n):
                            mark(nc.vector.max_index(idx[:, b, k8], vals[:, b, k8], rows[:, b, :]))
                        if half == 0:
                            for b in range(n):
                                mark(nc.vector.match_replace(rows[:, b, :], vals[:, b, k8], rows[:, b, :], low))
                        settle()
                mark(nc.vector.tensor_copy(top_f.rearrange("p h s k -> p (h s) k"), top_i))
                best_flat = best_i.rearrange("p h k -> p (h k)")
                for s, (op, arg) in enumerate(((ALU.logical_shift_right, 4), (ALU.bitwise_and, 15))):
                    mark(nc.vector.tensor_scalar(half_i, best_flat, arg, None, op))
                    settle()
                    mark(nc.vector.tensor_copy(half_f[s], half_i))
                    settle()
                    pick = score[t].rearrange("p (k j) -> p k j", j=TOPK)
                    mark(nc.vector.tensor_tensor(pick, half_f[s].unsqueeze(2).broadcast_to([P, PH * TOPK, TOPK]),
                                                 iota[:, 0:TOPK].unsqueeze(1).broadcast_to([P, PH * TOPK, TOPK]),
                                                 ALU.is_equal))
                    settle()
                    pick4 = score[t].rearrange("p (h k j) -> p h k j", h=PH, k=TOPK)
                    mark(nc.vector.tensor_tensor(pick4, pick4,
                                                 top_f[:, :, s, :].unsqueeze(2).broadcast_to([P, PH, TOPK, TOPK]),
                                                 ALU.mult))
                    settle()
                    mark(nc.vector.tensor_reduce(route[:, t, s, :], pick, axis=AX.X, op=ALU.add))
                if t:
                    settle()
                nc.vector.tensor_tensor(gate_e, best_v, best_v[:, :, 0:1].broadcast_to([P, PH, TOPK]),
                                        ALU.subtract).then_inc(gate_shift, 1)
                dve.wait_ge(gate_exp, t + 1)
                mark(nc.vector.tensor_reduce(gate_s, gate_e, axis=AX.X, op=ALU.add))
                settle()
                mark(nc.vector.reciprocal(gate_r, gate_s))
                settle()
                nc.vector.tensor_tensor(route[:, t, 2, :].rearrange("p (h k) -> p h k", h=PH), gate_e,
                                        gate_r.unsqueeze(2).broadcast_to([P, PH, TOPK]), ALU.mult).then_inc(routed, 1)
            dve.wait_ge(routed, TT)

            dve.wait_ge(route_in, 3)
            for hf in range(2):
                base8 = hf * (S // 8)
                def one_hots(i, first):
                    for k in range(2):
                        if not first:
                            dve.wait_ge(g_full, base8 + 2 * i + (k - 1))
                        for q in range(8):
                            tok = bass.ds(16 * i + (8 * k + q), 1)
                            nc.vector.tensor_scalar(one_a[k][:, q, :], iota[:, 0:P], routeT[:, 0, tok], None,
                                                    ALU.is_equal)
                            last = nc.vector.tensor_scalar(one_b[k][:, q, :], iota[:, hf * HALF:(hf + 1) * HALF],
                                                           routeT[:, 1, tok], routeT[:, 2, tok],
                                                           ALU.is_equal, ALU.mult)
                        last.then_inc(oh_ready, 1)

                one_hots(0, hf == 0)
                with dve.Fori(1, S // 16) as i:
                    one_hots(i, False)
                u0 = U_PEER + hf * 2 * NI
                base = hf * NI
                dve.wait_ge(g_free, base8 + S // 8)
                Gt = G.rearrange("p (t j) -> p j t", j=HALF)

                def gated(i, off=0):
                    dve.wait_ge(gelu_done, base + i + 1 + off)
                    nc.vector.tensor_tensor(act_w[i % 2].rearrange("p (j t) -> p j t", j=2),
                                            act_s[i % 2].rearrange("p (j t) -> p j t", j=2),
                                            Gt[:, bass.ds(2 * i + 2 * off, 2), :], ALU.mult).then_inc(w_done, 1)
                    dve.wait_ge(w_hi, base + i + 1 + off)
                    nc.vector.tensor_tensor(plo[:, i % 2, :], act_w[i % 2], phi[:, i % 2, :].bitcast(f32),
                                            ALU.subtract).then_inc(w_lo, 1)

                lo(u0 + 2)
                gated(0)
                lo(u0 + 3)
                gated(1)
                lo(u0 + 4)
                with dve.Fori(0, (NI - 2) // 2) as r:
                    for k in (1, 2):
                        lo(u0 + 2 * k + 3, 4 * r)
                        gated(k + 1, 2 * r)
                        lo(u0 + 2 * k + 4, 4 * r)
                lo(u0 + 2 * NI + 1)
            used(U_MIX - 1)
            for n in range(4):
                t, h = n // 2, n % 2
                cols = slice(h * 512, (h + 1) * 512)
                tmp = mid[:, n * 512:(n + 1) * 512]
                mark(nc.vector.tensor_tensor(tmp, ps[:, n, :], g2[:, cols], ALU.mult))
                settle()
                last = nc.vector.tensor_tensor(X[:, t, cols], X[:, t, cols], tmp, ALU.add)
                if n < 3:
                    mark(last)
            settle()
            last.then_inc(x_ready, 1)

            dve.wait_ge(x_ready, 2)
            norm(2, X, rows_ready)
            tr_low(T_MIX)
            mark(nc.vector.tensor_copy(lint, iota[:, 0:P]))
            mark(nc.vector.tensor_scalar(lup, iota[:, 0:P], pidx, None, ALU.is_gt))
            mark(nc.vector.tensor_copy(lmask[:, 7, :], ident[:, :]))
            mark(nc.vector.memset(keep, 1.0))
            settle()
            mark(nc.vector.memset(keep[:, 0:S:SEG], 0.0))
            mark(nc.vector.tensor_scalar(lint, lint, pidx_i, None, ALU.bitwise_xor))
            settle()
            for l in range(LEVELS):
                mark(nc.vector.tensor_scalar(lsh, lint, l, None, ALU.logical_shift_right))
                settle()
                mark(nc.vector.scalar_tensor_tensor(lmask[:, l, :], lsh, 1.0, lup, ALU.is_equal, ALU.mult))
                settle()
            for u in range(MIX_T):
                lo(U_MIX + u + 2)
            dve.wait_ge(mix_loaded, 48)
            nc.vector.tensor_tensor(lb, lb2[:, RH:2 * RH], lb2[:, 0:RH], ALU.subtract).then_inc(lb_diff, 1)
            for u in range(4):
                lo(U_MIX + MIX_T + u + 2)
            settle()
            dve.wait_ge(acc_free, N_MT + MIX_T)
            mark(nc.vector.tensor_tensor(conv_u, cc, cx, ALU.mult))
            settle()
            for j in (2, 1, 0):
                for b in range(4):
                    w = conv_w[:, 3 * b + j:3 * b + j + 1]
                    if j == 2:
                        mark(nc.vector.tensor_scalar(conv_y[:, b, :], conv_u[:, b, :], w, None, ALU.mult))
                    else:
                        d = 2 - j
                        mark(nc.vector.scalar_tensor_tensor(conv_y[:, b, d:S], conv_u[:, b, 0:S - d], w,
                                                            conv_y[:, b, d:S], ALU.mult, ALU.add))
                settle()
            nc.vector.tensor_tensor(conv_y, conv_y, cb, ALU.mult).then_inc(conv_ready, 1)
            dve.wait_ge(lb_exp, 1)
            mark(nc.vector.tensor_scalar(lb, lb, 1.0, None, ALU.add))
            settle()
            mark(nc.vector.reciprocal(lb, lb))
            settle()
            mark(nc.vector.tensor_scalar(omlb, lb, -1.0, 1.0, ALU.mult, ALU.add))
            dve.wait_ge(z_exp, 2)
            mark(nc.vector.tensor_scalar(sig, sig, 1.0, None, ALU.add))
            mark(nc.vector.tensor_scalar(rk, rk, 1.0, None, ALU.add))
            settle()
            mark(nc.vector.reciprocal(sig, sig))
            mark(nc.vector.reciprocal(rk, rk))
            settle()
            for h in range(RH):
                mark(nc.vector.tensor_scalar(rk[:, h, :], rk[:, h, :], omlb[:, h:h + 1], None, ALU.mult))
                last = nc.vector.tensor_scalar(sig[:, h, :], sig[:, h, :], omlb[:, h:h + 1], lb[:, h:h + 1],
                                               ALU.mult, ALU.add)
                if h < RH - 1:
                    mark(last)
            settle()
            last.then_inc(f_ready, 1)
            dve.wait_ge(conv_hi, 1)
            nc.vector.tensor_tensor(tlo[:, 0:4, :], conv_y, thi[:, 0:4, :].bitcast(f32), ALU.subtract
                                    ).then_inc(conv_lo, 1)
            dve.wait_ge(f_log, 1)
            for h in range(RH):
                mark(nc.vector.tensor_tensor_scan(sig[:, h, :], keep, dec[:, h, :], 0.0, ALU.mult, ALU.add))
            settle()
            bsum = sig
            seg = bsum.rearrange("p h (n s) -> p (h n) s", s=SEG)

            def exponents(l):
                e = lev_e[l % 2]
                if l <= 6:
                    c = 1 << (l - 1)
                    v = bsum.rearrange("p h (n s) -> p (h n) s", s=2 * c)
                    o = e.rearrange("p h (n s) -> p (h n) s", s=2 * c)
                    mark(nc.vector.tensor_tensor(o, v, v[:, :, c - 1:c].broadcast_to([P, RH * S // (2 * c), 2 * c]),
                                                 ALU.subtract))
                else:
                    v = bsum.rearrange("p h (n s) -> p h n s", s=SEG)
                    o = e.rearrange("p h (n s) -> p h n s", s=SEG)
                    end = v[:, :, :, SEG - 1:SEG]
                    if l == 7:
                        left = slice(0, 4, 2)
                        right = slice(1, 4, 2)
                        mark(nc.vector.tensor_tensor(o[:, :, left, :], v[:, :, left, :],
                                                     end[:, :, left, :].broadcast_to([P, RH, 2, SEG]), ALU.subtract))
                        mark(nc.vector.tensor_copy(o[:, :, right, :], v[:, :, right, :]))
                    else:
                        left = slice(0, 2)
                        mark(nc.vector.tensor_tensor(o[:, :, left, :], v[:, :, left, :],
                                                     end[:, :, left, :].broadcast_to([P, RH, 2, SEG]), ALU.subtract))
                        mark(nc.vector.tensor_copy(o[:, :, 2, :], v[:, :, 2, :]))
                        mark(nc.vector.tensor_tensor(o[:, :, 3, :], v[:, :, 3, :],
                                                     end[:, :, 2, :].broadcast_to([P, RH, SEG]), ALU.add))
                        settle()
                        mark(nc.vector.tensor_tensor(o[:, :, 0, :], o[:, :, 0, :],
                                                     end[:, :, 1, :].broadcast_to([P, RH, SEG]), ALU.subtract))
                settle()
                nc.vector.scalar_tensor_tensor(e, e, -1.0, e, ALU.mult, ALU.max).then_inc(lev_d, 1)

            def decayed(l):
                dve.wait_ge(lev_exp, l)
                dve.wait_ge(lev_full, l)
                mark(nc.vector.tensor_tensor(lev_k, rk, lev_e[l % 2], ALU.mult))
                settle()
                nc.vector.tensor_tensor(lev_q, hq, lev_e[l % 2], ALU.mult).then_inc(lev_qk, 1)

            def collect(l):
                dve.wait_ge(lev_full, l + 1)
                if l == LEVELS + 1:
                    nc.vector.tensor_copy(rsc_x, ps[:, 2 * (l % 2), :].rearrange("p (h n) -> p h n", h=RH)
                                          ).then_inc(lev_free, 1)
                    return
                m = lmask[:, (l - 1) % 8, :].unsqueeze(1).broadcast_to([P, RH, P])
                dst = rsc if l == 0 else lev_t
                for t in range(TT):
                    last = nc.vector.tensor_tensor(dst[:, t, :, :],
                                                   ps[:, 2 * (l % 2) + t, :].rearrange("p (h n) -> p h n", h=RH),
                                                   m, ALU.mult)
                    if t == 0:
                        mark(last)
                last.then_inc(lev_free, 1)
                if l:
                    settle()
                    dve.wait_ge(lev_free, l + 1)
                    last = nc.vector.tensor_tensor(rsc, rsc, lev_t, ALU.add)
                    if l == LEVELS:
                        last.then_inc(sc_ready, 1)
                    else:
                        mark(last)
                        settle()

            for l in range(1, LEVELS + 2):
                exponents(l)
                decayed(l)
                collect(l - 1)
            collect(LEVELS + 1)
            dve.wait_ge(ro_sq, 1)
            rst = r_stat[:, 0:TT * RH]
            mark(nc.vector.tensor_reduce(rst, lev_q.rearrange("p b t -> p (b t)").rearrange("p (h d) -> p h d", d=P),
                                         axis=AX.X, op=ALU.add))
            mark(nc.vector.tensor_tensor(hg, hg, hnorm.unsqueeze(1).broadcast_to([P, TT, CW]), ALU.mult))
            root_mean(rst, P, (dve_chain, chain[0]), ro_ms, ro_std, 1)
            rov = ro.rearrange("p t (h d) -> p (t h) d", d=P)
            mark(nc.vector.tensor_tensor(rov, rov, rst.unsqueeze(2).broadcast_to([P, TT * RH, P]), ALU.mult))
            settle()
            nc.vector.tensor_tensor(H[:, :, 0:CW], ro, hg, ALU.mult).then_inc(rows_ready, 1)
            tr_low(T_YB, 4)

            def residual(n0, u0):
                for b in range(2):
                    lo(u0 + 2 * b + 2)
                    lo(u0 + 2 * b + 3)
                    for t in range(TT):
                        n = n0 + 2 * b + t
                        used(u0 + 2 * b + 1)
                        cols = slice(b * 512, (b + 1) * 512)
                        nc.vector.tensor_tensor(X[:, t, cols], X[:, t, cols], ps[:, n % 4, :],
                                                ALU.add).then_inc(acc_free, 1)

            residual(N_W2, U_WO2)

            norm(3, mem, rows_ready)
            tr_low(T_MEM)
            for u in range(8):
                lo(U_KV + u + 2)
            norm(4, X, rows_ready)
            tr_low(T_HX)
            for u in range(4):
                lo(U_XQ + u + 2)
            for i in range(XH * TT):
                b, h, t = i % 2, i // TT, i % TT
                dve.wait_ge(x_scored, i + 1)
                mark(nc.vector.tensor_reduce(x_max[:, b:b + 1], ps[:, b, 0:S], axis=AX.X, op=ALU.max))
                settle()
                nc.vector.tensor_scalar(x_max[:, b:b + 1], x_max[:, b:b + 1], -(XD ** -0.5), None,
                                        ALU.mult).then_inc(x_bias, 1)
                dve.wait_ge(x_prob, i + 1)
                mark(nc.vector.reciprocal(x_rec[:, b:b + 1], x_sum[:, b:b + 1]))
                settle()
                nc.vector.tensor_scalar(x_p[b], x_p[b], x_rec[:, b:b + 1], None, ALU.mult).then_inc(x_norm, 1)
                if t == TT - 1:
                    dve.wait_ge(xo_hi, h + 1)
                    nc.vector.tensor_tensor(tlo[:, 2 * h:2 * h + 2, :],
                                            ps[:, 6 + h % 2, :].rearrange("p (c t) -> p c t", c=2),
                                            thi[:, 2 * h:2 * h + 2, :].bitcast(f32), ALU.subtract).then_inc(xo_lo, 1)
            residual(N_XO, U_XO)

            dve.wait_ge(wr_hi, 1)
            nc.vector.tensor_tensor(wrlo[:, :, :], wr, wrhi[:, :, :].bitcast(f32), ALU.subtract).then_inc(wr_lo, 1)
            norm(5, X, rows_ready)
            tr_low(T_HF)
            dve.wait_ge(r_full, 1)
            for t in range(TT):
                mark(nc.vector.tensor_tensor(r_log[:, t, :], ps[:, t, 0:20], r_bias, ALU.add))
            settle()
            NG5 = N_GRP + 1
            lv = r_log.rearrange("p t (g a) -> p (t g) a", a=4)
            pv5 = r_prob.rearrange("p t (g a) -> p (t g) a", a=4)
            st = big[:, 9216:9216 + TT * NG5]
            mark(nc.vector.tensor_reduce(st, lv, axis=AX.X, op=ALU.max))
            settle()
            nc.vector.tensor_tensor(lv, lv, st.unsqueeze(2).broadcast_to([P, TT * NG5, 4]),
                                    ALU.subtract).then_inc(r_ready, 1)
            for a in range(4):
                mark(nc.vector.tensor_scalar(r_low[:, a, :], iota[:, 0:4], float(a), None, ALU.is_lt))
            dve.wait_ge(r_exp, 1)
            mark(nc.vector.tensor_reduce(st, pv5, axis=AX.X, op=ALU.add))
            settle()
            mark(nc.vector.reciprocal(st, st))
            settle()
            mark(nc.vector.tensor_tensor(pv5, pv5, st.unsqueeze(2).broadcast_to([P, TT * NG5, 4]), ALU.mult))
            settle()
            cmp3 = r_cmp.rearrange("p t g a b -> p (t g) a b")
            tie3 = r_tie.rearrange("p t g a b -> p (t g) a b")
            own = pv5.unsqueeze(3).broadcast_to([P, TT * NG5, 4, 4])
            other = pv5.unsqueeze(2).broadcast_to([P, TT * NG5, 4, 4])
            mark(nc.vector.tensor_tensor(cmp3, other, own, ALU.is_gt))
            mark(nc.vector.tensor_tensor(tie3, other, own, ALU.is_equal))
            settle()
            mark(nc.vector.tensor_tensor(tie3, tie3, r_low.unsqueeze(1).broadcast_to([P, TT * NG5, 4, 4]), ALU.mult))
            settle()
            mark(nc.vector.tensor_tensor(cmp3, cmp3, tie3, ALU.add))
            settle()
            rank = r_rank.rearrange("p t (g a) -> p (t g) a", a=4)
            mark(nc.vector.tensor_reduce(rank, cmp3, axis=AX.X, op=ALU.add))
            settle()
            mark(nc.vector.scalar_tensor_tensor(r_sel[:, :, 0:4], r_rank[:, :, 0:4], 0.5, r_prob[:, :, 0:4],
                                                ALU.is_lt, ALU.mult))
            mark(nc.vector.scalar_tensor_tensor(r_sel[:, :, 4:20], r_rank[:, :, 4:20], 1.5, r_prob[:, :, 4:20],
                                                ALU.is_lt, ALU.mult))
            settle()
            for t in range(TT):
                es = r_sel[:, t, 4:20].rearrange("p (g a) -> p g a", a=4)
                esum = big[:, 9248 + 4 * t:9252 + 4 * t]
                mark(nc.vector.tensor_reduce(esum, es, axis=AX.X, op=ALU.add))
                settle()
                mark(nc.vector.reciprocal(esum, esum))
                settle()
                mark(nc.vector.tensor_tensor(esum, esum, r_sel[:, t, 0:4], ALU.mult))
                settle()
                mark(nc.vector.tensor_tensor(comb[:, t, :].rearrange("p (g a) -> p g a", a=4), es,
                                             esum.unsqueeze(2).broadcast_to([P, N_GRP, 4]), ALU.mult))
            settle()

            def expert(u, off, uoff, last, e):
                for j in range(2):
                    lo(u + 2 * j + 2, uoff)
                    lo(u + 2 * j + 3, uoff)
                    dve.wait_ge(m_silu, j + 1 + 2 * off)
                    used(u + 2 * j + 1, uoff)
                    nc.vector.tensor_tensor(hid[j], silu_g[j], ps[:, 5 + 2 * j, :], ALU.mult).then_inc(m_hid, 1)
                    dve.wait_ge(m_hi, j + 1 + 2 * off)
                    nc.vector.tensor_tensor(plo[:, j, :], hid[j], phi[:, j, :].bitcast(f32),
                                            ALU.subtract).then_inc(m_lo, 1)
                if not last:
                    lo(u + 6, uoff)
                    lo(u + 7, uoff)
                for h in range(2):
                    used(u + 4 + h, uoff)
                    for t in range(TT):
                        cols = slice(h * 512, (h + 1) * 512)
                        nc.vector.scalar_tensor_tensor(X[:, t, cols], ps[:, 2 * h + t, :], comb[:, t, e], X[:, t, cols],
                                                       ALU.mult, ALU.add).then_inc(d_free, 1)

            with dve.Fori(0, N_EXP - 1) as e:
                expert(U_MOE, e, 6 * e, False, bass.ds(e, 1))
                dve.wait_ge(d_free, 4 * e + 4)
            expert(U_MOE + 6 * (N_EXP - 1), N_EXP - 1, 0, True, slice(N_EXP - 1, N_EXP))
            dve.wait_ge(d_free, 4 * N_EXP)
            norm(6, X, out_ready)

        @block.tensor
        def _(pe):
            def mm3(out, ahi, alo, bhi, blo, start, stop):
                nc.tensor.matmul(out, ahi, bhi, start=start, stop=False)
                nc.tensor.matmul(out, ahi, blo, start=False, stop=False)
                return nc.tensor.matmul(out, alo, bhi, start=False, stop=stop)

            def arrived(u, off=0):
                pe.wait_ge(unit_split, u + 1 + off)

            def free_bank(n, off=0):
                if n >= 4:
                    pe.wait_ge(acc_free, n - 3 + off)

            def transposes(t, src, chunks):
                if t == T_OA:
                    pe.wait_ge(a_out, A_SLOTS * TT)
                else:
                    pe.wait_ge(rows_ready, ROWS[t])
                for k in range(T_GROUPS[t]):
                    g = T_BASE[t] + k
                    if g >= 2:
                        pe.wait_ge(tr_lo, g - 1)
                    for c in range(2):
                        for tt in range(TT):
                            last = nc.tensor.transpose(ps[:, 4 + g % 2, (2 * c + tt) * P:(2 * c + tt + 1) * P],
                                                       src[:, tt, (2 * k + c) * P:(2 * k + c + 1) * P], ident[:, :])
                    last.then_inc(tr_done, 1)

            def split_rows(t):
                pe.wait_ge(tr_lo, T_BASE[t + 1])

            def block_rows(n, u, off=0, uoff=0):
                for t in range(TT):
                    free_bank(n + t, off)
                for k in range(2):
                    arrived(u + k, uoff)
                    s = (u + k) % 2
                    for t in range(TT):
                        for c in range(4):
                            rows = slice(t * P, (t + 1) * P)
                            cols = slice(c * 512, (c + 1) * 512)
                            last = mm3(ps[:, (n + t) % 4, :], thi[:, 4 * k + c, rows], tlo[:, 4 * k + c, rows],
                                       whi[:, s, cols], wlo[:, s, cols], k == 0 and c == 0, k == 1 and c == 3)
                    last.then_inc(unit_used, 1)

            def block_T(out, u, uoff=0):
                arrived(u, uoff)
                s = u % 2
                for fb in range(2):
                    for c in range(DC):
                        cols = slice(c * 256 + fb * P, c * 256 + (fb + 1) * P)
                        last = mm3(out[:, fb * S:(fb + 1) * S], whi[:, s, cols], wlo[:, s, cols],
                                   thi[:, c, :], tlo[:, c, :], c == 0, c == DC - 1)
                last.then_inc(unit_used, 1)

            def group_T(n, u):
                free_bank(n)
                block_T(ps[:, n % 4, :], u)

            pe.wait_ge(ones_ready, 1)
            pe.wait_ge(rows_loaded, 16 * 7)
            for g in range(ADA_GROUPS):
                pe.wait_ge(unit_split, DC * (g + 1))
                for m in range(4):
                    if g == 2:
                        pe.wait_ge(ada_free, m + 1)
                    o = ps[:, (4 * g + m) % 8, :]
                    row = 4 * g + m
                    nc.tensor.matmul(o, ones, ada_acc[g][:, m * 512:(m + 1) * 512], start=True, stop=False)
                    last = nc.tensor.matmul(o, ones[0:1, :], b_ada_row[:, row * 512:(row + 1) * 512],
                                            start=False, stop=True)
                last.then_inc(ada_full, 1)

            pe.wait_ge(consts_ready, 3)
            transposes(T_H1, H, DC)
            split_rows(T_H1)
            for b in range(2):
                block_rows(2 * b, U_IN + 2 * b)
            with pe.Fori(0, (IN_BLOCKS - 2) // 2) as i:
                for b in range(2, 4):
                    block_rows(2 * b, U_IN + 2 * b, 4 * i, 4 * i)
            u = U_PA - 1
            arrived(u)
            for t in range(TT):
                n = N_PA - 2 + t
                free_bank(n)
                for c in range(DC):
                    rows = slice(t * P, (t + 1) * P)
                    cols = slice(c * 256, (c + 1) * 256)
                    last = mm3(ps[:, n % 4, 0:256], thi[:, c, rows], tlo[:, c, rows], whi[:, u % 2, cols],
                               wlo[:, u % 2, cols], c == 0, c == DC - 1)
            last.then_inc(unit_used, 1)

            pe.wait_ge(rope_done, TT)
            pe.wait_ge(gate_biased, 1)
            for g in range(NQK // 4 * TT):
                t, b4 = g % TT, g // TT
                if g >= 2:
                    pe.wait_ge(qkT_odd if g % 2 else qkT_even, g // 2)
                for b in range(4):
                    last = nc.tensor.transpose(ps[:, 4 + g % 2, b * P:(b + 1) * P],
                                               proj[:, t, (4 * b4 + b) * P:(4 * b4 + b + 1) * P], ident[:, :])
                last.then_inc(qkT_done, 1)
            pe.wait_ge(qkT_even, NQK // 4 * TT // 2)
            pe.wait_ge(qkT_odd, NQK // 4 * TT // 2)

            def a_groups(t):
                return (0, 1, 2) if t == 0 else (1, 2, 0)

            def a_scores(i):
                t, h, b = i // A_SLOTS, i % A_SLOTS, i % 2
                if i >= 2:
                    pe.wait_ge(a_masked, i - 1)
                sc = ps[:, 2 * b:2 * b + 2, :].rearrange("p a n -> p (a n)")
                for k, g in enumerate(a_groups(t)):
                    hd = g * A_SLOTS + h
                    part = slice(HD * (hd % 2), HD * (hd % 2) + HD)
                    last = nc.tensor.matmul(sc[:, k * S:(k + 1) * S], qkT[part, hd // 2, t * P:(t + 1) * P],
                                            qkT[part, 6 + hd // 2, :], start=True, stop=True)
                last.then_inc(a_scored, 1)

            def a_values(i):
                t, h, b = i // A_SLOTS, i % A_SLOTS, i % 2
                pe.wait_ge(a_prob, i + 1)
                if i:
                    pe.wait_ge(a_trT, i)
                trp = ps[:, 4:6, :].rearrange("p a n -> p (a n)")
                for k in range(6):
                    last = nc.tensor.transpose(trp[:, k * P:(k + 1) * P], a_s[b][:, k * P:(k + 1) * P], ident[:, :])
                last.then_inc(a_tr, 1)
                if i >= 2:
                    pe.wait_ge(a_out, i - 1)
                pe.wait_ge(a_trT, i + 1)
                for k in range(6):
                    hd = a_groups(t)[k // 2] * A_SLOTS + h
                    last = nc.tensor.matmul(ps[:, 6 + b, 0:HD], a_pT[b][:, k * P:(k + 1) * P],
                                            proj[:, k % 2, V0 + hd * HD:V0 + (hd + 1) * HD], start=k == 0, stop=k == 5)
                last.then_inc(a_pv, 1)

            n_a = A_SLOTS * TT
            a_scores(0)
            for i in range(n_a):
                if i + 1 < n_a:
                    a_scores(i + 1)
                a_values(i)

            def b_scores(i):
                t, h = i // B_HEADS, i % B_HEADS
                if i >= 2:
                    pe.wait_ge(b_prob, 2 * (i - 1))
                elif i == 0:
                    pe.wait_ge(a_masked, n_a)
                for m in range(2):
                    part = slice(HD * m, HD * m + HD)
                    last = nc.tensor.matmul(ps[:, 2 * (i % 2) + m, 0:S], qkT[part, 12 + h, t * P:(t + 1) * P],
                                            qkT[part, 20 + h, :], start=True, stop=True)
                last.then_inc(b_scored, 1)

            def b_values(i):
                t, h = i // B_HEADS, i % B_HEADS
                pe.wait_ge(b_mix, i + 1)
                if i >= 2:
                    pe.wait_ge(b_trT, i - 1)
                for k in range(2):
                    last = nc.tensor.transpose(ps[:, 4 + i % 2, k * P:(k + 1) * P], b_p[i % 2][:, k * P:(k + 1) * P],
                                               ident[:, :])
                last.then_inc(b_tr, 1)
                if i >= 2:
                    pe.wait_ge(b_out, i - 1)
                elif i == 0:
                    pe.wait_ge(a_out, n_a)
                pe.wait_ge(b_trT, i + 1)
                for k in range(2):
                    last = nc.tensor.matmul(ps[:, 6 + i % 2, 0:P], b_pT[i % 2][:, k * P:(k + 1) * P],
                                            proj[:, k, V0 + A_W + h * P:V0 + A_W + (h + 1) * P],
                                            start=k == 0, stop=k == 1)
                last.then_inc(b_pv, 1)

            n_b = B_HEADS * TT
            b_scores(0)
            for i in range(n_b):
                if i + 1 < n_b:
                    b_scores(i + 1)
                b_values(i)

            transposes(T_OA, oa, 2)
            split_rows(T_OA)
            arrived(U_PA)
            for n in range(4):
                t, h = n // 2, n % 2
                free_bank(N_PA + n)
                for c in range(2):
                    cols = slice(c * D + h * 512, c * D + (h + 1) * 512)
                    rows = slice(t * P, (t + 1) * P)
                    last = mm3(ps[:, (N_PA + n) % 4, :], thi[:, c, rows], tlo[:, c, rows], whi[:, U_PA % 2, cols],
                               wlo[:, U_PA % 2, cols], c == 0, c == 1)
            last.then_inc(unit_used, 1)
            transposes(T_OB, H, DC)
            split_rows(T_OB)
            for b in range(2):
                block_rows(N_PB + 2 * b, U_PB + 2 * b)
            transposes(T_MIXED, H, DC)
            split_rows(T_MIXED)
            for b in range(2):
                block_rows(N_WO + 2 * b, U_WO + 2 * b)

            transposes(T_H2, H, DC)
            split_rows(T_H2)
            for u in range(8):
                group_T(N_WQ + u, U_WQ + u)
            pe.wait_ge(keys_loaded, 16)
            pe.wait_ge(acc_free, N_SC)
            for n in range(8):
                t = n // 4
                free_bank(N_SC + n)
                for b in range(4):
                    hh = 4 * (n % 4) + b
                    last = nc.tensor.matmul(ps[:, (N_SC + n) % 4, b * P:(b + 1) * P], qT[:, hh, t * P:(t + 1) * P],
                                            keysT[:, hh, :], start=True, stop=True)
                last.then_inc(keys_scored, 1)
            pe.wait_ge(routed, TT)
            for q in range(3):
                if q == 2:
                    pe.wait_ge(route_in, 1)
                for t in range(TT):
                    last = nc.tensor.transpose(ps[:, 4 + q % 2, t * P:(t + 1) * P], route[:, t, q, :], ident[:, :])
                last.then_inc(route_tr, 1)

            pe.wait_ge(route_in, 3)
            for hf in range(2):
                base8 = hf * (S // 8)
                def gates(i, first):
                    for k in range(2):
                        pe.wait_ge(oh_ready, base8 + 2 * i + (k + 1))
                        if not first:
                            pe.wait_ge(g_free, base8 + 2 * i + (k - 1))
                        for q in range(8):
                            last = nc.tensor.matmul(ps[:, 6 + k, q * HALF:(q + 1) * HALF], one_a[k][:, q, :],
                                                    one_b[k][:, q, :], start=True, stop=True)
                        last.then_inc(g_full, 1)

                gates(0, hf == 0)
                with pe.Fori(1, S // 16) as i:
                    gates(i, False)
                u0 = U_PEER + hf * 2 * NI
                base = hf * NI

                def scores_of(i, u, off=0, uoff=0):
                    if i >= 2:
                        pe.wait_ge(gelu_done, base + i - 1 + off)
                    block_T(ps[:, 4 + i % 2, :], u, uoff)

                def values_of(i, u, off=0, uoff=0):
                    arrived(u, uoff)
                    pe.wait_ge(w_lo, base + i + 1 + off)
                    for j in range(2):
                        for t in range(TT):
                            for h in range(2):
                                rows = slice(j * S + t * P, j * S + (t + 1) * P)
                                cols = slice(j * D + h * 512, j * D + (h + 1) * 512)
                                last = mm3(ps[:, 2 * t + h, :], phi[:, i % 2, rows], plo[:, i % 2, rows],
                                           whi[:, u % 2, cols], wlo[:, u % 2, cols],
                                           hf == 0 and u == u0 + 2 and j == 0,
                                           hf == 1 and u == u0 + 2 * NI - 1 and j == 1)
                    last.then_inc(unit_used, 1)

                scores_of(0, u0)
                scores_of(1, u0 + 1)
                values_of(0, u0 + 2)
                with pe.Fori(0, (NI - 2) // 2) as r:
                    for k in (1, 2):
                        scores_of(k + 1, u0 + 2 * k + 1, 2 * r, 4 * r)
                        values_of(k, u0 + 2 * k + 2, 2 * r, 4 * r)
                values_of(NI - 1, u0 + 2 * NI - 1)

            transposes(T_MIX, H, DC)
            split_rows(T_MIX)
            for u in range(MIX_T):
                group_T(N_MT + u, U_MIX + u)
            for b in range(2):
                block_rows(N_MV + 2 * b, U_MIX + MIX_T + 2 * b)
            for l in range(LEVELS + 2):
                qs, ks = (hq, rk) if l == 0 else (lev_q, lev_k)
                if l == 0:
                    pe.wait_ge(acc_free, N_W2)
                    pe.wait_ge(f_ready, 1)
                else:
                    pe.wait_ge(lev_qk, l)
                    if l >= 2:
                        pe.wait_ge(lev_free, l - 1)
                for t in range(1 if l == LEVELS + 1 else TT):
                    for h in range(RH):
                        kt, qt = (0, 1) if l == LEVELS + 1 else (t, t)
                        last = nc.tensor.matmul(ps[:, 2 * (l % 2) + t, h * P:(h + 1) * P],
                                                ks[:, h, kt * P:(kt + 1) * P], qs[:, h, qt * P:(qt + 1) * P],
                                                start=True, stop=True)
                last.then_inc(lev_full, 1)
            pe.wait_ge(sc_ready, 1)
            pe.wait_ge(lev_free, LEVELS + 2)
            for t in range(TT):
                for h in range(RH):
                    cols = slice(h * P, (h + 1) * P)
                    if t:
                        nc.tensor.matmul(ps[:, t, cols], rsc_x[:, h, :], hv[:, 0, cols], start=True, stop=False)
                    last = nc.tensor.matmul(ps[:, t, cols], rsc[:, t, h, :], hv[:, t, cols], start=t == 0, stop=True)
                last.then_inc(ro_full, 1)
            pe.wait_ge(conv_lo, 1)
            transposes(T_YB, H, 4)
            split_rows(T_YB)
            for b in range(2):
                block_rows(N_W2 + 2 * b, U_WO2 + 2 * b)

            transposes(T_MEM, H, DC)
            split_rows(T_MEM)
            for u in range(4):
                group_T(N_K + u, U_KV + u)
            for b in range(2):
                block_rows(N_V + 2 * b, U_KV + 4 + 2 * b)
            transposes(T_HX, H, DC)
            split_rows(T_HX)
            for u in range(4):
                group_T(N_XQ + u, U_XQ + u)
            pe.wait_ge(acc_free, N_XO)

            def x_scores(i):
                h, t = i // TT, i % TT
                if i >= 2:
                    pe.wait_ge(x_prob, i - 1)
                for c in range(2):
                    last = nc.tensor.matmul(ps[:, i % 2, 0:S], xqT[:, 2 * h + c, t * P:(t + 1) * P], kT[:, 2 * h + c, :],
                                            start=c == 0, stop=c == 1)
                last.then_inc(x_scored, 1)

            x_scores(0)
            for i in range(XH * TT):
                h, t = i // TT, i % TT
                if i + 1 < XH * TT:
                    x_scores(i + 1)
                pe.wait_ge(x_norm, i + 1)
                if i >= 2:
                    pe.wait_ge(x_trT, i - 1)
                for k in range(TT):
                    last = nc.tensor.transpose(ps[:, 4 + i % 2, k * P:(k + 1) * P], x_p[i % 2][:, k * P:(k + 1) * P],
                                               ident[:, :])
                last.then_inc(x_tr, 1)
                if t == TT - 1:
                    pe.wait_ge(x_trT, i + 1)
                    if h >= 2:
                        pe.wait_ge(xo_lo, h - 1)
                    for c in range(2):
                        for k in range(TT):
                            cols = slice(h * XD + c * P, h * XD + (c + 1) * P)
                            last = nc.tensor.matmul(ps[:, 6 + h % 2, c * S:(c + 1) * S], vm[:, k, cols],
                                                    x_pT[h % 2][:, k, :], start=k == 0, stop=k == TT - 1)
                    last.then_inc(xo_full, 1)
            pe.wait_ge(xo_lo, XH)
            for b in range(2):
                block_rows(N_XO + 2 * b, U_XO + 2 * b)

            transposes(T_HF, H, DC)
            split_rows(T_HF)
            pe.wait_ge(wr_lo, 1)
            pe.wait_ge(acc_free, N_XO + 4)
            for t in range(TT):
                for c in range(DC):
                    rows = slice(t * P, (t + 1) * P)
                    last = mm3(ps[:, t, 0:20], thi[:, c, rows], tlo[:, c, rows], wrhi[:, c, :], wrlo[:, c, :],
                               c == 0, c == DC - 1)
            last.then_inc(r_full, 1)

            def expert(u, off, uoff, first):
                for j in range(2):
                    for k in range(2):
                        block_T(ps[:, 4 + 2 * j + k, :], u + 2 * j + k, uoff)
                if not first:
                    pe.wait_ge(d_free, 4 * off)
                for h in range(2):
                    s = (u + 4 + h) % 2
                    arrived(u + 4 + h, uoff)
                    for j in range(2):
                        pe.wait_ge(m_lo, j + 1 + 2 * off)
                        for t in range(TT):
                            for c in range(2):
                                rows = slice(c * S + t * P, c * S + (t + 1) * P)
                                cols = slice((2 * j + c) * 512, (2 * j + c + 1) * 512)
                                last = mm3(ps[:, 2 * h + t, :], phi[:, j, rows], plo[:, j, rows], whi[:, s, cols],
                                           wlo[:, s, cols], j == 0 and c == 0, j == 1 and c == 1)
                    last.then_inc(unit_used, 1)

            pe.wait_ge(r_ready, 1)
            expert(U_MOE, 0, 0, True)
            with pe.Fori(1, N_EXP) as e:
                expert(U_MOE, e, 6 * e, False)


def _stream(i):
    import numpy as np

    def rows(w):
        k, n = w.shape
        return w.reshape(2, 4, P, n // 512, 512).transpose(3, 0, 2, 1, 4).reshape(-1, P, UW)

    def cols(w):
        return w.reshape(DC, P, w.shape[1] // 256, 256).transpose(2, 1, 0, 3).reshape(-1, P, UW)

    ada = i["w_ada"][0].reshape(DC, P, ADA_GROUPS, UW).transpose(2, 0, 1, 3).reshape(-1, P, UW)
    w = i["w_in"][0]
    qa_ka, va = w[:, 0:2 * A_W], w[:, 2 * A_W:3 * A_W]
    b0 = 3 * A_W
    qb_kb, vb, gl = w[:, b0:b0 + 2 * D], w[:, b0 + 2 * D:b0 + 3 * D], w[:, b0 + 3 * D:]
    w = np.concatenate([qa_ka, qb_kb, gl, va, vb], axis=1)
    full = 512 * IN_BLOCKS
    pa = i["w_proj_a"][0].reshape(2, P, D).transpose(1, 0, 2).reshape(1, P, UW)
    eu = i["expert_u"][0].reshape(P, HALF, 2, DC, P).transpose(1, 4, 3, 2, 0).reshape(HALF, P, UW)
    ev = i["expert_v"][0].reshape(P, HALF, 2, D).transpose(1, 0, 2, 3).reshape(HALF, P, UW)
    peer = []
    for h in range(2):
        u, v = eu[h * NI:(h + 1) * NI], ev[h * NI:(h + 1) * NI]
        body = np.stack([u[1:], v[:-1]], axis=1).reshape(-1, P, UW)
        peer += [u[:1], body, v[-1:]]
    w2 = i["w_in_2"][0]
    wkv = i["w_kv_2"][0]
    moe = []
    for e in range(N_EXP):
        g, u = cols(i["w_gate_2"][0, e]), cols(i["w_up_2"][0, e])
        d = i["w_down_2"][0, e].reshape(4, P, 2, 512).transpose(2, 1, 0, 3).reshape(2, P, UW)
        moe += [g[:1], u[:1], g[1:], u[1:], d]
    return np.concatenate([
        ada, rows(w[:, :full]), cols(w[:, full:]), pa, rows(i["w_proj_b"][0]), rows(i["w_out"][0]),
        cols(i["w_query"][0]), *peer, cols(w2[:, :5 * CW]), rows(w2[:, 5 * CW:]), rows(i["w_out_2"][0]),
        cols(wkv[:, :D]), rows(wkv[:, D:]), cols(i["w_q_2"][0]), rows(i["w_o_2"][0]), *moe], axis=0)


def kernel(**inputs):
    import numpy as np
    import concourse.bacc as _bacc
    from concourse import mybir as _mybir
    from concourse.bass_utils import run_bass_kernel_spmd as _run

    i = {k: np.asarray(v) for k, v in inputs.items()}
    arrays = {
        "stream": _stream(i),
        "x": i["x"][0], "c": i["c"][0].reshape(DC, P).T,
        "positions": i["positions"][0].reshape(TT, P).T, "b_ada": i["b_ada"][0],
        "gains": np.concatenate([i["norm1_g"], i["norm2_g"], i["mix_norm_2"], i["mem_norm_2"], i["xattn_norm_2"],
                                 i["ffn_norm_2"], i["final_norm_2"][None]], axis=0),
        "lam": np.concatenate([i["lam_q1"], i["lam_k1"], i["lam_q2"], i["lam_k2"]], axis=0),
        "qk_gain": np.concatenate([i["qn_a"], i["kn_a"], i["qn_b"], i["kn_b"]], axis=0),
        "subln": i["subln_g"][0], "b_gate": i["b_gate"][0],
        "inv_freq": (1.0 / (10000.0 ** (np.arange(0, HD, 2, dtype=np.float32) / HD))).astype(np.float32),
        "keysT": i["sub_keys"][0].transpose(3, 0, 1, 2).reshape(P, NHH * N_KEYS),
        "conv_w": i["conv_w_2"][0].reshape(3, 4, P).transpose(2, 1, 0).reshape(P, 12),
        "hgrn_lb": i["hgrn_lb_2"].reshape(2, RH, P).transpose(2, 0, 1).reshape(P, 2 * RH),
        "hgrn_norm": i["hgrn_norm_2"][0], "mem": i["mem_2"][0],
        "router": np.concatenate([i["w_group_2"][0], i["w_expert_2"][0]], axis=1).reshape(DC, P, 20)
                    .transpose(1, 0, 2).reshape(P, DC * 20),
        "router_b": np.concatenate([i["b_group_2"][0], i["b_expert_2"][0]], axis=0),
    }
    nc = _bacc.Bacc("TRN2", target_bir_lowering=False, num_devices=1)
    io, feeds = {}, {}
    for name, a in arrays.items():
        feeds[f"in_{name}_dram"] = np.ascontiguousarray(a)
        io[name] = nc.dram_tensor(f"in_{name}_dram", a.shape, _mybir.dt.from_np(a.dtype), kind="ExternalInput").ap()
    io["out"] = nc.dram_tensor("out_dram", (S, D), _mybir.dt.float32, kind="ExternalOutput").ap()
    hybrid_block_then_mixer_memory_moe_kernel(nc, io)
    r = _run(nc, [feeds], core_ids=[0])
    return r.results[0]["out_dram"].reshape(1, S, D)
```

```python
import concourse.bass as bass
from concourse import mybir
from contextlib import ExitStack
import math

P = 128
S = 256
TT = S // P
D = 1024
DC = D // P
HD = 64
A_SLOTS, A_GROUPS = 4, 3
A_HEADS = A_SLOTS * A_GROUPS
A_DIL = (1, 4, 16)
A_REACH = 64
A_W = A_HEADS * HD
B_HEADS = 8
QK_W = 2 * A_W + 2 * D
GL_W = 2 * D
V_W = A_W + D
IN_W = QK_W + GL_W + V_W
NQK = QK_W // P
QK_HEADS = QK_W // HD
EPS = 1e-6
NEG = -1e30
LAM_INIT = 0.8 - 0.6 * math.exp(0.0)
N_KEYS, PH, TOPK = 128, 8, 16
NHH = 2 * PH
CW = 512
RH = 4
SEG = 64
LEVELS = 7
XH, XD = 4, 256
N_EXP, N_GRP, PER_GRP = 16, 4, 4
FE = 512
UW = 2048
NP = N_KEYS // 2
NB = NP // 2
GT = 8
GC = 32

ADA_GROUPS = 6 * D // UW
U_IN = ADA_GROUPS * DC
IN_BLOCKS = IN_W // 512
IN_MIXED = (ADA_GROUPS - 1) * DC


def in_at(k):
    return U_IN + k if k >= IN_MIXED else DC + 4 * (k // 2) + k % 2


U_PA = U_IN + 2 * IN_BLOCKS + 1
U_PB = U_PA + 1
U_WO = U_PB + 4
U_WQ = U_WO + 4
U_PEER = U_WQ + 8
U_MIX = U_PEER + 2 * NP
MIX_T = 5 * CW // 256
U_WO2 = U_MIX + MIX_T + 4
U_KV = U_WO2 + 4
U_XQ = U_KV + 8
U_XO = U_XQ + 4
U_MOE = U_XO + 4
NU = U_MOE + 6 * N_EXP

T_H1, T_OA, T_OB, T_MIXED, T_H2, T_MIX, T_YB, T_MEM, T_HX, T_HF = range(10)
ROWS = {t: n + 1 for n, t in enumerate(t for t in range(10) if t != T_OA)}
T_GROUPS = [4, 1, 4, 4, 4, 4, 2, 4, 4, 4]
T_BASE = [sum(T_GROUPS[:k]) for k in range(11)]
NORM_USE = [T_H1, T_H2, T_MIX, T_MEM, T_HX, T_HF]


def hybrid_block_then_mixer_memory_moe_kernel(nc, io):
    f32, f32r = mybir.dt.float32, mybir.dt.float32r
    i32, u32 = mybir.dt.int32, mybir.dt.uint32
    ALU, ACT, AX = mybir.AluOpType, mybir.ActivationFunctionType, mybir.AxisListType

    ctx = ExitStack()
    with ctx:
        def sb(name, shape, dt=f32):
            return ctx.enter_context(nc.sbuf_tensor(name, shape, dt))

        def sem(name):
            return ctx.enter_context(nc.semaphore(name))

        raw = sb("raw", [P, 2, UW])
        whi = sb("whi", [P, 2, UW], f32r)
        wlo = sb("wlo", [P, 2, UW], f32r)
        X = sb("X", [P, TT, D])
        H = sb("H", [P, TT, D])
        thi = sb("thi", [P, DC, S], f32r)
        tlo = sb("tlo", [P, DC, S], f32r)
        MOD = sb("MOD", [P, 6 * D])
        BIG = sb("BIG", [P, 16384])
        MID = sb("MID", [P, 7168])
        phi = sb("phi", [P, 2, 512], f32r)
        plo = sb("plo", [P, 2, 512], f32r)
        ident = sb("ident", [P, P])
        iota = sb("iota", [P, S])
        SM = sb("SM", [P, 276])
        ps = ctx.enter_context(nc.psum_tensor("ps", [P, 8, 512], f32))

        used_cols = [0]

        def col(n):
            used_cols[0] += n
            return SM[:, used_cols[0] - n:used_cols[0]]

        pidx = col(1)
        pidx_i = col(1).bitcast(i32)
        cT, siluc = col(DC), col(DC)
        sumsq, meansq, std, rstd = col(TT), col(TT), col(TT), col(TT)
        pos_i, pos = col(TT).bitcast(i32), col(TT)
        lam2, lam = col(2), col(1)
        a_max, a_nmax, a_sum, a_rec = col(2), col(2), col(2), col(2)
        b_max, b_sum, b_rec = col(8), col(8), col(8)
        qk_stat = col(2 * QK_HEADS)
        ob_stat = col(TT * B_HEADS)
        conv_w = col(12)
        lb2, lb, omlb = col(2 * RH), col(RH), col(RH)

        x_max, x_sum, x_rec = col(2), col(2), col(2)
        r_stat = col(8 * TT)

        big = BIG[:, :]
        mid = MID[:, :]
        mod = MOD[:, :].rearrange("p (m d) -> p m d", m=6)
        sh1, sc1, g1, sh2, sc2, g2 = (mod[:, m, :] for m in range(6))
        ada_acc = [big[:, 0:UW], mid[:, 0:UW], mid[:, UW:2 * UW]]
        ones = big[:, 16128:16128 + P]
        proj = big[:, 0:TT * IN_W].rearrange("p (t n) -> p t n", t=TT)
        lam_vec = big[:, 14848:15104].rearrange("p (k d) -> p k d", k=4)
        qk_gain = big[:, 15104:15360].rearrange("p (k d) -> p k d", k=4)
        subln = big[:, 15360:15488]
        inv_freq = big[:, 15488:15520]
        oa = big[:, 15520:15520 + TT * 256].rearrange("p (t n) -> p t n", t=TT)
        b_gate = mid[:, 4096:4096 + GL_W]
        gain = mid[:, 6144:7168]
        masks = MOD[:, 0:1024]
        rope_c = MOD[:, 1024:1536].rearrange("p (t k d) -> p t k d", t=TT, k=4)
        rope_s = MOD[:, 1536:2048].rearrange("p (t k d) -> p t k d", t=TT, k=4)
        rot = mid[:, 0:QK_W]
        ang = mid[:, 6144:6208].rearrange("p (t d) -> p t d", t=TT)
        cos = mid[:, 6208:6272].rearrange("p (t d) -> p t d", t=TT)
        sin = mid[:, 6272:6336].rearrange("p (t d) -> p t d", t=TT)
        atmp = mid[:, 6336:6400].rearrange("p (t d) -> p t d", t=TT)
        key_i = mid[:, 6400:6656].bitcast(i32)
        mtmp_i = mid[:, 6656:6912].bitcast(i32)
        qkT = mid[:, 0:NQK * S].rearrange("p (b t) -> p b t", b=NQK)
        a_s = [big[:, i * 768:(i + 1) * 768] for i in range(2)]
        a_pT = [big[:, 1536 + i * 768:1536 + (i + 1) * 768] for i in range(2)]
        b_p = [big[:, IN_W + i * 512:IN_W + (i + 1) * 512] for i in range(2)]
        b_p2 = [big[:, IN_W + 1024 + i * 512:IN_W + 1536 + i * 512] for i in range(2)]
        b_pT = [big[:, IN_W + 2048 + i * 512:IN_W + 2560 + i * 512] for i in range(2)]
        ob_sq = big[:, 0:2048]
        mixed = big[:, 0:2048].rearrange("p (t n) -> p t n", t=TT)
        lin_tmp = mid[:, 0:512]
        qT = big[:, 0:NHH * S].rearrange("p (b t) -> p b t", b=NHH)
        keysT = big[:, 4096:4096 + NHH * N_KEYS].rearrange("p (b n) -> p b n", b=NHH)
        score = [mid[:, t * 2048:(t + 1) * 2048] for t in range(TT)]
        cand = mid[:, 4096:6144]
        top_v = [MOD[:, 2048 + t * 256:2304 + t * 256].rearrange("p (b k) -> p b k", b=NHH) for t in range(TT)]
        top_i = [MOD[:, 2560 + t * 256:2816 + t * 256].bitcast(u32).rearrange("p (b k) -> p b k", b=NHH)
                 for t in range(TT)]
        top_f = MOD[:, 3072:3328].rearrange("p (h s k) -> p h s k", h=PH, s=2)
        best_v = MOD[:, 3328:3456].rearrange("p (h k) -> p h k", h=PH)
        best_i = MOD[:, 3456:3584].bitcast(u32).rearrange("p (h k) -> p h k", h=PH)
        half_i = MOD[:, 3584:3712].bitcast(u32)
        half_f = [MOD[:, 3712:3840], MOD[:, 3840:3968]]
        gate_e = MOD[:, 3968:4096].rearrange("p (h k) -> p h k", h=PH)
        gate_s, gate_r = MOD[:, 4096:4104], MOD[:, 4104:4112]
        route = MOD[:, 0:768].rearrange("p (t q k) -> p t q k", t=TT, q=3)
        routeT = MOD[:, 1024:1792].rearrange("p (q t) -> p q t", q=3)
        G = big.rearrange("p (j t) -> p j t", t=S)
        one_a = [mid[:, i * 1024:(i + 1) * 1024].rearrange("p (t n) -> p t n", t=GT) for i in range(2)]
        one_b = [mid[:, 2048 + i * 1024:3072 + i * 1024].rearrange("p (t n) -> p t n", t=GT) for i in range(2)]
        g_stage = [a.rearrange("p (j t) -> p j t", t=GC)
                   for a in (H[:, :, :].rearrange("p t n -> p (t n)"), MOD[:, 2048:4096])]
        g_spill = nc.dram_tensor("g_spill", (S // GC, P, N_KEYS // 2, GC), f32).ap()
        act_s = [mid[:, 4096 + i * 512:4608 + i * 512] for i in range(2)]
        act_w = [mid[:, 5120 + i * 512:5632 + i * 512] for i in range(2)]
        mixT = big[:, 0:20 * S].rearrange("p (b t) -> p b t", b=20)
        cb, cc, cx, hq, hz = (mixT[:, 4 * k:4 * k + 4, :] for k in range(5))
        hv = big[:, 5120:6144].rearrange("p (t n) -> p t n", t=TT)
        hg = big[:, 6144:7168].rearrange("p (t n) -> p t n", t=TT)
        conv_u = big[:, 7168:8192].rearrange("p (b t) -> p b t", b=4)
        conv_y = big[:, 8192:9216].rearrange("p (b t) -> p b t", b=4)
        sig = big[:, 9216:10240].rearrange("p (b t) -> p b t", b=4)
        dec = big[:, 10240:11264].rearrange("p (b t) -> p b t", b=4)
        rk = big[:, 11264:12288].rearrange("p (b t) -> p b t", b=4)
        lev_e = [big[:, 12288 + i * 1024:13312 + i * 1024].rearrange("p (b t) -> p b t", b=4) for i in range(2)]
        lev_q = big[:, 14336:15360].rearrange("p (b t) -> p b t", b=4)
        lev_k = big[:, 15360:16384].rearrange("p (b t) -> p b t", b=4)
        lmask = mid[:, 0:1024].rearrange("p (l t) -> p l t", l=8)
        lev_t = mid[:, 1024:2048].rearrange("p (t h n) -> p t h n", t=TT, h=RH)
        rsc = mid[:, 2048:3072].rearrange("p (t h n) -> p t h n", t=TT, h=RH)
        rsc_x = mid[:, 3072:3584].rearrange("p (h n) -> p h n", h=RH)
        keep = mid[:, 3584:3840]
        lint = mid[:, 3840:3968].bitcast(i32)
        lsh = mid[:, 3968:4096].bitcast(i32)
        lup = mid[:, 4096:4224]
        hnorm = mid[:, 4608:5120]
        ro = mid[:, 5120:6144].rearrange("p (t n) -> p t n", t=TT)
        mem = MOD[:, 0:2048].rearrange("p (t n) -> p t n", t=TT)
        kT = MOD[:, 2048:4096].rearrange("p (b t) -> p b t", b=DC)
        vm = MOD[:, 4096:6144].rearrange("p (t n) -> p t n", t=TT)
        xqT = big[:, 0:2048].rearrange("p (b t) -> p b t", b=DC)
        x_p = [big[:, 2048 + i * 256:2304 + i * 256] for i in range(2)]
        x_pT = [big[:, 2560 + i * 512:3072 + i * 512].rearrange("p (k t) -> p k t", k=TT) for i in range(2)]
        wr = big[:, 8192:8192 + DC * 20].rearrange("p (c n) -> p c n", c=DC)
        r_bias = big[:, 8400:8420]
        r_log = big[:, 8448:8488].rearrange("p (t n) -> p t n", t=TT)
        r_prob = big[:, 8512:8552].rearrange("p (t n) -> p t n", t=TT)
        r_cmp = big[:, 8576:8576 + TT * 80].rearrange("p (t g a b) -> p t g a b", t=TT, g=5, a=4)
        r_tie = big[:, 8768:8768 + TT * 80].rearrange("p (t g a b) -> p t g a b", t=TT, g=5, a=4)
        r_rank = big[:, 8960:9000].rearrange("p (t n) -> p t n", t=TT)
        r_sel = big[:, 9024:9064].rearrange("p (t n) -> p t n", t=TT)
        r_low = big[:, 9088:9104].rearrange("p (a b) -> p a b", a=4)
        comb = big[:, 9152:9152 + TT * N_EXP].rearrange("p (t n) -> p t n", t=TT)
        silu_g = [big[:, i * 512:(i + 1) * 512] for i in range(2)]
        hid = [big[:, 1024 + i * 512:1536 + i * 512] for i in range(2)]
        wrhi = sb("wrhi", [P, DC, 20], f32r)
        wrlo = sb("wrlo", [P, DC, 20], f32r)

        raw_loaded = [sem("raw_loaded0"), sem("raw_loaded1")]
        unit_hi, unit_split, unit_used = sem("unit_hi"), sem("unit_split"), sem("unit_used")
        x_loaded, c_loaded, rows_loaded, gain_loaded = (
            sem("x_loaded"), sem("c_loaded"), sem("rows_loaded"), sem("gain_loaded"))
        keys_loaded, mix_loaded, mem_loaded, router_loaded = (
            sem("keys_loaded"), sem("mix_loaded"), sem("mem_loaded"), sem("router_loaded"))
        pool_chain, consts_ready = sem("pool_chain"), sem("consts_ready")
        dve_chain, act_chain = sem("dve_chain"), sem("act_chain")
        siluc_ready, ones_ready = sem("siluc_ready"), sem("ones_ready")
        ada_zeroed, b_ada_loaded = sem("ada_zeroed"), sem("b_ada_loaded")
        ada_full, ada_free = sem("ada_full"), sem("ada_free")
        x_ready, norm_ss, norm_ms, norm_std = sem("x_ready"), sem("norm_ss"), sem("norm_ms"), sem("norm_std")
        rows_ready, tr_done, tr_hi, tr_lo = sem("rows_ready"), sem("tr_done"), sem("tr_hi"), sem("tr_lo")
        acc_free, keys_scored = sem("acc_free"), sem("keys_scored")
        angles_ready, sincos_ready, lam_dots, lam_exp = (
            sem("angles_ready"), sem("sincos_ready"), sem("lam_dots"), sem("lam_exp"))
        qk_sq, qk_summed, qk_ms, qk_std, rope_done = (
            sem("qk_sq"), sem("qk_summed"), sem("qk_ms"), sem("qk_std"), sem("rope_done"))
        gate_biased, gate_ready = sem("gate_biased"), sem("gate_ready")
        qkT_done, qkT_even, qkT_odd = sem("qkT_done"), sem("qkT_even"), sem("qkT_odd")
        a_scored, a_masked, a_prob, a_tr, a_trT, a_pv, a_out = (
            sem("a_scored"), sem("a_masked"), sem("a_prob"), sem("a_tr"), sem("a_trT"), sem("a_pv"), sem("a_out"))
        b_scored, b_bias, b_prob, b_mix, b_tr, b_trT, b_pv, b_out = (
            sem("b_scored"), sem("b_bias"), sem("b_prob"), sem("b_mix"), sem("b_tr"), sem("b_trT"),
            sem("b_pv"), sem("b_out"))
        ob_sqd, ob_ms, ob_std = sem("ob_sqd"), sem("ob_ms"), sem("ob_std")
        gate_shift, gate_exp, routed, route_tr, route_in = (
            sem("gate_shift"), sem("gate_exp"), sem("routed"), sem("route_tr"), sem("route_in"))
        oa_ready, ob_ready, g_full, g_free = sem("oa_ready"), sem("ob_ready"), sem("g_full"), sem("g_free")
        g_spilled, g_loaded = [sem("g_spilled0"), sem("g_spilled1")], sem("g_loaded")
        gelu_done, w_done, w_hi, w_lo = sem("gelu_done"), sem("w_done"), sem("w_hi"), sem("w_lo")
        lb_diff, lb_exp, z_exp, f_ready, f_log, lev_d, lev_exp, lev_qk, lev_full, lev_free = (
            sem("lb_diff"), sem("lb_exp"), sem("z_exp"), sem("f_ready"), sem("f_log"), sem("lev_d"), sem("lev_exp"), sem("lev_qk"),
            sem("lev_full"), sem("lev_free"))
        conv_ready, conv_hi, conv_lo, sc_ready, ro_full, ro_copied, ro_sq, ro_ms, ro_std = (
            sem("conv_ready"), sem("conv_hi"), sem("conv_lo"), sem("sc_ready"), sem("ro_full"),
            sem("ro_copied"), sem("ro_sq"), sem("ro_ms"), sem("ro_std"))
        x_scored, x_bias, x_prob, x_norm, x_tr, x_trT, xo_full, xo_hi, xo_lo = (
            sem("x_scored"), sem("x_bias"), sem("x_prob"), sem("x_norm"), sem("x_tr"), sem("x_trT"),
            sem("xo_full"), sem("xo_hi"), sem("xo_lo"))
        wr_hi, wr_lo, r_full, r_ready, r_exp = (
            sem("wr_hi"), sem("wr_lo"), sem("r_full"), sem("r_ready"), sem("r_exp"))
        m_silu, m_hid, m_hi, m_lo, d_free = sem("m_silu"), sem("m_hid"), sem("m_hi"), sem("m_lo"), sem("d_free")
        out_ready, out_stored = sem("out_ready"), sem("out_stored")

        N_IN = 0
        N_PA = N_IN + 2 * (IN_BLOCKS + 1)
        N_PB = N_PA + 4
        N_WO = N_PB + 4
        N_WQ = N_WO + 4

        def n_query(h):
            return N_WQ + max(0, 2 * h - 1)

        def n_scores(h):
            return N_WQ + min(2 * h + 2, 2 * PH - 1)

        N_MT = N_WQ + 2 * PH
        N_MV = N_MT + MIX_T
        N_W2 = N_MV + 4
        N_K = N_W2 + 4
        N_V = N_K + 4
        N_XQ = N_V + 4
        N_XO = N_XQ + 4
        SPLIT_U = U_IN

        GL0, V0 = QK_W, QK_W + GL_W

        block = ctx.enter_context(nc.Block())

        @block.sync
        def _(sp):
            stream = io["stream"]
            for k in range(2):
                sp.dma_start(raw[:, k, :], stream[k, :, :]).then_inc(raw_loaded[k], 16)
            with sp.Fori(1, NU // 2) as i:
                for k in range(2):
                    sp.wait_ge(unit_split, 2 * i + (k - 1))
                    sp.dma_start(raw[:, k, :], stream[bass.ds(2 * i + k, 1), :, :].rearrange("a p n -> (a p) n")
                                 ).then_inc(raw_loaded[k], 16)
            sp.wait_ge(out_ready, 1)
            sp.dma_start(io["out"].rearrange("(t p) d -> p t d", p=P), H[:, :, :]).then_inc(out_stored, 16)
            sp.wait_ge(out_stored, 16)

        @block.gpsimd
        def _(pool):
            nc.gpsimd.iota(iota[:, :], [[1, S]], base=0, channel_multiplier=0,
                           allow_small_or_imprecise_dtypes=True).then_inc(consts_ready, 1)
            nc.gpsimd.iota(pidx, [[0, 1]], base=0, channel_multiplier=1,
                           allow_small_or_imprecise_dtypes=True).then_inc(consts_ready, 1)
            nc.gpsimd.memset(ident[:, :], 0.0).then_inc(pool_chain, 1)
            pool.wait_ge(pool_chain, 1)
            nc.gpsimd.affine_select(out=ident[:, :], in_=ident[:, :], compare_op=ALU.not_equal, fill=1.0, base=0,
                                    pattern=[[-1, P]], channel_multiplier=1).then_inc(consts_ready, 1)

            def load_gain(j):
                pool.dma_start(gain, io["gains"][j, :].partition_broadcast(P)).then_inc(gain_loaded, 16)

            load_gain(0)
            pool.wait_ge(rope_done, TT)
            pool.wait_ge(rows_ready, ROWS[T_OB])
            load_gain(1)
            pool.wait_ge(rows_ready, ROWS[T_MIXED])
            pool.dma_start(keysT, io["keysT"].rearrange("p (b n) -> p b n", b=NHH)).then_inc(keys_loaded, 16)
            pool.wait_ge(rows_ready, ROWS[T_H2])
            load_gain(2)
            for b in range(2):
                pool.wait_ge(g_spilled[b], 16 * (S // GC // 2))
            with pool.Fori(0, NB) as i:
                pool.wait_ge(w_done, i + 1)
                for j in range(2):
                    pool.dma_start(G[:, bass.ds(2 * i + j, 1), :].rearrange("p j (c t) -> p (j c) t", t=GC),
                                   g_spill[:, :, bass.ds(2 * i + j, 1), :].rearrange("c p j t -> p (c j) t")
                                   ).then_inc(g_loaded, 16)
            pool.wait_ge(x_ready, 2)
            pool.dma_start(conv_w, io["conv_w"]).then_inc(mix_loaded, 16)
            pool.dma_start(lb2, io["hgrn_lb"]).then_inc(mix_loaded, 16)
            pool.dma_start(hnorm, io["hgrn_norm"].partition_broadcast(P)).then_inc(mix_loaded, 16)
            pool.dma_start(mem, io["mem"].rearrange("(t p) d -> p t d", p=P)).then_inc(mem_loaded, 16)
            pool.wait_ge(rows_ready, ROWS[T_MIX])
            load_gain(3)
            pool.wait_ge(rows_ready, ROWS[T_MEM])
            load_gain(4)
            pool.wait_ge(rows_ready, ROWS[T_HX])
            load_gain(5)
            pool.dma_start(wr[:, :, :], io["router"].rearrange("p (c n) -> p c n", c=DC)).then_inc(router_loaded, 16)
            pool.dma_start(r_bias, io["router_b"].partition_broadcast(P)).then_inc(router_loaded, 16)
            pool.wait_ge(rows_ready, ROWS[T_HF])
            load_gain(6)

        @block.scalar
        def _(act):
            chain = [0]

            def mark(ins):
                chain[0] += 1
                ins.then_inc(act_chain, 1)

            def settle():
                act.wait_ge(act_chain, chain[0])

            def hi(u, off=0, at=None, at_off=None):
                s = u - SPLIT_U
                at, at_off = (u, off) if at is None else (at, at_off)
                act.wait_ge(raw_loaded[u % 2], 16 * (at // 2 + 1) + 8 * at_off)
                if s >= 2:
                    act.wait_ge(unit_used, s - 1 + off)
                nc.scalar.activation(whi[:, u % 2, :], raw[:, u % 2, :], ACT.Copy).then_inc(unit_hi, 1)

            def used(u, off=0):
                act.wait_ge(unit_used, u - SPLIT_U + 1 + off)

            def evac(n, u, out, func=ACT.Copy, uoff=0, width=512):
                used(u, uoff)
                nc.scalar.activation(out, ps[:, n % 4, 0:width], func).then_inc(acc_free, 1)

            def norm(j, src, ready):
                act.wait_ge(*ready)
                for t in range(TT):
                    nc.scalar.activation(H[:, t, :], src[:, t, :], ACT.Square,
                                         accum_out=sumsq[:, t:t + 1]).then_inc(norm_ss, 1)
                act.wait_ge(norm_ms, j + 1)
                nc.scalar.activation(std, meansq, ACT.Sqrt).then_inc(norm_std, 1)

            def tr_high(t, first=0, skip=0):
                for k in range(T_GROUPS[t]):
                    g = T_BASE[t] + k
                    act.wait_ge(tr_done, g + 1)
                    nc.scalar.activation(thi[:, first + 2 * k:first + 2 * k + 2, :].rearrange("p c t -> p (c t)"),
                                         ps[:, 4 + g % 2, :], ACT.Copy).then_inc(tr_hi, 1)

            act.dma_start(cT, io["c"]).then_inc(c_loaded, 16)
            act.dma_start(X[:, :, :], io["x"].rearrange("(t p) d -> p t d", p=P)).then_inc(x_loaded, 16)
            act.wait_ge(ada_zeroed, 1)
            act.dma_start(ada_acc[0][0:1, :], io["b_ada"][0:UW].rearrange("(a n) -> a n", a=1)).then_inc(b_ada_loaded, 16)
            act.wait_ge(ada_zeroed, 2)
            act.dma_start(mid[0:1, 0:2 * UW], io["b_ada"][UW:3 * UW].rearrange("(a n) -> a n", a=1)
                          ).then_inc(b_ada_loaded, 16)
            act.dma_start(lam_vec, io["lam"].partition_broadcast(P)).then_inc(rows_loaded, 16)
            act.dma_start(qk_gain, io["qk_gain"].partition_broadcast(P)).then_inc(rows_loaded, 16)
            act.dma_start(subln, io["subln"].partition_broadcast(P)).then_inc(rows_loaded, 16)
            act.dma_start(inv_freq, io["inv_freq"].partition_broadcast(P)).then_inc(rows_loaded, 16)
            act.dma_start(b_gate, io["b_gate"].partition_broadcast(P)).then_inc(rows_loaded, 16)
            act.dma_start(pos_i, io["positions"]).then_inc(rows_loaded, 16)

            act.wait_ge(c_loaded, 16)
            nc.scalar.activation(siluc, cT, ACT.Silu).then_inc(siluc_ready, 1)
            norm(0, X, (x_loaded, 16))
            hi(U_IN, 0, in_at(0), 0)
            hi(U_IN + 1, 0, in_at(1), 0)
            tr_high(T_H1)

            with act.Fori(0, IN_MIXED // 4) as i:
                for b in range(2):
                    hi(U_IN + 2 * b + 2, 4 * i, in_at(2 * b + 2), 8 * i)
                    hi(U_IN + 2 * b + 3, 4 * i, in_at(2 * b + 3), 8 * i)
                    for t in range(TT):
                        evac(2 * b + t, U_IN + 2 * b + 1, proj[:, t, bass.ds(1024 * i + 512 * b, 512)], uoff=4 * i)

            def in_block(b):
                hi(U_IN + 2 * b + 2)
                if b < IN_BLOCKS:
                    hi(U_IN + 2 * b + 3)
                w = 512 if b < IN_BLOCKS else 256
                for t in range(TT):
                    evac(2 * b + t, min(U_IN + 2 * b + 1, U_PA - 1), proj[:, t, 512 * b:512 * b + w], width=w)

            in_block(8)
            act.wait_ge(angles_ready, 1)
            nc.scalar.activation(sin, ang, ACT.Sin).then_inc(sincos_ready, 1)
            nc.scalar.activation(cos, atmp, ACT.Sin).then_inc(sincos_ready, 1)
            act.wait_ge(lam_dots, 1)
            nc.scalar.activation(lam2, lam2, ACT.Exp).then_inc(lam_exp, 1)
            in_block(9)
            act.wait_ge(acc_free, 2 * (QK_W // 512))
            for t in range(TT):
                if t:
                    act.wait_ge(rope_done, t)
                nc.scalar.activation(rot, proj[:, t, 0:QK_W], ACT.Square).then_inc(qk_sq, 1)
                act.wait_ge(qk_ms, t + 1)
                nc.scalar.activation(qk_stat[:, t * QK_HEADS:(t + 1) * QK_HEADS],
                                     qk_stat[:, t * QK_HEADS:(t + 1) * QK_HEADS], ACT.Sqrt).then_inc(qk_std, 1)
                in_block(10 + 2 * t)
                in_block(11 + 2 * t)
            in_block(14)
            act.wait_ge(gate_biased, 1)
            for t in range(TT):
                nc.scalar.activation(proj[:, t, GL0:GL0 + GL_W], proj[:, t, GL0:GL0 + GL_W],
                                     ACT.Sigmoid).then_inc(gate_ready, 1)

            for g in range(0, NQK // 4 * TT, 2):
                act.wait_ge(qkT_done, g + 1)
                t, b4 = g % TT, g // TT
                nc.scalar.activation(qkT[:, 4 * b4:4 * b4 + 4, t * P:(t + 1) * P],
                                     ps[:, 4, :].rearrange("p (b t) -> p b t", b=4), ACT.Copy).then_inc(qkT_even, 1)

            for i in range(A_SLOTS * TT):
                act.wait_ge(a_masked, i + 1)
                nc.scalar.activation(a_s[i % 2], a_s[i % 2], ACT.Exp, bias=a_nmax[:, i % 2:i % 2 + 1],
                                     accum_out=a_sum[:, i % 2:i % 2 + 1]).then_inc(a_prob, 1)

            def b_copy(h):
                act.wait_ge(b_tr, h + 1)
                nc.scalar.activation(b_pT[h % 2], ps[:, 4 + h % 2, :], ACT.Copy).then_inc(b_trT, 1)

            for h in range(B_HEADS):
                act.wait_ge(b_bias, h + 1)
                if h >= 2:
                    act.wait_ge(b_tr, h - 1)
                for t in range(TT):
                    for m in range(2):
                        k = 4 * (h % 2) + 2 * m + t
                        nc.scalar.activation((b_p, b_p2)[m][h % 2][:, t * S:(t + 1) * S],
                                             ps[:, 2 * (h % 2) + m, t * S:(t + 1) * S], ACT.Exp,
                                             bias=b_max[:, k:k + 1], scale=HD ** -0.5,
                                             accum_out=b_sum[:, k:k + 1]).then_inc(b_prob, 1)
                if h:
                    b_copy(h - 1)
            b_copy(B_HEADS - 1)
            act.wait_ge(b_out, B_HEADS)
            nc.scalar.activation(ob_sq, H[:, :, :].rearrange("p t n -> p (t n)"), ACT.Square).then_inc(ob_sqd, 1)
            act.wait_ge(ob_ms, 1)
            nc.scalar.activation(ob_stat, ob_stat, ACT.Sqrt).then_inc(ob_std, 1)

            tr_high(T_OA)
            hi(U_PA + 2)
            tr_high(T_OB)
            for u in range(U_PB, U_WO):
                hi(u + 2)
            tr_high(T_MIXED)
            for u in range(U_WO, U_WQ):
                hi(u + 2)

            norm(1, X, (x_ready, 1))
            tr_high(T_H2)
            def head_scores(h):
                act.wait_ge(keys_scored, h + 1)
                nc.scalar.activation(mid[:, 0:TT * 2048].rearrange("p (t n) -> p t n", t=TT)[:, :, 256 * h:256 * (h + 1)],
                                     ps[:, n_scores(h) % 4, :].rearrange("p (t n) -> p t n", t=TT), ACT.Copy
                                     ).then_inc(acc_free, 1)

            for h in range(PH):
                hi(U_WQ + h + 2)
                evac(n_query(h), U_WQ + h, qT[:, 2 * h:2 * h + 2, :].rearrange("p b t -> p (b t)"))
                if h:
                    head_scores(h - 1)
            head_scores(PH - 1)
            for t in range(TT):
                act.wait_ge(gate_shift, t + 1)
                nc.scalar.activation(gate_e, gate_e, ACT.Exp).then_inc(gate_exp, 1)
            for q in range(3):
                act.wait_ge(route_tr, q + 1)
                nc.scalar.activation(routeT[:, q, :], ps[:, 4 + q % 2, 0:S], ACT.Copy).then_inc(route_in, 1)

            def gates_out(i, first):
                per = GC // GT
                for b in range(2):
                    for k in range(per):
                        n = b * per + k
                        act.wait_ge(g_full, 2 * per * i + (n + 1))
                        got = (ps[:, 4 + 2 * (n % 2):6 + 2 * (n % 2), :].rearrange("p a n -> p (a n)")
                               .rearrange("p (t j) -> p j t", j=N_KEYS))
                        nc.scalar.activation(G[:, :, bass.ds(2 * GC * i + n * GT, GT)], got[:, 0:2 * NB, :],
                                             ACT.Copy).then_inc(g_free, 1)
                        if k == 0 and not first:
                            act.wait_ge(g_spilled[b], 16 * i)
                        nc.scalar.activation(g_stage[b][:, :, k * GT:(k + 1) * GT], got[:, 2 * NB:, :],
                                             ACT.Copy).then_inc(g_free, 1)
                    act.wait_ge(g_free, 4 * per * i + 2 * per * (b + 1))
                    act.dma_start(g_spill[bass.ds(2 * i + b, 1), :, :, :].rearrange("c p j t -> (c p) j t"),
                                  g_stage[b]).then_inc(g_spilled[b], 16)

            gates_out(0, True)
            with act.Fori(1, S // (2 * GC)) as i:
                gates_out(i, False)
            u0 = U_PEER

            def expert_act(i, off=0):
                used(u0 if i == 0 else u0 + 2 * i - 1, 2 * off)
                nc.scalar.activation(act_s[i % 2], ps[:, 4 + i % 2, :], ACT.Gelu).then_inc(gelu_done, 1)
                act.wait_ge(w_done, i + 1 + off)
                nc.scalar.activation(phi[:, i % 2, :], act_w[i % 2], ACT.Copy).then_inc(w_hi, 1)

            hi(u0 + 2)
            expert_act(0)
            hi(u0 + 3)
            expert_act(1)
            hi(u0 + 4)
            with act.Fori(0, (NP - 2) // 2) as r:
                for k in (1, 2):
                    hi(u0 + 2 * k + 3, 4 * r)
                    expert_act(k + 1, 2 * r)
                    hi(u0 + 2 * k + 4, 4 * r)
            hi(u0 + 2 * NP + 1)

            norm(2, X, (x_ready, 2))
            tr_high(T_MIX)
            for u in range(MIX_T):
                hi(U_MIX + u + 2)
                evac(N_MT + u, U_MIX + u, mixT[:, 2 * u:2 * u + 2, :].rearrange("p b t -> p (b t)"))
            for b in range(2):
                hi(U_MIX + MIX_T + 2 * b + 2)
                hi(U_MIX + MIX_T + 2 * b + 3)
                for t in range(TT):
                    if b == 0:
                        evac(N_MV + t, U_MIX + MIX_T + 1, hv[:, t, :])
                    else:
                        evac(N_MV + 2 + t, U_MIX + MIX_T + 3, hg[:, t, :], ACT.Silu)
            act.wait_ge(lb_diff, 1)
            nc.scalar.activation(lb, lb, ACT.Exp).then_inc(lb_exp, 1)
            act.wait_ge(acc_free, N_MT + MIX_T)
            nc.scalar.activation(sig, hz, ACT.Exp, scale=-1.0).then_inc(z_exp, 1)
            nc.scalar.activation(rk, hz, ACT.Exp).then_inc(z_exp, 1)
            act.wait_ge(f_ready, 1)
            nc.scalar.activation(dec, sig, ACT.Ln).then_inc(f_log, 1)
            act.wait_ge(conv_ready, 1)
            used(U_WO2 - 1)
            nc.scalar.activation(thi[:, 0:4, :], conv_y, ACT.Copy).then_inc(conv_hi, 1)
            for l in range(1, LEVELS + 2):
                act.wait_ge(lev_d, l)
                nc.scalar.activation(lev_e[l % 2], lev_e[l % 2], ACT.Exp, scale=-1.0).then_inc(lev_exp, 1)
            for t in range(TT):
                act.wait_ge(ro_full, t + 1)
                nc.scalar.activation(ro[:, t, :], ps[:, t, :], ACT.Copy).then_inc(ro_copied, 1)
            act.wait_ge(ro_copied, TT)
            nc.scalar.activation(lev_q.rearrange("p b t -> p (b t)"), ro.rearrange("p t n -> p (t n)"),
                                 ACT.Square).then_inc(ro_sq, 1)
            act.wait_ge(ro_ms, 1)
            nc.scalar.activation(r_stat[:, 0:TT * RH], r_stat[:, 0:TT * RH], ACT.Sqrt).then_inc(ro_std, 1)
            tr_high(T_YB, 4)
            for u in range(U_WO2, U_KV):
                hi(u + 2)

            norm(3, mem, (mem_loaded, 16))
            tr_high(T_MEM)
            for u in range(4):
                hi(U_KV + u + 2)
                evac(N_K + u, U_KV + u, kT[:, 2 * u:2 * u + 2, :].rearrange("p b t -> p (b t)"))
            for b in range(2):
                hi(U_KV + 4 + 2 * b + 2)
                hi(U_KV + 4 + 2 * b + 3)
                for t in range(TT):
                    evac(N_V + 2 * b + t, U_KV + 4 + 2 * b + 1, vm[:, t, 512 * b:512 * (b + 1)])
            norm(4, X, (acc_free, N_W2 + 4))
            tr_high(T_HX)
            for u in range(4):
                hi(U_XQ + u + 2)
                evac(N_XQ + u, U_XQ + u, xqT[:, 2 * u:2 * u + 2, :].rearrange("p b t -> p (b t)"))
            for i in range(XH * TT):
                act.wait_ge(x_bias, i + 1)
                nc.scalar.activation(x_p[i % 2], ps[:, i % 2, 0:S], ACT.Exp, bias=x_max[:, i % 2:i % 2 + 1],
                                     scale=XD ** -0.5, accum_out=x_sum[:, i % 2:i % 2 + 1]).then_inc(x_prob, 1)
                act.wait_ge(x_tr, i + 1)
                h, t = i // TT, i % TT
                nc.scalar.activation(x_pT[h % 2][:, :, t * P:(t + 1) * P],
                                     ps[:, 4 + i % 2, 0:S].rearrange("p (k t) -> p k t", k=TT),
                                     ACT.Copy).then_inc(x_trT, 1)
                if t == TT - 1:
                    act.wait_ge(xo_full, h + 1)
                    nc.scalar.activation(thi[:, 2 * h:2 * h + 2, :].rearrange("p c t -> p (c t)"),
                                         ps[:, 6 + h % 2, :], ACT.Copy).then_inc(xo_hi, 1)
            for u in range(U_XO, U_MOE):
                hi(u + 2)

            act.wait_ge(router_loaded, 32)
            nc.scalar.activation(wrhi[:, :, :], wr, ACT.Copy).then_inc(wr_hi, 1)
            norm(5, X, (acc_free, N_XO + 4))
            tr_high(T_HF)
            act.wait_ge(r_ready, 1)
            nc.scalar.activation(r_prob, r_log, ACT.Exp).then_inc(r_exp, 1)

            def expert(u, off, uoff, last):
                for j in range(2):
                    used(u + 2 * j, uoff)
                    nc.scalar.activation(silu_g[j], ps[:, 4 + 2 * j, :], ACT.Silu).then_inc(m_silu, 1)
                    hi(u + 2 * j + 2, uoff)
                    hi(u + 2 * j + 3, uoff)
                    act.wait_ge(m_hid, j + 1 + 2 * off)
                    nc.scalar.activation(phi[:, j, :], hid[j], ACT.Copy).then_inc(m_hi, 1)
                if not last:
                    hi(u + 6, uoff)
                    hi(u + 7, uoff)

            with act.Fori(0, N_EXP - 1) as e:
                expert(U_MOE, e, 6 * e, False)
            expert(U_MOE + 6 * (N_EXP - 1), N_EXP - 1, 0, True)
            norm(6, X, (d_free, 4 * N_EXP))

        @block.vector
        def _(dve):
            chain = [0]

            def mark(ins):
                chain[0] += 1
                ins.then_inc(dve_chain, 1)

            def settle():
                dve.wait_ge(dve_chain, chain[0])

            def lo(u, off=0):
                s = u - SPLIT_U
                dve.wait_ge(unit_hi, s + 1 + off)
                nc.vector.tensor_tensor(wlo[:, u % 2, :], raw[:, u % 2, :], whi[:, u % 2, :].bitcast(f32),
                                        ALU.subtract).then_inc(unit_split, 1)

            def used(u, off=0):
                dve.wait_ge(unit_used, u - SPLIT_U + 1 + off)

            def tr_low(t, first=0):
                for k in range(T_GROUPS[t]):
                    g = T_BASE[t] + k
                    dve.wait_ge(tr_hi, g + 1)
                    c = first + 2 * k
                    nc.vector.tensor_tensor(tlo[:, c:c + 2, :], ps[:, 4 + g % 2, :].rearrange("p (c t) -> p c t", c=2),
                                            thi[:, c:c + 2, :].bitcast(f32), ALU.subtract).then_inc(tr_lo, 1)

            def norm(j, src, out_sem, scale=None, shift=None):
                dve.wait_ge(norm_ss, TT * (j + 1))
                nc.vector.tensor_scalar(meansq, sumsq, 1.0 / D, EPS, ALU.mult, ALU.add).then_inc(norm_ms, 1)
                dve.wait_ge(norm_std, j + 1)
                mark(nc.vector.reciprocal(rstd, std))
                dve.wait_ge(gain_loaded, 16 * (j + 1))
                settle()
                for t in range(TT):
                    last = nc.vector.scalar_tensor_tensor(H[:, t, :], src[:, t, :], rstd[:, t:t + 1], gain,
                                                          ALU.mult, ALU.mult)
                    if scale is None and t == TT - 1:
                        last.then_inc(out_sem, 1)
                    else:
                        mark(last)
                if scale is not None:
                    settle()
                    for t in range(TT):
                        mark(nc.vector.tensor_tensor(H[:, t, :], H[:, t, :], scale, ALU.mult))
                    settle()
                    for t in range(TT):
                        last = nc.vector.tensor_tensor(H[:, t, :], H[:, t, :], shift, ALU.add)
                        if t == TT - 1:
                            last.then_inc(out_sem, 1)
                        else:
                            mark(last)

            def root_mean(stat, width, ready, ms, rooted, count):
                dve.wait_ge(*ready)
                nc.vector.tensor_scalar(stat, stat, 1.0 / width, EPS, ALU.mult, ALU.add).then_inc(ms, 1)
                dve.wait_ge(rooted, count)
                mark(nc.vector.reciprocal(stat, stat))
                settle()

            nc.vector.memset(ada_acc[0], 0.0).then_inc(ada_zeroed, 1)
            dve.wait_ge(ada_zeroed, 1)
            nc.vector.memset(mid[:, 0:2 * UW], 0.0).then_inc(ada_zeroed, 1)
            nc.vector.memset(ones, 1.0).then_inc(ones_ready, 1)
            dve.wait_ge(siluc_ready, 1)
            dve.wait_ge(b_ada_loaded, 32)

            def ada_sum(g, at, c, at_off, c_off, back):
                dve.wait_ge(raw_loaded[at % 2], 16 * (at // 2 + 1) + 8 * at_off)
                if at + 1 > back:
                    dve.wait_ge(unit_split, at + 1 - back + at_off)
                column = siluc[:, c:c + 1] if c_off is None else siluc[:, bass.ds(c_off + c, 1)]
                nc.vector.scalar_tensor_tensor(ada_acc[g], raw[:, at % 2, :], column, ada_acc[g],
                                               ALU.mult, ALU.add).then_inc(unit_split, 1)

            def ada_rows(g):
                dve.wait_ge(ada_full, g + 1)
                for m in range(4):
                    row = 4 * g + m
                    plus = 1.0 if row // 2 in (1, 4) else 0.0
                    nc.vector.tensor_scalar(MOD[:, row * 512:(row + 1) * 512], ps[:, 4 + m, :], plus, None,
                                            ALU.add).then_inc(ada_free, 1)

            for c in range(DC):
                ada_sum(0, c, c, 0, None, 1)
            ada_rows(0)

            dve.wait_ge(ada_free, 4)
            norm(0, X, rows_ready, sc1, sh1)
            lo(U_IN)
            lo(U_IN + 1)
            tr_low(T_H1)

            for g in range(1, ADA_GROUPS):
                with dve.Fori(0, DC // 4) as i:
                    for b in range(2):
                        for k in range(2):
                            ada_sum(g, in_at(2 * b + k) + 2 + 16 * (g - 1), 2 * b + k, 8 * i, 4 * i, 1 if k else 3)
                        for k in range(2):
                            lo(U_IN + 8 * (g - 1) + 2 * b + k + 2, 4 * i)

            def in_block(b):
                lo(U_IN + 2 * b + 2)
                if b < IN_BLOCKS:
                    lo(U_IN + 2 * b + 3)

            ada_rows(1)
            in_block(8)
            ada_rows(2)
            dve.wait_ge(rows_loaded, 16 * 6)
            dve.wait_ge(rows_ready, ROWS[T_H1])
            dve.wait_ge(consts_ready, 3)
            mark(nc.vector.tensor_copy(pos, pos_i))
            mark(nc.vector.tensor_copy(pidx_i, pidx))
            mark(nc.vector.tensor_copy(key_i, iota[:, :]))
            settle()
            for t in range(TT):
                mark(nc.vector.tensor_scalar(ang[:, t, :], inv_freq, pos[:, t:t + 1], None, ALU.mult))
            settle()
            magic = 1.5 * 2.0 ** 23
            mark(nc.vector.tensor_scalar(atmp, ang, 1.0 / (2.0 * math.pi), magic, ALU.mult, ALU.add))
            settle()
            mark(nc.vector.tensor_scalar(atmp, atmp, magic, None, ALU.subtract))
            for part in (6.28125, 1.9350051879882812e-3, 3.0199159819566e-7):
                settle()
                mark(nc.vector.scalar_tensor_tensor(ang, atmp, -part, ang, ALU.mult, ALU.add))
            settle()
            mark(nc.vector.tensor_scalar(ang, ang, 3.1415925, -3.1415925, ALU.min, ALU.max))
            settle()
            mark(nc.vector.scalar_tensor_tensor(atmp, ang, -1.0, ang, ALU.mult, ALU.max))
            settle()
            nc.vector.tensor_scalar(atmp, atmp, -1.0, math.pi / 2, ALU.mult, ALU.add).then_inc(angles_ready, 1)
            lam_prod = mid[:, 6912:7040].rearrange("p (a d) -> p a d", a=2)
            mark(nc.vector.tensor_tensor(lam_prod, lam_vec[:, 0:4:2, :], lam_vec[:, 1:4:2, :], ALU.mult))
            settle()
            nc.vector.tensor_reduce(lam2, lam_prod, axis=AX.X, op=ALU.add).then_inc(lam_dots, 1)
            for t, at in ((0, 0), (1, 768)):
                band = masks[:, at:at + S]
                mark(nc.vector.tensor_scalar(band, iota[:, :], pidx, float(t * P), ALU.subtract, ALU.subtract))
                settle()
                mark(nc.vector.scalar_tensor_tensor(band, band, -1.0, band, ALU.mult, ALU.max))
                settle()
                mark(nc.vector.tensor_scalar(band, band, float(A_REACH), NEG, ALU.is_gt, ALU.mult))
            for g in (1, 2):
                mark(nc.vector.tensor_scalar(mtmp_i, key_i, pidx_i, A_DIL[g] - 1, ALU.bitwise_xor, ALU.bitwise_and))
                settle()
                mark(nc.vector.tensor_scalar(masks[:, g * S:(g + 1) * S], mtmp_i, 0.0, NEG, ALU.not_equal, ALU.mult))
                settle()
            in_block(9)
            dve.wait_ge(sincos_ready, 2)
            hf32 = HD // 2
            for t in range(TT):
                for k in range(4):
                    g_lo, g_hi = qk_gain[:, k, 0:hf32], qk_gain[:, k, hf32:HD]
                    mark(nc.vector.tensor_tensor(rope_c[:, t, k, 0:hf32], cos[:, t, :], g_lo, ALU.mult))
                    mark(nc.vector.tensor_tensor(rope_c[:, t, k, hf32:HD], cos[:, t, :], g_hi, ALU.mult))
                    mark(nc.vector.scalar_tensor_tensor(rope_s[:, t, k, 0:hf32], sin[:, t, :], -1.0, g_hi,
                                                        ALU.mult, ALU.mult))
                    mark(nc.vector.tensor_tensor(rope_s[:, t, k, hf32:HD], sin[:, t, :], g_lo, ALU.mult))
            dve.wait_ge(lam_exp, 1)
            mark(nc.vector.tensor_scalar(lam, lam2[:, 0:1], lam2[:, 1:2], LAM_INIT, ALU.subtract, ALU.add))
            settle()
            mark(nc.vector.tensor_scalar(lam, lam, -1.0, None, ALU.mult))
            mark(nc.vector.tensor_scalar(subln, subln, 1.0 - LAM_INIT, None, ALU.mult))
            settle()
            kinds = ((0, 12), (12, 24), (24, 40), (40, 56))
            for t in range(TT):
                stat = qk_stat[:, t * QK_HEADS:(t + 1) * QK_HEADS]
                rows = proj[:, t, 0:QK_W].rearrange("p (h d) -> p h d", d=HD)
                rots = rot.rearrange("p (h d) -> p h d", d=HD)
                dve.wait_ge(qk_sq, t + 1)
                nc.vector.tensor_reduce(stat, rots, axis=AX.X, op=ALU.add).then_inc(qk_summed, 1)
                root_mean(stat, HD, (qk_summed, t + 1), qk_ms, qk_std, t + 1)
                mark(nc.vector.tensor_tensor(rows, rows, stat.unsqueeze(2).broadcast_to([P, QK_HEADS, HD]), ALU.mult))
                in_block(10 + 2 * t)
                settle()
                for k, (a, b) in enumerate(kinds):
                    for out_h, in_h in ((0, hf32), (hf32, 0)):
                        table = rope_s[:, t, k, out_h:out_h + hf32].unsqueeze(1).broadcast_to([P, b - a, hf32])
                        mark(nc.vector.tensor_tensor(rots[:, a:b, out_h:out_h + hf32], rows[:, a:b, in_h:in_h + hf32],
                                                     table, ALU.mult))
                settle()
                for k, (a, b) in enumerate(kinds):
                    table = rope_c[:, t, k, :].unsqueeze(1).broadcast_to([P, b - a, HD])
                    mark(nc.vector.tensor_tensor(rows[:, a:b, :], rows[:, a:b, :], table, ALU.mult))
                in_block(11 + 2 * t)
                settle()
                nc.vector.tensor_tensor(rows, rows, rots, ALU.add).then_inc(rope_done, 1)
            in_block(14)
            dve.wait_ge(ada_free, 4 * ADA_GROUPS)
            dve.wait_ge(acc_free, N_PA)
            for t in range(TT):
                last = nc.vector.tensor_tensor(proj[:, t, GL0:GL0 + GL_W], proj[:, t, GL0:GL0 + GL_W], b_gate, ALU.add)
            last.then_inc(gate_biased, 1)

            for g in range(1, NQK // 4 * TT, 2):
                dve.wait_ge(qkT_done, g + 1)
                t, b4 = g % TT, g // TT
                nc.vector.tensor_copy(qkT[:, 4 * b4:4 * b4 + 4, t * P:(t + 1) * P],
                                      ps[:, 5, :].rearrange("p (b t) -> p b t", b=4)).then_inc(qkT_odd, 1)

            def a_mask(i):
                t, b = i // A_SLOTS, i % 2
                sc = ps[:, 2 * b:2 * b + 2, :].rearrange("p a n -> p (a n)")[:, 0:768]
                dve.wait_ge(a_scored, i + 1)
                mark(nc.vector.scalar_tensor_tensor(a_s[b], sc, HD ** -0.5, masks[:, t * S:t * S + 768],
                                                    ALU.mult, ALU.add))
                settle()
                mark(nc.vector.tensor_reduce(a_max[:, b:b + 1], a_s[b], axis=AX.X, op=ALU.max))
                settle()
                nc.vector.tensor_scalar(a_nmax[:, b:b + 1], a_max[:, b:b + 1], -1.0, None,
                                        ALU.mult).then_inc(a_masked, 1)

            def a_weights(i):
                b = i % 2
                dve.wait_ge(a_tr, i + 1)
                if i >= 2:
                    dve.wait_ge(a_out, i - 1)
                mark(nc.vector.reciprocal(a_rec[:, b:b + 1], a_sum[:, b:b + 1]))
                nc.vector.tensor_copy(a_pT[b], ps[:, 4:6, :].rearrange("p a n -> p (a n)")[:, 0:768]
                                      ).then_inc(a_trT, 1)

            def a_rows(i):
                t, h, b = i // A_SLOTS, i % A_SLOTS, i % 2
                dve.wait_ge(a_pv, i + 1)
                settle()
                nc.vector.tensor_scalar(oa[:, t, h * HD:(h + 1) * HD], ps[:, 6 + b, 0:HD], a_rec[:, b:b + 1], None,
                                        ALU.mult).then_inc(a_out, 1)

            n_a = A_SLOTS * TT
            a_mask(0)
            a_mask(1)
            for i in range(n_a):
                a_weights(i)
                if i + 2 < n_a:
                    a_mask(i + 2)
                if i:
                    a_rows(i - 1)
            a_rows(n_a - 1)

            def b_maxima(h):
                b = h % 2
                dve.wait_ge(b_scored, h + 1)
                mark(nc.vector.tensor_reduce(b_max[:, 4 * b:4 * b + 4],
                                             ps[:, 2 * b:2 * b + 2, :].rearrange("p m (t n) -> p (m t) n", t=TT),
                                             axis=AX.X, op=ALU.max))
                settle()
                nc.vector.tensor_scalar(b_max[:, 4 * b:4 * b + 4], b_max[:, 4 * b:4 * b + 4], -(HD ** -0.5), None,
                                        ALU.mult).then_inc(b_bias, 1)

            def b_weights(h):
                b = h % 2
                r = b_rec[:, 4 * b:4 * b + 4]
                dve.wait_ge(b_prob, 4 * (h + 1))
                mark(nc.vector.reciprocal(r, b_sum[:, 4 * b:4 * b + 4]))
                settle()
                mark(nc.vector.tensor_scalar(r[:, 2:4], r[:, 2:4], lam, None, ALU.mult))
                settle()
                for t in range(TT):
                    mark(nc.vector.tensor_scalar(b_p2[b][:, t * S:(t + 1) * S], b_p2[b][:, t * S:(t + 1) * S],
                                                 r[:, 2 + t:3 + t], None, ALU.mult))
                settle()
                for t in range(TT):
                    nc.vector.scalar_tensor_tensor(b_p[b][:, t * S:(t + 1) * S], b_p[b][:, t * S:(t + 1) * S],
                                                   r[:, t:t + 1], b_p2[b][:, t * S:(t + 1) * S],
                                                   ALU.mult, ALU.add).then_inc(b_mix, 1)

            def b_rows(h):
                dve.wait_ge(b_pv, h + 1)
                nc.vector.tensor_copy(H[:, :, h * P:(h + 1) * P],
                                      ps[:, 6 + h % 2, 0:TT * P].rearrange("p (t n) -> p t n", t=TT)).then_inc(b_out, 1)

            b_maxima(0)
            for h in range(B_HEADS):
                if h + 1 < B_HEADS:
                    b_maxima(h + 1)
                b_weights(h)
                if h:
                    b_rows(h - 1)
            b_rows(B_HEADS - 1)
            dve.wait_ge(ob_sqd, 1)
            mark(nc.vector.tensor_reduce(ob_stat, ob_sq.rearrange("p (h d) -> p h d", d=P), axis=AX.X, op=ALU.add))
            root_mean(ob_stat, P, (dve_chain, chain[0]), ob_ms, ob_std, 1)
            obv = H[:, :, :].rearrange("p t (h d) -> p (t h) d", d=P)
            mark(nc.vector.tensor_tensor(obv, obv, ob_stat.unsqueeze(2).broadcast_to([P, TT * B_HEADS, P]), ALU.mult))
            settle()
            nc.vector.tensor_tensor(obv, obv, subln.unsqueeze(1).broadcast_to([P, TT * B_HEADS, P]),
                                    ALU.mult).then_inc(rows_ready, 1)

            def group(n, u, t, h, mul, out, first, last_sem):
                used(u)
                cols = slice(h * 512, (h + 1) * 512)
                if first:
                    ins = nc.vector.tensor_tensor(out[:, t, cols], ps[:, n % 4, :], mul, ALU.mult)
                    ins.then_inc(acc_free, 1)
                    return
                settle()
                nc.vector.tensor_tensor(lin_tmp, ps[:, n % 4, :], mul, ALU.mult).then_inc(acc_free, 1)
                dve.wait_ge(acc_free, n + 1)
                ins = nc.vector.tensor_tensor(out[:, t, cols], out[:, t, cols], lin_tmp, ALU.add)
                if last_sem is None:
                    mark(ins)
                else:
                    ins.then_inc(last_sem, 1)

            tr_low(T_OA)
            lo(U_PA + 2)
            dve.wait_ge(gate_ready, TT)
            for n in range(4):
                t, h = n // 2, n % 2
                group(N_PA + n, U_PA, t, h, proj[:, t, GL0 + h * 512:GL0 + (h + 1) * 512], mixed, True, None)
            tr_low(T_OB)
            for b in range(2):
                lo(U_PB + 2 * b + 2)
                lo(U_PB + 2 * b + 3)
                for t in range(TT):
                    group(N_PB + 2 * b + t, U_PB + 2 * b + 1, t, b, proj[:, t, GL0 + D + b * 512:GL0 + D + (b + 1) * 512],
                          mixed, False, None)
            settle()
            mark(nc.vector.tensor_copy(H[:, 0, :], mixed[:, 0, :]))
            nc.vector.tensor_copy(H[:, 1, :], mixed[:, 1, :]).then_inc(rows_ready, 1)
            tr_low(T_MIXED)
            for b in range(2):
                lo(U_WO + 2 * b + 2)
                lo(U_WO + 2 * b + 3)
                for t in range(TT):
                    end = b == 1 and t == 1
                    group(N_WO + 2 * b + t, U_WO + 2 * b + 1, t, b, g1[:, b * 512:(b + 1) * 512], X, False, x_ready if end else None)

            settle()
            dve.wait_ge(x_ready, 1)
            norm(1, X, rows_ready, sc2, sh2)
            tr_low(T_H2)
            low = -3.0e38

            def keep_16(rows, vals, idx, n):
                for half in range(2):
                    k8 = slice(8 * half, 8 * half + 8)
                    for b in range(n):
                        mark(nc.vector.max(vals(b)[:, k8], rows(b)))
                    settle()
                    for b in range(n):
                        mark(nc.vector.max_index(idx(b)[:, k8], vals(b)[:, k8], rows(b)))
                    if half == 0:
                        for b in range(n):
                            mark(nc.vector.match_replace(rows(b), vals(b)[:, k8], rows(b), low))
                        settle()

            def head_keys(h):
                dve.wait_ge(acc_free, n_scores(h) + 1)
                keep_16(lambda b: score[b // 2][:, (2 * h + b % 2) * N_KEYS:(2 * h + b % 2 + 1) * N_KEYS],
                        lambda b: top_v[b // 2][:, 2 * h + b % 2, :], lambda b: top_i[b // 2][:, 2 * h + b % 2, :],
                        2 * TT)

            for h in range(PH):
                lo(U_WQ + h + 2)
                if h >= 2:
                    head_keys(h - 2)
            head_keys(PH - 2)
            head_keys(PH - 1)
            for t in range(TT):
                cd = cand.rearrange("p (h n) -> p h n", h=PH)
                v4 = top_v[t].rearrange("p (h s) k -> p h s k", s=2)
                settle()
                mark(nc.vector.tensor_tensor(
                    cand.rearrange("p (h a b) -> p h a b", h=PH, a=TOPK),
                    v4[:, :, 0, :].unsqueeze(3).broadcast_to([P, PH, TOPK, TOPK]),
                    v4[:, :, 1, :].unsqueeze(2).broadcast_to([P, PH, TOPK, TOPK]), ALU.add))
                settle()
                keep_16(lambda b: cd[:, b, :], lambda b: best_v[:, b, :], lambda b: best_i[:, b, :], PH)
                settle()
                mark(nc.vector.tensor_copy(top_f.rearrange("p h s k -> p (h s) k"), top_i[t]))
                best_flat = best_i.rearrange("p h k -> p (h k)")
                for s, (op, arg) in enumerate(((ALU.logical_shift_right, 4), (ALU.bitwise_and, 15))):
                    mark(nc.vector.tensor_scalar(half_i, best_flat, arg, None, op))
                    settle()
                    mark(nc.vector.tensor_copy(half_f[s], half_i))
                    settle()
                    pick = score[t].rearrange("p (k j) -> p k j", j=TOPK)
                    mark(nc.vector.tensor_tensor(pick, half_f[s].unsqueeze(2).broadcast_to([P, PH * TOPK, TOPK]),
                                                 iota[:, 0:TOPK].unsqueeze(1).broadcast_to([P, PH * TOPK, TOPK]),
                                                 ALU.is_equal))
                    settle()
                    pick4 = score[t].rearrange("p (h k j) -> p h k j", h=PH, k=TOPK)
                    mark(nc.vector.tensor_tensor(pick4, pick4,
                                                 top_f[:, :, s, :].unsqueeze(2).broadcast_to([P, PH, TOPK, TOPK]),
                                                 ALU.mult))
                    settle()
                    mark(nc.vector.tensor_reduce(route[:, t, s, :], pick, axis=AX.X, op=ALU.add))
                if t:
                    settle()
                nc.vector.tensor_tensor(gate_e, best_v, best_v[:, :, 0:1].broadcast_to([P, PH, TOPK]),
                                        ALU.subtract).then_inc(gate_shift, 1)
                dve.wait_ge(gate_exp, t + 1)
                mark(nc.vector.tensor_reduce(gate_s, gate_e, axis=AX.X, op=ALU.add))
                settle()
                mark(nc.vector.reciprocal(gate_r, gate_s))
                settle()
                nc.vector.tensor_tensor(route[:, t, 2, :].rearrange("p (h k) -> p h k", h=PH), gate_e,
                                        gate_r.unsqueeze(2).broadcast_to([P, PH, TOPK]), ALU.mult).then_inc(routed, 1)
            dve.wait_ge(routed, TT)

            dve.wait_ge(route_in, 3)

            def one_hots(i, first):
                for k in range(2):
                    if not first:
                        dve.wait_ge(g_full, 2 * i + (k - 1))
                    nc.vector.tensor_tensor(one_a[k], iota[:, 0:P].unsqueeze(1).broadcast_to([P, GT, P]),
                                            routeT[:, 0, bass.ds(2 * GT * i + GT * k, GT)].unsqueeze(2)
                                            .broadcast_to([P, GT, P]), ALU.is_equal).then_inc(oa_ready, 1)
                    for q in range(GT):
                        tok = bass.ds(2 * GT * i + (GT * k + q), 1)
                        last = nc.vector.tensor_scalar(one_b[k][:, q, :], iota[:, 0:P], routeT[:, 1, tok],
                                                       routeT[:, 2, tok], ALU.is_equal, ALU.mult)
                    last.then_inc(ob_ready, 1)

            one_hots(0, True)
            with dve.Fori(1, S // (2 * GT)) as i:
                one_hots(i, False)

            u0 = U_PEER
            dve.wait_ge(g_free, 2 * S // GT)

            def gated(i, off=0, place=None):
                place = 2 * (i if place is None else place)
                dve.wait_ge(gelu_done, i + 1 + off)
                nc.vector.tensor_tensor(act_w[i % 2].rearrange("p (j t) -> p j t", j=2),
                                        act_s[i % 2].rearrange("p (j t) -> p j t", j=2),
                                        G[:, bass.ds(place + 2 * off, 2), :], ALU.mult).then_inc(w_done, 1)
                dve.wait_ge(w_hi, i + 1 + off)
                nc.vector.tensor_tensor(plo[:, i % 2, :], act_w[i % 2], phi[:, i % 2, :].bitcast(f32),
                                        ALU.subtract).then_inc(w_lo, 1)

            lo(u0 + 2)
            gated(0)
            lo(u0 + 3)
            gated(1)
            lo(u0 + 4)
            for first, count, place in ((2, NB - 2, 2), (NB, NB, 0)):
                if first == NB:
                    dve.wait_ge(g_loaded, 32 * NB)
                with dve.Fori(0, count // 2) as r:
                    for k in range(2):
                        i = first + k
                        lo(u0 + 2 * i + 1, 4 * r)
                        gated(i, 2 * r, place + k)
                        lo(u0 + 2 * i + 2, 4 * r)
            lo(u0 + 2 * NP + 1)
            used(U_MIX - 1)
            for n in range(4):
                t, h = n // 2, n % 2
                cols = slice(h * 512, (h + 1) * 512)
                tmp = mid[:, n * 512:(n + 1) * 512]
                mark(nc.vector.tensor_tensor(tmp, ps[:, n, :], g2[:, cols], ALU.mult))
                settle()
                last = nc.vector.tensor_tensor(X[:, t, cols], X[:, t, cols], tmp, ALU.add)
                if n < 3:
                    mark(last)
            settle()
            last.then_inc(x_ready, 1)

            dve.wait_ge(x_ready, 2)
            norm(2, X, rows_ready)
            tr_low(T_MIX)
            mark(nc.vector.tensor_copy(lint, iota[:, 0:P]))
            mark(nc.vector.tensor_scalar(lup, iota[:, 0:P], pidx, None, ALU.is_gt))
            mark(nc.vector.tensor_copy(lmask[:, 7, :], ident[:, :]))
            mark(nc.vector.memset(keep, 1.0))
            settle()
            mark(nc.vector.memset(keep[:, 0:S:SEG], 0.0))
            mark(nc.vector.tensor_scalar(lint, lint, pidx_i, None, ALU.bitwise_xor))
            settle()
            for l in range(LEVELS):
                mark(nc.vector.tensor_scalar(lsh, lint, l, None, ALU.logical_shift_right))
                settle()
                mark(nc.vector.scalar_tensor_tensor(lmask[:, l, :], lsh, 1.0, lup, ALU.is_equal, ALU.mult))
                settle()
            for u in range(MIX_T):
                lo(U_MIX + u + 2)
            dve.wait_ge(mix_loaded, 48)
            nc.vector.tensor_tensor(lb, lb2[:, RH:2 * RH], lb2[:, 0:RH], ALU.subtract).then_inc(lb_diff, 1)
            for u in range(4):
                lo(U_MIX + MIX_T + u + 2)
            settle()
            dve.wait_ge(acc_free, N_MT + MIX_T)
            mark(nc.vector.tensor_tensor(conv_u, cc, cx, ALU.mult))
            settle()
            for j in (2, 1, 0):
                for b in range(4):
                    w = conv_w[:, 3 * b + j:3 * b + j + 1]
                    if j == 2:
                        mark(nc.vector.tensor_scalar(conv_y[:, b, :], conv_u[:, b, :], w, None, ALU.mult))
                    else:
                        d = 2 - j
                        mark(nc.vector.scalar_tensor_tensor(conv_y[:, b, d:S], conv_u[:, b, 0:S - d], w,
                                                            conv_y[:, b, d:S], ALU.mult, ALU.add))
                settle()
            nc.vector.tensor_tensor(conv_y, conv_y, cb, ALU.mult).then_inc(conv_ready, 1)
            dve.wait_ge(lb_exp, 1)
            mark(nc.vector.tensor_scalar(lb, lb, 1.0, None, ALU.add))
            settle()
            mark(nc.vector.reciprocal(lb, lb))
            settle()
            mark(nc.vector.tensor_scalar(omlb, lb, -1.0, 1.0, ALU.mult, ALU.add))
            dve.wait_ge(z_exp, 2)
            mark(nc.vector.tensor_scalar(sig, sig, 1.0, None, ALU.add))
            mark(nc.vector.tensor_scalar(rk, rk, 1.0, None, ALU.add))
            settle()
            mark(nc.vector.reciprocal(sig, sig))
            mark(nc.vector.reciprocal(rk, rk))
            settle()
            for h in range(RH):
                mark(nc.vector.tensor_scalar(rk[:, h, :], rk[:, h, :], omlb[:, h:h + 1], None, ALU.mult))
                last = nc.vector.tensor_scalar(sig[:, h, :], sig[:, h, :], omlb[:, h:h + 1], lb[:, h:h + 1],
                                               ALU.mult, ALU.add)
                if h < RH - 1:
                    mark(last)
            settle()
            last.then_inc(f_ready, 1)
            dve.wait_ge(conv_hi, 1)
            nc.vector.tensor_tensor(tlo[:, 0:4, :], conv_y, thi[:, 0:4, :].bitcast(f32), ALU.subtract
                                    ).then_inc(conv_lo, 1)
            dve.wait_ge(f_log, 1)
            for h in range(RH):
                mark(nc.vector.tensor_tensor_scan(sig[:, h, :], keep, dec[:, h, :], 0.0, ALU.mult, ALU.add))
            settle()
            bsum = sig
            seg = bsum.rearrange("p h (n s) -> p (h n) s", s=SEG)

            def exponents(l):
                e = lev_e[l % 2]
                if l <= 6:
                    c = 1 << (l - 1)
                    v = bsum.rearrange("p h (n s) -> p (h n) s", s=2 * c)
                    o = e.rearrange("p h (n s) -> p (h n) s", s=2 * c)
                    mark(nc.vector.tensor_tensor(o, v, v[:, :, c - 1:c].broadcast_to([P, RH * S // (2 * c), 2 * c]),
                                                 ALU.subtract))
                else:
                    v = bsum.rearrange("p h (n s) -> p h n s", s=SEG)
                    o = e.rearrange("p h (n s) -> p h n s", s=SEG)
                    end = v[:, :, :, SEG - 1:SEG]
                    if l == 7:
                        left = slice(0, 4, 2)
                        right = slice(1, 4, 2)
                        mark(nc.vector.tensor_tensor(o[:, :, left, :], v[:, :, left, :],
                                                     end[:, :, left, :].broadcast_to([P, RH, 2, SEG]), ALU.subtract))
                        mark(nc.vector.tensor_copy(o[:, :, right, :], v[:, :, right, :]))
                    else:
                        left = slice(0, 2)
                        mark(nc.vector.tensor_tensor(o[:, :, left, :], v[:, :, left, :],
                                                     end[:, :, left, :].broadcast_to([P, RH, 2, SEG]), ALU.subtract))
                        mark(nc.vector.tensor_copy(o[:, :, 2, :], v[:, :, 2, :]))
                        mark(nc.vector.tensor_tensor(o[:, :, 3, :], v[:, :, 3, :],
                                                     end[:, :, 2, :].broadcast_to([P, RH, SEG]), ALU.add))
                        settle()
                        mark(nc.vector.tensor_tensor(o[:, :, 0, :], o[:, :, 0, :],
                                                     end[:, :, 1, :].broadcast_to([P, RH, SEG]), ALU.subtract))
                settle()
                nc.vector.scalar_tensor_tensor(e, e, -1.0, e, ALU.mult, ALU.max).then_inc(lev_d, 1)

            def decayed(l):
                dve.wait_ge(lev_exp, l)
                dve.wait_ge(lev_full, l)
                mark(nc.vector.tensor_tensor(lev_k, rk, lev_e[l % 2], ALU.mult))
                settle()
                nc.vector.tensor_tensor(lev_q, hq, lev_e[l % 2], ALU.mult).then_inc(lev_qk, 1)

            def collect(l):
                dve.wait_ge(lev_full, l + 1)
                if l == LEVELS + 1:
                    nc.vector.tensor_copy(rsc_x, ps[:, 2 * (l % 2), :].rearrange("p (h n) -> p h n", h=RH)
                                          ).then_inc(lev_free, 1)
                    return
                m = lmask[:, (l - 1) % 8, :].unsqueeze(1).broadcast_to([P, RH, P])
                dst = rsc if l == 0 else lev_t
                for t in range(TT):
                    last = nc.vector.tensor_tensor(dst[:, t, :, :],
                                                   ps[:, 2 * (l % 2) + t, :].rearrange("p (h n) -> p h n", h=RH),
                                                   m, ALU.mult)
                    if t == 0:
                        mark(last)
                last.then_inc(lev_free, 1)
                if l:
                    settle()
                    dve.wait_ge(lev_free, l + 1)
                    last = nc.vector.tensor_tensor(rsc, rsc, lev_t, ALU.add)
                    if l == LEVELS:
                        last.then_inc(sc_ready, 1)
                    else:
                        mark(last)
                        settle()

            for l in range(1, LEVELS + 2):
                exponents(l)
                decayed(l)
                collect(l - 1)
            collect(LEVELS + 1)
            dve.wait_ge(ro_sq, 1)
            rst = r_stat[:, 0:TT * RH]
            mark(nc.vector.tensor_reduce(rst, lev_q.rearrange("p b t -> p (b t)").rearrange("p (h d) -> p h d", d=P),
                                         axis=AX.X, op=ALU.add))
            mark(nc.vector.tensor_tensor(hg, hg, hnorm.unsqueeze(1).broadcast_to([P, TT, CW]), ALU.mult))
            root_mean(rst, P, (dve_chain, chain[0]), ro_ms, ro_std, 1)
            rov = ro.rearrange("p t (h d) -> p (t h) d", d=P)
            mark(nc.vector.tensor_tensor(rov, rov, rst.unsqueeze(2).broadcast_to([P, TT * RH, P]), ALU.mult))
            settle()
            nc.vector.tensor_tensor(H[:, :, 0:CW], ro, hg, ALU.mult).then_inc(rows_ready, 1)
            tr_low(T_YB, 4)

            def residual(n0, u0):
                for b in range(2):
                    lo(u0 + 2 * b + 2)
                    lo(u0 + 2 * b + 3)
                    for t in range(TT):
                        n = n0 + 2 * b + t
                        used(u0 + 2 * b + 1)
                        cols = slice(b * 512, (b + 1) * 512)
                        nc.vector.tensor_tensor(X[:, t, cols], X[:, t, cols], ps[:, n % 4, :],
                                                ALU.add).then_inc(acc_free, 1)

            residual(N_W2, U_WO2)

            norm(3, mem, rows_ready)
            tr_low(T_MEM)
            for u in range(8):
                lo(U_KV + u + 2)
            norm(4, X, rows_ready)
            tr_low(T_HX)
            for u in range(4):
                lo(U_XQ + u + 2)
            for i in range(XH * TT):
                b, h, t = i % 2, i // TT, i % TT
                dve.wait_ge(x_scored, i + 1)
                mark(nc.vector.tensor_reduce(x_max[:, b:b + 1], ps[:, b, 0:S], axis=AX.X, op=ALU.max))
                settle()
                nc.vector.tensor_scalar(x_max[:, b:b + 1], x_max[:, b:b + 1], -(XD ** -0.5), None,
                                        ALU.mult).then_inc(x_bias, 1)
                dve.wait_ge(x_prob, i + 1)
                mark(nc.vector.reciprocal(x_rec[:, b:b + 1], x_sum[:, b:b + 1]))
                settle()
                nc.vector.tensor_scalar(x_p[b], x_p[b], x_rec[:, b:b + 1], None, ALU.mult).then_inc(x_norm, 1)
                if t == TT - 1:
                    dve.wait_ge(xo_hi, h + 1)
                    nc.vector.tensor_tensor(tlo[:, 2 * h:2 * h + 2, :],
                                            ps[:, 6 + h % 2, :].rearrange("p (c t) -> p c t", c=2),
                                            thi[:, 2 * h:2 * h + 2, :].bitcast(f32), ALU.subtract).then_inc(xo_lo, 1)
            residual(N_XO, U_XO)

            dve.wait_ge(wr_hi, 1)
            nc.vector.tensor_tensor(wrlo[:, :, :], wr, wrhi[:, :, :].bitcast(f32), ALU.subtract).then_inc(wr_lo, 1)
            norm(5, X, rows_ready)
            tr_low(T_HF)
            dve.wait_ge(r_full, 1)
            for t in range(TT):
                mark(nc.vector.tensor_tensor(r_log[:, t, :], ps[:, t, 0:20], r_bias, ALU.add))
            settle()
            NG5 = N_GRP + 1
            lv = r_log.rearrange("p t (g a) -> p (t g) a", a=4)
            pv5 = r_prob.rearrange("p t (g a) -> p (t g) a", a=4)
            st = big[:, 9216:9216 + TT * NG5]
            mark(nc.vector.tensor_reduce(st, lv, axis=AX.X, op=ALU.max))
            settle()
            nc.vector.tensor_tensor(lv, lv, st.unsqueeze(2).broadcast_to([P, TT * NG5, 4]),
                                    ALU.subtract).then_inc(r_ready, 1)
            for a in range(4):
                mark(nc.vector.tensor_scalar(r_low[:, a, :], iota[:, 0:4], float(a), None, ALU.is_lt))
            dve.wait_ge(r_exp, 1)
            mark(nc.vector.tensor_reduce(st, pv5, axis=AX.X, op=ALU.add))
            settle()
            mark(nc.vector.reciprocal(st, st))
            settle()
            mark(nc.vector.tensor_tensor(pv5, pv5, st.unsqueeze(2).broadcast_to([P, TT * NG5, 4]), ALU.mult))
            settle()
            cmp3 = r_cmp.rearrange("p t g a b -> p (t g) a b")
            tie3 = r_tie.rearrange("p t g a b -> p (t g) a b")
            own = pv5.unsqueeze(3).broadcast_to([P, TT * NG5, 4, 4])
            other = pv5.unsqueeze(2).broadcast_to([P, TT * NG5, 4, 4])
            mark(nc.vector.tensor_tensor(cmp3, other, own, ALU.is_gt))
            mark(nc.vector.tensor_tensor(tie3, other, own, ALU.is_equal))
            settle()
            mark(nc.vector.tensor_tensor(tie3, tie3, r_low.unsqueeze(1).broadcast_to([P, TT * NG5, 4, 4]), ALU.mult))
            settle()
            mark(nc.vector.tensor_tensor(cmp3, cmp3, tie3, ALU.add))
            settle()
            rank = r_rank.rearrange("p t (g a) -> p (t g) a", a=4)
            mark(nc.vector.tensor_reduce(rank, cmp3, axis=AX.X, op=ALU.add))
            settle()
            mark(nc.vector.scalar_tensor_tensor(r_sel[:, :, 0:4], r_rank[:, :, 0:4], 0.5, r_prob[:, :, 0:4],
                                                ALU.is_lt, ALU.mult))
            mark(nc.vector.scalar_tensor_tensor(r_sel[:, :, 4:20], r_rank[:, :, 4:20], 1.5, r_prob[:, :, 4:20],
                                                ALU.is_lt, ALU.mult))
            settle()
            for t in range(TT):
                es = r_sel[:, t, 4:20].rearrange("p (g a) -> p g a", a=4)
                esum = big[:, 9248 + 4 * t:9252 + 4 * t]
                mark(nc.vector.tensor_reduce(esum, es, axis=AX.X, op=ALU.add))
                settle()
                mark(nc.vector.reciprocal(esum, esum))
                settle()
                mark(nc.vector.tensor_tensor(esum, esum, r_sel[:, t, 0:4], ALU.mult))
                settle()
                mark(nc.vector.tensor_tensor(comb[:, t, :].rearrange("p (g a) -> p g a", a=4), es,
                                             esum.unsqueeze(2).broadcast_to([P, N_GRP, 4]), ALU.mult))
            settle()

            def expert(u, off, uoff, last, e):
                for j in range(2):
                    lo(u + 2 * j + 2, uoff)
                    dve.wait_ge(m_silu, j + 1 + 2 * off)
                    used(u + 2 * j + 1, uoff)
                    nc.vector.tensor_tensor(hid[j], silu_g[j], ps[:, 5 + 2 * j, :], ALU.mult).then_inc(m_hid, 1)
                    lo(u + 2 * j + 3, uoff)
                    dve.wait_ge(m_hi, j + 1 + 2 * off)
                    nc.vector.tensor_tensor(plo[:, j, :], hid[j], phi[:, j, :].bitcast(f32),
                                            ALU.subtract).then_inc(m_lo, 1)
                if not last:
                    lo(u + 6, uoff)
                used(u + 5, uoff)
                for h in range(2):
                    if h and not last:
                        lo(u + 7, uoff)
                    for t in range(TT):
                        cols = slice(h * 512, (h + 1) * 512)
                        nc.vector.scalar_tensor_tensor(X[:, t, cols], ps[:, 2 * h + t, :], comb[:, t, e], X[:, t, cols],
                                                       ALU.mult, ALU.add).then_inc(d_free, 1)

            with dve.Fori(0, N_EXP - 1) as e:
                expert(U_MOE, e, 6 * e, False, bass.ds(e, 1))
                dve.wait_ge(d_free, 4 * e + 4)
            expert(U_MOE + 6 * (N_EXP - 1), N_EXP - 1, 0, True, slice(N_EXP - 1, N_EXP))
            dve.wait_ge(d_free, 4 * N_EXP)
            norm(6, X, out_ready)

        @block.tensor
        def _(pe):
            def mm3(out, ahi, alo, bhi, blo, start, stop):
                nc.tensor.matmul(out, ahi, bhi, start=start, stop=False)
                nc.tensor.matmul(out, ahi, blo, start=False, stop=False)
                return nc.tensor.matmul(out, alo, bhi, start=False, stop=stop)

            def arrived(u, off=0):
                pe.wait_ge(unit_split, u + 1 + off)

            def free_bank(n, off=0):
                if n >= 4:
                    pe.wait_ge(acc_free, n - 3 + off)

            def transposes(t, src, chunks):
                if t == T_OA:
                    pe.wait_ge(a_out, A_SLOTS * TT)
                else:
                    pe.wait_ge(rows_ready, ROWS[t])
                for k in range(T_GROUPS[t]):
                    g = T_BASE[t] + k
                    if g >= 2:
                        pe.wait_ge(tr_lo, g - 1)
                    for c in range(2):
                        for tt in range(TT):
                            last = nc.tensor.transpose(ps[:, 4 + g % 2, (2 * c + tt) * P:(2 * c + tt + 1) * P],
                                                       src[:, tt, (2 * k + c) * P:(2 * k + c + 1) * P], ident[:, :])
                    last.then_inc(tr_done, 1)

            def split_rows(t):
                pe.wait_ge(tr_lo, T_BASE[t + 1])

            def block_rows(n, u, off=0, uoff=0, at=None):
                for t in range(TT):
                    free_bank(n + t, off)
                for k in range(2):
                    arrived((u if at is None else at) + k, uoff)
                    s = (u + k) % 2
                    for t in range(TT):
                        for c in range(4):
                            rows = slice(t * P, (t + 1) * P)
                            cols = slice(c * 512, (c + 1) * 512)
                            last = mm3(ps[:, (n + t) % 4, :], thi[:, 4 * k + c, rows], tlo[:, 4 * k + c, rows],
                                       whi[:, s, cols], wlo[:, s, cols], k == 0 and c == 0, k == 1 and c == 3)
                    last.then_inc(unit_used, 1)

            def block_T(out, u, uoff=0):
                arrived(u, uoff)
                s = u % 2
                for fb in range(2):
                    for c in range(DC):
                        cols = slice(c * 256 + fb * P, c * 256 + (fb + 1) * P)
                        last = mm3(out[:, fb * S:(fb + 1) * S], whi[:, s, cols], wlo[:, s, cols],
                                   thi[:, c, :], tlo[:, c, :], c == 0, c == DC - 1)
                last.then_inc(unit_used, 1)

            def group_T(n, u):
                free_bank(n)
                block_T(ps[:, n % 4, :], u)

            def ada_sums(g, units):
                pe.wait_ge(unit_split, units)
                for m in range(4):
                    if g:
                        pe.wait_ge(ada_free, 4 * (g - 1) + m + 1)
                    last = nc.tensor.matmul(ps[:, 4 + m, :], ones, ada_acc[g][:, m * 512:(m + 1) * 512],
                                            start=True, stop=True)
                last.then_inc(ada_full, 1)

            pe.wait_ge(ones_ready, 1)
            ada_sums(0, DC)

            pe.wait_ge(consts_ready, 3)
            transposes(T_H1, H, DC)
            split_rows(T_H1)
            for b in range(2):
                block_rows(2 * b, U_IN + 2 * b, at=in_at(2 * b))
            with pe.Fori(0, IN_MIXED // 4 - 1) as i:
                for b in range(2, 4):
                    block_rows(2 * b, U_IN + 2 * b, 4 * i, 8 * i, in_at(2 * b))
            ada_sums(1, in_at(2 * DC - 1))
            block_rows(16, U_IN + 16)
            ada_sums(2, in_at(IN_MIXED))
            block_rows(18, U_IN + 18)
            with pe.Fori(0, (IN_BLOCKS - 10) // 2) as i:
                for b in range(10, 12):
                    block_rows(2 * b, U_IN + 2 * b, 4 * i, 4 * i)
            u = U_PA - 1
            arrived(u)
            for t in range(TT):
                n = N_PA - 2 + t
                free_bank(n)
                for c in range(DC):
                    rows = slice(t * P, (t + 1) * P)
                    cols = slice(c * 256, (c + 1) * 256)
                    last = mm3(ps[:, n % 4, 0:256], thi[:, c, rows], tlo[:, c, rows], whi[:, u % 2, cols],
                               wlo[:, u % 2, cols], c == 0, c == DC - 1)
            last.then_inc(unit_used, 1)

            pe.wait_ge(rope_done, TT)
            pe.wait_ge(gate_biased, 1)
            for g in range(NQK // 4 * TT):
                t, b4 = g % TT, g // TT
                if g >= 2:
                    pe.wait_ge(qkT_odd if g % 2 else qkT_even, g // 2)
                for b in range(4):
                    last = nc.tensor.transpose(ps[:, 4 + g % 2, b * P:(b + 1) * P],
                                               proj[:, t, (4 * b4 + b) * P:(4 * b4 + b + 1) * P], ident[:, :])
                last.then_inc(qkT_done, 1)
            pe.wait_ge(qkT_even, NQK // 4 * TT // 2)
            pe.wait_ge(qkT_odd, NQK // 4 * TT // 2)

            def a_groups(t):
                return (0, 1, 2) if t == 0 else (1, 2, 0)

            def a_scores(i):
                t, h, b = i // A_SLOTS, i % A_SLOTS, i % 2
                if i >= 2:
                    pe.wait_ge(a_masked, i - 1)
                sc = ps[:, 2 * b:2 * b + 2, :].rearrange("p a n -> p (a n)")
                for k, g in enumerate(a_groups(t)):
                    hd = g * A_SLOTS + h
                    part = slice(HD * (hd % 2), HD * (hd % 2) + HD)
                    last = nc.tensor.matmul(sc[:, k * S:(k + 1) * S], qkT[part, hd // 2, t * P:(t + 1) * P],
                                            qkT[part, 6 + hd // 2, :], start=True, stop=True)
                last.then_inc(a_scored, 1)

            def a_transposes(i):
                b = i % 2
                pe.wait_ge(a_prob, i + 1)
                if i:
                    pe.wait_ge(a_trT, i)
                trp = ps[:, 4:6, :].rearrange("p a n -> p (a n)")
                for k in range(6):
                    last = nc.tensor.transpose(trp[:, k * P:(k + 1) * P], a_s[b][:, k * P:(k + 1) * P], ident[:, :])
                last.then_inc(a_tr, 1)

            def a_values(i):
                t, h, b = i // A_SLOTS, i % A_SLOTS, i % 2
                if i >= 2:
                    pe.wait_ge(a_out, i - 1)
                pe.wait_ge(a_trT, i + 1)
                for k in range(6):
                    hd = a_groups(t)[k // 2] * A_SLOTS + h
                    last = nc.tensor.matmul(ps[:, 6 + b, 0:HD], a_pT[b][:, k * P:(k + 1) * P],
                                            proj[:, k % 2, V0 + hd * HD:V0 + (hd + 1) * HD], start=k == 0, stop=k == 5)
                last.then_inc(a_pv, 1)

            n_a = A_SLOTS * TT
            a_scores(0)
            a_scores(1)
            for i in range(n_a):
                a_transposes(i)
                if i + 2 < n_a:
                    a_scores(i + 2)
                if i:
                    a_values(i - 1)
            a_values(n_a - 1)

            def b_scores(h):
                if h >= 2:
                    pe.wait_ge(b_prob, 4 * (h - 1))
                elif h == 0:
                    pe.wait_ge(a_masked, n_a)
                for m in range(2):
                    part = slice(HD * m, HD * m + HD)
                    for t in range(TT):
                        last = nc.tensor.matmul(ps[:, 2 * (h % 2) + m, t * S:(t + 1) * S],
                                                qkT[part, 12 + h, t * P:(t + 1) * P],
                                                qkT[part, 20 + h, :], start=True, stop=True)
                last.then_inc(b_scored, 1)

            def b_transposes(h):
                pe.wait_ge(b_mix, TT * (h + 1))
                if h >= 2:
                    pe.wait_ge(b_trT, h - 1)
                elif h == 0:
                    pe.wait_ge(a_trT, n_a)
                for t in range(TT):
                    for k in range(2):
                        last = nc.tensor.transpose(ps[:, 4 + h % 2, (2 * t + k) * P:(2 * t + k + 1) * P],
                                                   b_p[h % 2][:, t * S + k * P:t * S + (k + 1) * P], ident[:, :])
                last.then_inc(b_tr, 1)

            def b_values(h):
                if h >= 2:
                    pe.wait_ge(b_out, h - 1)
                elif h == 0:
                    pe.wait_ge(a_out, n_a)
                pe.wait_ge(b_trT, h + 1)
                for t in range(TT):
                    for k in range(2):
                        last = nc.tensor.matmul(ps[:, 6 + h % 2, t * P:(t + 1) * P],
                                                b_pT[h % 2][:, (2 * t + k) * P:(2 * t + k + 1) * P],
                                                proj[:, k, V0 + A_W + h * P:V0 + A_W + (h + 1) * P],
                                                start=k == 0, stop=k == 1)
                last.then_inc(b_pv, 1)

            b_scores(0)
            b_scores(1)
            for h in range(B_HEADS):
                b_transposes(h)
                if h + 2 < B_HEADS:
                    b_scores(h + 2)
                if h:
                    b_values(h - 1)
            b_values(B_HEADS - 1)

            transposes(T_OA, oa, 2)
            split_rows(T_OA)
            arrived(U_PA)
            for n in range(4):
                t, h = n // 2, n % 2
                free_bank(N_PA + n)
                for c in range(2):
                    cols = slice(c * D + h * 512, c * D + (h + 1) * 512)
                    rows = slice(t * P, (t + 1) * P)
                    last = mm3(ps[:, (N_PA + n) % 4, :], thi[:, c, rows], tlo[:, c, rows], whi[:, U_PA % 2, cols],
                               wlo[:, U_PA % 2, cols], c == 0, c == 1)
            last.then_inc(unit_used, 1)
            transposes(T_OB, H, DC)
            split_rows(T_OB)
            for b in range(2):
                block_rows(N_PB + 2 * b, U_PB + 2 * b)
            transposes(T_MIXED, H, DC)
            split_rows(T_MIXED)
            for b in range(2):
                block_rows(N_WO + 2 * b, U_WO + 2 * b)

            transposes(T_H2, H, DC)
            split_rows(T_H2)
            def head_scores(h):
                if h == 0:
                    pe.wait_ge(keys_loaded, 16)
                pe.wait_ge(acc_free, n_query(h) + 1)
                free_bank(n_scores(h))
                for t in range(TT):
                    for k in range(2):
                        last = nc.tensor.matmul(ps[:, n_scores(h) % 4, (2 * t + k) * P:(2 * t + k + 1) * P],
                                                qT[:, 2 * h + k, t * P:(t + 1) * P], keysT[:, 2 * h + k, :],
                                                start=True, stop=True)
                last.then_inc(keys_scored, 1)

            for h in range(PH):
                group_T(n_query(h), U_WQ + h)
                if h:
                    head_scores(h - 1)
            head_scores(PH - 1)
            pe.wait_ge(routed, TT)
            for q in range(3):
                if q == 2:
                    pe.wait_ge(route_in, 1)
                for t in range(TT):
                    last = nc.tensor.transpose(ps[:, 4 + q % 2, t * P:(t + 1) * P], route[:, t, q, :], ident[:, :])
                last.then_inc(route_tr, 1)

            pe.wait_ge(route_in, 3)

            def gates(i, first):
                for k in range(2):
                    pe.wait_ge(oa_ready, 2 * i + (k + 1))
                    pe.wait_ge(ob_ready, 2 * i + (k + 1))
                    if not first:
                        pe.wait_ge(g_free, 4 * i + 2 * (k - 1))
                    out = ps[:, 4 + 2 * k:6 + 2 * k, :].rearrange("p a n -> p (a n)")
                    for q in range(GT):
                        last = nc.tensor.matmul(out[:, q * N_KEYS:(q + 1) * N_KEYS], one_a[k][:, q, :],
                                                one_b[k][:, q, :], start=True, stop=True)
                    last.then_inc(g_full, 1)

            gates(0, True)
            with pe.Fori(1, S // (2 * GT)) as i:
                gates(i, False)

            u0 = U_PEER
            pe.wait_ge(g_free, 2 * S // GT)

            def scores_of(i, u, off=0, uoff=0):
                if i >= 2:
                    pe.wait_ge(gelu_done, i - 1 + off)
                block_T(ps[:, 4 + i % 2, :], u, uoff)

            def values_of(i, u, off=0, uoff=0):
                arrived(u, uoff)
                pe.wait_ge(w_lo, i + 1 + off)
                for j in range(2):
                    for t in range(TT):
                        for h in range(2):
                            rows = slice(j * S + t * P, j * S + (t + 1) * P)
                            cols = slice(j * D + h * 512, j * D + (h + 1) * 512)
                            last = mm3(ps[:, 2 * t + h, :], phi[:, i % 2, rows], plo[:, i % 2, rows],
                                       whi[:, u % 2, cols], wlo[:, u % 2, cols],
                                       u == u0 + 2 and j == 0, u == u0 + 2 * NP - 1 and j == 1)
                last.then_inc(unit_used, 1)

            scores_of(0, u0)
            scores_of(1, u0 + 1)
            values_of(0, u0 + 2)
            with pe.Fori(0, (NP - 2) // 2) as r:
                for k in (1, 2):
                    scores_of(k + 1, u0 + 2 * k + 1, 2 * r, 4 * r)
                    values_of(k, u0 + 2 * k + 2, 2 * r, 4 * r)
            values_of(NP - 1, u0 + 2 * NP - 1)

            transposes(T_MIX, H, DC)
            split_rows(T_MIX)
            for u in range(MIX_T):
                group_T(N_MT + u, U_MIX + u)
            for b in range(2):
                block_rows(N_MV + 2 * b, U_MIX + MIX_T + 2 * b)
            for l in range(LEVELS + 2):
                qs, ks = (hq, rk) if l == 0 else (lev_q, lev_k)
                if l == 0:
                    pe.wait_ge(acc_free, N_W2)
                    pe.wait_ge(f_ready, 1)
                else:
                    pe.wait_ge(lev_qk, l)
                    if l >= 2:
                        pe.wait_ge(lev_free, l - 1)
                for t in range(1 if l == LEVELS + 1 else TT):
                    for h in range(RH):
                        kt, qt = (0, 1) if l == LEVELS + 1 else (t, t)
                        last = nc.tensor.matmul(ps[:, 2 * (l % 2) + t, h * P:(h + 1) * P],
                                                ks[:, h, kt * P:(kt + 1) * P], qs[:, h, qt * P:(qt + 1) * P],
                                                start=True, stop=True)
                last.then_inc(lev_full, 1)
            pe.wait_ge(sc_ready, 1)
            pe.wait_ge(lev_free, LEVELS + 2)
            for t in range(TT):
                for h in range(RH):
                    cols = slice(h * P, (h + 1) * P)
                    if t:
                        nc.tensor.matmul(ps[:, t, cols], rsc_x[:, h, :], hv[:, 0, cols], start=True, stop=False)
                    last = nc.tensor.matmul(ps[:, t, cols], rsc[:, t, h, :], hv[:, t, cols], start=t == 0, stop=True)
                last.then_inc(ro_full, 1)
            pe.wait_ge(conv_lo, 1)
            transposes(T_YB, H, 4)
            split_rows(T_YB)
            for b in range(2):
                block_rows(N_W2 + 2 * b, U_WO2 + 2 * b)

            transposes(T_MEM, H, DC)
            split_rows(T_MEM)
            for u in range(4):
                group_T(N_K + u, U_KV + u)
            for b in range(2):
                block_rows(N_V + 2 * b, U_KV + 4 + 2 * b)
            transposes(T_HX, H, DC)
            split_rows(T_HX)
            for u in range(4):
                group_T(N_XQ + u, U_XQ + u)
            pe.wait_ge(acc_free, N_XO)

            def x_scores(i):
                h, t = i // TT, i % TT
                if i >= 2:
                    pe.wait_ge(x_prob, i - 1)
                for c in range(2):
                    last = nc.tensor.matmul(ps[:, i % 2, 0:S], xqT[:, 2 * h + c, t * P:(t + 1) * P], kT[:, 2 * h + c, :],
                                            start=c == 0, stop=c == 1)
                last.then_inc(x_scored, 1)

            x_scores(0)
            for i in range(XH * TT):
                h, t = i // TT, i % TT
                if i + 1 < XH * TT:
                    x_scores(i + 1)
                pe.wait_ge(x_norm, i + 1)
                if i >= 2:
                    pe.wait_ge(x_trT, i - 1)
                for k in range(TT):
                    last = nc.tensor.transpose(ps[:, 4 + i % 2, k * P:(k + 1) * P], x_p[i % 2][:, k * P:(k + 1) * P],
                                               ident[:, :])
                last.then_inc(x_tr, 1)
                if t == TT - 1:
                    pe.wait_ge(x_trT, i + 1)
                    if h >= 2:
                        pe.wait_ge(xo_lo, h - 1)
                    for c in range(2):
                        for k in range(TT):
                            cols = slice(h * XD + c * P, h * XD + (c + 1) * P)
                            last = nc.tensor.matmul(ps[:, 6 + h % 2, c * S:(c + 1) * S], vm[:, k, cols],
                                                    x_pT[h % 2][:, k, :], start=k == 0, stop=k == TT - 1)
                    last.then_inc(xo_full, 1)
            pe.wait_ge(xo_lo, XH)
            for b in range(2):
                block_rows(N_XO + 2 * b, U_XO + 2 * b)

            transposes(T_HF, H, DC)
            split_rows(T_HF)
            pe.wait_ge(wr_lo, 1)
            pe.wait_ge(acc_free, N_XO + 4)
            for t in range(TT):
                for c in range(DC):
                    rows = slice(t * P, (t + 1) * P)
                    last = mm3(ps[:, t, 0:20], thi[:, c, rows], tlo[:, c, rows], wrhi[:, c, :], wrlo[:, c, :],
                               c == 0, c == DC - 1)
            last.then_inc(r_full, 1)

            def expert(u, off, uoff, first):
                for j in range(2):
                    for k in range(2):
                        block_T(ps[:, 4 + 2 * j + k, :], u + 2 * j + k, uoff)
                if not first:
                    pe.wait_ge(d_free, 4 * off)
                for j in range(2):
                    s = (u + 4 + j) % 2
                    arrived(u + 4 + j, uoff)
                    pe.wait_ge(m_lo, j + 1 + 2 * off)
                    for c in range(2):
                        for t in range(TT):
                            for h in range(2):
                                rows = slice(c * S + t * P, c * S + (t + 1) * P)
                                cols = slice(c * D + h * 512, c * D + (h + 1) * 512)
                                last = mm3(ps[:, 2 * h + t, :], phi[:, j, rows], plo[:, j, rows], whi[:, s, cols],
                                           wlo[:, s, cols], j == 0 and c == 0, j == 1 and c == 1)
                    last.then_inc(unit_used, 1)

            pe.wait_ge(r_ready, 1)
            expert(U_MOE, 0, 0, True)
            with pe.Fori(1, N_EXP) as e:
                expert(U_MOE, e, 6 * e, False)


def _stream(i):
    import numpy as np

    def rows(w):
        k, n = w.shape
        return w.reshape(2, 4, P, n // 512, 512).transpose(3, 0, 2, 1, 4).reshape(-1, P, UW)

    def cols(w):
        return w.reshape(DC, P, w.shape[1] // 256, 256).transpose(2, 1, 0, 3).reshape(-1, P, UW)

    ada = i["w_ada"][0].reshape(DC, P, ADA_GROUPS, UW).transpose(2, 0, 1, 3).reshape(-1, P, UW)
    w = i["w_in"][0]
    qa_ka, va = w[:, 0:2 * A_W], w[:, 2 * A_W:3 * A_W]
    b0 = 3 * A_W
    qb_kb, vb, gl = w[:, b0:b0 + 2 * D], w[:, b0 + 2 * D:b0 + 3 * D], w[:, b0 + 3 * D:]
    w = np.concatenate([qa_ka, qb_kb, gl, va, vb], axis=1)
    full = 512 * IN_BLOCKS
    pa = i["w_proj_a"][0].reshape(2, P, D).transpose(1, 0, 2).reshape(1, P, UW)
    eu = i["expert_u"][0].reshape(P, NP, 2, DC, P).transpose(1, 4, 3, 2, 0).reshape(NP, P, UW)
    ev = i["expert_v"][0].reshape(P, NP, 2, D).transpose(1, 0, 2, 3).reshape(NP, P, UW)
    peer = [eu[:1], np.stack([eu[1:], ev[:-1]], axis=1).reshape(-1, P, UW), ev[-1:]]
    w2 = i["w_in_2"][0]
    wkv = i["w_kv_2"][0]
    moe = []
    for e in range(N_EXP):
        g, u = cols(i["w_gate_2"][0, e]), cols(i["w_up_2"][0, e])
        d = i["w_down_2"][0, e].reshape(2, 2, P, D).transpose(0, 2, 1, 3).reshape(2, P, UW)
        moe += [g[:1], u[:1], g[1:], u[1:], d]
    w_in = np.concatenate([rows(w[:, :full]), cols(w[:, full:])], axis=0)
    shared = np.stack([w_in[:IN_MIXED].reshape(-1, 2, P, UW), ada[DC:].reshape(-1, 2, P, UW)], axis=1).reshape(-1, P, UW)
    return np.concatenate([
        ada[:DC], shared, w_in[IN_MIXED:], pa, rows(i["w_proj_b"][0]), rows(i["w_out"][0]),
        cols(i["w_query"][0]), *peer, cols(w2[:, :5 * CW]), rows(w2[:, 5 * CW:]), rows(i["w_out_2"][0]),
        cols(wkv[:, :D]), rows(wkv[:, D:]), cols(i["w_q_2"][0]), rows(i["w_o_2"][0]), *moe], axis=0)


def kernel(**inputs):
    import numpy as np
    import concourse.bacc as _bacc
    from concourse import mybir as _mybir
    from concourse.bass_utils import run_bass_kernel_spmd as _run

    i = {k: np.asarray(v) for k, v in inputs.items()}
    arrays = {
        "stream": _stream(i),
        "x": i["x"][0], "c": i["c"][0].reshape(DC, P).T,
        "positions": i["positions"][0].reshape(TT, P).T, "b_ada": i["b_ada"][0],
        "gains": np.concatenate([i["norm1_g"], i["norm2_g"], i["mix_norm_2"], i["mem_norm_2"], i["xattn_norm_2"],
                                 i["ffn_norm_2"], i["final_norm_2"][None]], axis=0),
        "lam": np.concatenate([i["lam_q1"], i["lam_k1"], i["lam_q2"], i["lam_k2"]], axis=0),
        "qk_gain": np.concatenate([i["qn_a"], i["kn_a"], i["qn_b"], i["kn_b"]], axis=0),
        "subln": i["subln_g"][0], "b_gate": i["b_gate"][0],
        "inv_freq": (1.0 / (10000.0 ** (np.arange(0, HD, 2, dtype=np.float32) / HD))).astype(np.float32),
        "keysT": i["sub_keys"][0].transpose(3, 0, 1, 2).reshape(P, NHH * N_KEYS),
        "conv_w": i["conv_w_2"][0].reshape(3, 4, P).transpose(2, 1, 0).reshape(P, 12),
        "hgrn_lb": i["hgrn_lb_2"].reshape(2, RH, P).transpose(2, 0, 1).reshape(P, 2 * RH),
        "hgrn_norm": i["hgrn_norm_2"][0], "mem": i["mem_2"][0],
        "router": np.concatenate([i["w_group_2"][0], i["w_expert_2"][0]], axis=1).reshape(DC, P, 20)
                    .transpose(1, 0, 2).reshape(P, DC * 20),
        "router_b": np.concatenate([i["b_group_2"][0], i["b_expert_2"][0]], axis=0),
    }
    nc = _bacc.Bacc("TRN2", target_bir_lowering=False, num_devices=1)
    io, feeds = {}, {}
    for name, a in arrays.items():
        feeds[f"in_{name}_dram"] = np.ascontiguousarray(a)
        io[name] = nc.dram_tensor(f"in_{name}_dram", a.shape, _mybir.dt.from_np(a.dtype), kind="ExternalInput").ap()
    io["out"] = nc.dram_tensor("out_dram", (S, D), _mybir.dt.float32, kind="ExternalOutput").ap()
    hybrid_block_then_mixer_memory_moe_kernel(nc, io)
    r = _run(nc, [feeds], core_ids=[0])
    return r.results[0]["out_dram"].reshape(1, S, D)
```

```python
import concourse.bass as bass
from concourse import mybir
from contextlib import ExitStack
import math

P = 128
S = 256
TT = S // P
D = 1024
DC = D // P
HD = 64
A_SLOTS, A_GROUPS = 4, 3
A_HEADS = A_SLOTS * A_GROUPS
A_DIL = (1, 4, 16)
A_REACH = 64
A_W = A_HEADS * HD
B_HEADS = 8
QK_W = 2 * A_W + 2 * D
GL_W = 2 * D
V_W = A_W + D
IN_W = QK_W + GL_W + V_W
NQK = QK_W // P
QK_HEADS = QK_W // HD
EPS = 1e-6
NEG = -1e30
LAM_INIT = 0.8 - 0.6 * math.exp(0.0)
N_KEYS, PH, TOPK = 128, 8, 16
NHH = 2 * PH
PAIR_BLOCKS = ((0, 1, 16), (1, 3, 8), (4, 4, 4), (8, 8, 1))
PAIRS = sum(n * w for _, n, w in PAIR_BLOCKS)
CW = 512
RH = 4
SEG = 64
LEVELS = 7
XH, XD = 4, 256
N_EXP, N_GRP, PER_GRP = 16, 4, 4
FE = 512
UW = 2048
NP = N_KEYS // 2
NB = NP // 2
NE = 8
GT = 8
GC = 32

ADA_GROUPS = 6 * D // UW
U_IN = ADA_GROUPS * DC
IN_BLOCKS = IN_W // 512
ADA_LATE = (ADA_GROUPS - 1) * DC


def in_at(k):
    return DC + k


U_PA = U_IN + 2 * IN_BLOCKS + 1
U_PB = U_PA + 1
U_WO = U_PB + 4
U_WQ = U_WO + 4
U_PEER = U_WQ + 8
U_MIX = U_PEER + 2 * NP
MIX_T = 5 * CW // 256
U_KV = U_MIX + MIX_T + 4
U_WO2 = U_KV + 8
U_XQ = U_WO2 + 4
U_XO = U_XQ + 4
U_MOE = U_XO + 4
NU = U_MOE + 6 * N_EXP

T_H1, T_OA, T_OB, T_MIXED, T_H2, T_MIX, T_MEM, T_YB, T_HX, T_HF = range(10)
ROWS = {t: TT * (n + 1) for n, t in enumerate(t for t in range(10) if t != T_OA)}
T_GROUPS = [4, 1, 4, 4, 4, 4, 4, 2, 4, 4]
T_BASE = [sum(T_GROUPS[:k]) for k in range(11)]


def hybrid_block_then_mixer_memory_moe_kernel(nc, io):
    f32, f32r = mybir.dt.float32, mybir.dt.float32r
    i32, u32 = mybir.dt.int32, mybir.dt.uint32
    ALU, ACT, AX = mybir.AluOpType, mybir.ActivationFunctionType, mybir.AxisListType

    ctx = ExitStack()
    with ctx:
        def sb(name, shape, dt=f32):
            return ctx.enter_context(nc.sbuf_tensor(name, shape, dt))

        def sem(name):
            return ctx.enter_context(nc.semaphore(name))

        raw = sb("raw", [P, 2, UW])
        whi = sb("whi", [P, 2, UW], f32r)
        wlo = sb("wlo", [P, 2, UW], f32r)
        X = sb("X", [P, TT, D])
        H = sb("H", [P, TT, D])
        thi = sb("thi", [P, DC, S], f32r)
        tlo = sb("tlo", [P, DC, S], f32r)
        MOD = sb("MOD", [P, 6 * D])
        BIG = sb("BIG", [P, 16384])
        MID = sb("MID", [P, 7168])
        phi = sb("phi", [P, 2, 512], f32r)
        plo = sb("plo", [P, 2, 512], f32r)
        ident = sb("ident", [P, P])
        iota = sb("iota", [P, S])
        SM = sb("SM", [P, 280])
        ps = ctx.enter_context(nc.psum_tensor("ps", [P, 8, 512], f32))

        used_cols = [0]

        def col(n):
            used_cols[0] += n
            return SM[:, used_cols[0] - n:used_cols[0]]

        pidx = col(1)
        pidx_i = col(1).bitcast(i32)
        cT, siluc = col(DC), col(DC)
        sumsq, meansq, std, rstd = col(TT), col(TT), col(TT), col(TT)
        pos_i, pos = col(TT).bitcast(i32), col(TT)
        lam2, lam = col(2), col(1)
        a_max, a_nmax, a_sum, a_rec = col(2), col(2), col(2), col(2)
        b_max, b_sum, b_rec = col(8), col(8), col(8)
        qk_stat = col(2 * QK_HEADS)
        ob_stat = col(TT * B_HEADS)
        conv_w = col(12)
        lb2, lb, omlb = col(2 * RH), col(RH), col(RH)

        warm = col(1)
        x_max, x_sum, x_rec = col(2), col(2), col(2)
        r_stat = col(8 * TT)

        big = BIG[:, :]
        mid = MID[:, :]
        mod = MOD[:, :].rearrange("p (m d) -> p m d", m=6)
        sh1, sc1, g1, sh2, sc2, g2 = (mod[:, m, :] for m in range(6))
        ada_acc = [big[:, 0:UW], H[:, :, :].rearrange("p t n -> p (t n)"), big[:, 0:UW]]
        ones = big[:, 16128:16128 + P]
        proj = big[:, 0:TT * IN_W].rearrange("p (t n) -> p t n", t=TT)
        lam_vec = big[:, 14848:15104].rearrange("p (k d) -> p k d", k=4)
        qk_gain = big[:, 15104:15360].rearrange("p (k d) -> p k d", k=4)
        subln = big[:, 15360:15488]
        inv_freq = big[:, 15488:15520]
        oa = big[:, 15520:15520 + TT * 256].rearrange("p (t n) -> p t n", t=TT)
        b_gate = mid[:, 4096:4096 + GL_W]
        gain = mid[:, 6144:7168]
        masks = MOD[:, 0:1024]
        rope_c = MOD[:, 1024:1536].rearrange("p (t k d) -> p t k d", t=TT, k=4)
        rope_s = MOD[:, 1536:2048].rearrange("p (t k d) -> p t k d", t=TT, k=4)
        rot = mid[:, 0:QK_W]
        ang = mid[:, 6144:6208].rearrange("p (t d) -> p t d", t=TT)
        cos = mid[:, 6208:6272].rearrange("p (t d) -> p t d", t=TT)
        sin = mid[:, 6272:6336].rearrange("p (t d) -> p t d", t=TT)
        atmp = mid[:, 6336:6400].rearrange("p (t d) -> p t d", t=TT)
        key_i = mid[:, 6400:6656].bitcast(i32)
        mtmp_i = mid[:, 6656:6912].bitcast(i32)
        qkT = mid[:, 0:NQK * S].rearrange("p (b t) -> p b t", b=NQK)
        a_s = [big[:, i * 768:(i + 1) * 768] for i in range(2)]
        a_pT = [big[:, 1536 + i * 768:1536 + (i + 1) * 768] for i in range(2)]
        b_p = [big[:, IN_W + i * 512:IN_W + (i + 1) * 512] for i in range(2)]
        b_p2 = [big[:, IN_W + 1024 + i * 512:IN_W + 1536 + i * 512] for i in range(2)]
        b_pT = [big[:, IN_W + 2048 + i * 512:IN_W + 2560 + i * 512] for i in range(2)]
        ob_sq = big[:, IN_W:IN_W + 2048]
        mixed = big[:, 0:2048].rearrange("p (t n) -> p t n", t=TT)
        lin_tmp = [mid[:, i * 512:(i + 1) * 512] for i in range(2)]
        qT = big[:, 0:NHH * S].rearrange("p (b t) -> p b t", b=NHH)
        keysT = big[:, 4096:4096 + NHH * N_KEYS].rearrange("p (b n) -> p b n", b=NHH)
        score = [mid[:, t * 2048:(t + 1) * 2048] for t in range(TT)]
        cand = big[:, 0:PH * PAIRS].rearrange("p (h n) -> p h n", h=PH)
        pair_f = [big[:, 512 + i * P:640 + i * P] for i in range(4)]
        top_v = [MOD[:, 2048 + t * 256:2304 + t * 256].rearrange("p (b k) -> p b k", b=NHH) for t in range(TT)]
        top_i = [MOD[:, 2560 + t * 256:2816 + t * 256].bitcast(u32).rearrange("p (b k) -> p b k", b=NHH)
                 for t in range(TT)]
        top_f = MOD[:, 3072:3328].rearrange("p (h s k) -> p h s k", h=PH, s=2)
        best_v = MOD[:, 3328:3456].rearrange("p (h k) -> p h k", h=PH)
        best_i = MOD[:, 3456:3584].bitcast(u32).rearrange("p (h k) -> p h k", h=PH)
        half_i = MOD[:, 3584:3712].bitcast(u32)
        quarter_i = big[:, 1024:1152].bitcast(u32)
        half_f = [MOD[:, 3712:3840], MOD[:, 3840:3968]]
        gate_e = MOD[:, 3968:4096].rearrange("p (h k) -> p h k", h=PH)
        gate_s, gate_r = MOD[:, 1792:1800], MOD[:, 1800:1808]
        route = MOD[:, 0:768].rearrange("p (t q k) -> p t q k", t=TT, q=3)
        routeT = MOD[:, 1024:1792].rearrange("p (q t) -> p q t", q=3)
        G = big.rearrange("p (j t) -> p j t", t=S)
        one_a = [mid[:, i * 1024:(i + 1) * 1024].rearrange("p (t n) -> p t n", t=GT) for i in range(2)]
        one_b = [mid[:, 2048 + i * 1024:3072 + i * 1024].rearrange("p (t n) -> p t n", t=GT) for i in range(2)]
        g_stage = [a.rearrange("p (j t) -> p j t", t=GC)
                   for a in (H[:, :, :].rearrange("p t n -> p (t n)"), MOD[:, 2048:4096])]
        g_spill = nc.dram_tensor("g_spill", (S // GC, P, N_KEYS // 2, GC), f32).ap()
        act_s = [mid[:, 4096 + i * 512:4608 + i * 512] for i in range(2)]
        act_w = [mid[:, 5120 + i * 512:5632 + i * 512] for i in range(2)]
        early = act_w + act_s + [a[:, i * 512:(i + 1) * 512] for a in (gain, MOD[:, 4096:5120]) for i in range(2)]
        mixT = big[:, 0:20 * S].rearrange("p (b t) -> p b t", b=20)
        conv_phi, conv_plo = (a[:, :, :].rearrange("p j (c t) -> p (j c) t", t=S) for a in (phi, plo))
        cb, cc, cx, hq, hz = (mixT[:, 4 * k:4 * k + 4, :] for k in range(5))
        hv = big[:, 5120:6144].rearrange("p (t n) -> p t n", t=TT)
        hg = big[:, 6144:7168].rearrange("p (t n) -> p t n", t=TT)
        conv_u = big[:, 7168:8192].rearrange("p (b t) -> p b t", b=4)
        conv_y = big[:, 8192:9216].rearrange("p (b t) -> p b t", b=4)
        sig = big[:, 9216:10240].rearrange("p (b t) -> p b t", b=4)
        dec = big[:, 10240:11264].rearrange("p (b t) -> p b t", b=4)
        rk = big[:, 11264:12288].rearrange("p (b t) -> p b t", b=4)
        lev_e = [big[:, 12288 + i * 1024:13312 + i * 1024].rearrange("p (b t) -> p b t", b=4) for i in range(2)]
        lev_q = big[:, 14336:15360].rearrange("p (b t) -> p b t", b=4)
        lev_k = big[:, 15360:16384].rearrange("p (b t) -> p b t", b=4)
        lmask = mid[:, 0:1024].rearrange("p (l t) -> p l t", l=8)
        rsc = mid[:, 2048:3072].rearrange("p (t h n) -> p t h n", t=TT, h=RH)
        rsc_x = mid[:, 3072:3584].rearrange("p (h n) -> p h n", h=RH)
        keep = mid[:, 3584:3840]
        lint = mid[:, 3840:3968].bitcast(i32)
        lsh = mid[:, 3968:4096].bitcast(i32)
        lup = mid[:, 4096:4224]
        hnorm = mid[:, 4608:5120]
        ro = mid[:, 5120:6144].rearrange("p (t n) -> p t n", t=TT)
        mem = MOD[:, 0:2048].rearrange("p (t n) -> p t n", t=TT)
        kT = MOD[:, 2048:4096].rearrange("p (b t) -> p b t", b=DC)
        vm = MOD[:, 4096:6144].rearrange("p (t n) -> p t n", t=TT)
        xqT = big[:, 0:2048].rearrange("p (b t) -> p b t", b=DC)
        x_p = [big[:, 2048 + i * 256:2304 + i * 256] for i in range(2)]
        x_pT = [big[:, 2560 + i * 512:3072 + i * 512].rearrange("p (k t) -> p k t", k=TT) for i in range(2)]
        wr = big[:, 8192:8192 + DC * 20].rearrange("p (c n) -> p c n", c=DC)
        r_bias = big[:, 8400:8420]
        r_log = big[:, 8448:8488].rearrange("p (t n) -> p t n", t=TT)
        r_prob = big[:, 8512:8552].rearrange("p (t n) -> p t n", t=TT)
        r_cmp = big[:, 8576:8576 + TT * 80].rearrange("p (t g a b) -> p t g a b", t=TT, g=5, a=4)
        r_tie = big[:, 8768:8768 + TT * 80].rearrange("p (t g a b) -> p t g a b", t=TT, g=5, a=4)
        r_rank = big[:, 8960:9000].rearrange("p (t n) -> p t n", t=TT)
        r_sel = big[:, 9024:9064].rearrange("p (t n) -> p t n", t=TT)
        r_low = big[:, 9088:9104].rearrange("p (a b) -> p a b", a=4)
        comb = big[:, 9152:9152 + TT * N_EXP].rearrange("p (t n) -> p t n", t=TT)
        silu_g = [big[:, i * 512:(i + 1) * 512] for i in range(2)]
        hid = [big[:, 1024 + i * 512:1536 + i * 512] for i in range(2)]
        wrhi = sb("wrhi", [P, DC, 20], f32r)
        wrlo = sb("wrlo", [P, DC, 20], f32r)

        raw_loaded = [sem("raw_loaded0"), sem("raw_loaded1")]
        unit_hi, unit_split, unit_used = sem("unit_hi"), sem("unit_split"), sem("unit_used")
        x_loaded, c_loaded, rows_loaded, gain_loaded = (
            sem("x_loaded"), sem("c_loaded"), sem("rows_loaded"), sem("gain_loaded"))
        keys_loaded, mix_loaded, mem_loaded, router_loaded = (
            sem("keys_loaded"), sem("mix_loaded"), sem("mem_loaded"), sem("router_loaded"))
        pool_chain, consts_ready = sem("pool_chain"), sem("consts_ready")
        dve_chain, act_chain = sem("dve_chain"), sem("act_chain")
        siluc_ready, ones_ready = sem("siluc_ready"), sem("ones_ready")
        ada_zeroed, b_ada_loaded, b_ada_late = sem("ada_zeroed"), sem("b_ada_loaded"), sem("b_ada_late")
        b_gate_loaded = sem("b_gate_loaded")
        ada_full, ada_free = sem("ada_full"), sem("ada_free")
        x_ready, norm_ss, norm_ms, norm_std = sem("x_ready"), sem("norm_ss"), sem("norm_ms"), sem("norm_std")
        rows_ready, tr_done, tr_hi, tr_lo = sem("rows_ready"), sem("tr_done"), sem("tr_hi"), sem("tr_lo")
        acc_free, keys_scored = sem("acc_free"), sem("keys_scored")
        angles_ready, sincos_ready, lam_dots, lam_exp = (
            sem("angles_ready"), sem("sincos_ready"), sem("lam_dots"), sem("lam_exp"))
        qk_sq, qk_summed, qk_ms, qk_std, rope_done = (
            sem("qk_sq"), sem("qk_summed"), sem("qk_ms"), sem("qk_std"), sem("rope_done"))
        gate_biased, gate_ready = sem("gate_biased"), sem("gate_ready")
        qkT_done, qkT_even, qkT_odd = sem("qkT_done"), sem("qkT_even"), sem("qkT_odd")
        a_scored, a_masked, a_prob, a_tr, a_trT, a_pv, a_out = (
            sem("a_scored"), sem("a_masked"), sem("a_prob"), sem("a_tr"), sem("a_trT"), sem("a_pv"), sem("a_out"))
        b_scored, b_bias, b_prob, b_mix, b_tr, b_trT, b_pv, b_out = (
            sem("b_scored"), sem("b_bias"), sem("b_prob"), sem("b_mix"), sem("b_tr"), sem("b_trT"),
            sem("b_pv"), sem("b_out"))
        ob_sqd, ob_ms, ob_std = sem("ob_sqd"), sem("ob_ms"), sem("ob_std")
        gate_shift, gate_exp, routed, route_tr, route_in = (
            sem("gate_shift"), sem("gate_exp"), sem("routed"), sem("route_tr"), sem("route_in"))
        oa_ready, ob_ready, g_full, g_free = sem("oa_ready"), sem("ob_ready"), sem("g_full"), sem("g_free")
        g_spilled, g_loaded = [sem("g_spilled0"), sem("g_spilled1")], sem("g_loaded")
        gelu_done, w_done, w_hi, w_lo = sem("gelu_done"), sem("w_done"), sem("w_hi"), sem("w_lo")
        lb_diff, lb_exp, z_sig, f_ready, f_log, lev_d, lev_exp, lev_qk, lev_full, lev_free = (
            sem("lb_diff"), sem("lb_exp"), sem("z_sig"), sem("f_ready"), sem("f_log"), sem("lev_d"), sem("lev_exp"), sem("lev_qk"),
            sem("lev_full"), sem("lev_free"))
        conv_ready, conv_hi, conv_lo, ro_full, ro_copied, ro_sq, ro_ms, ro_std = (
            sem("conv_ready"), sem("conv_hi"), sem("conv_lo"), sem("ro_full"),
            sem("ro_copied"), sem("ro_sq"), sem("ro_ms"), sem("ro_std"))
        x_scored, x_bias, x_prob, x_norm, x_tr, x_trT, xo_full, xo_hi, xo_lo = (
            sem("x_scored"), sem("x_bias"), sem("x_prob"), sem("x_norm"), sem("x_tr"), sem("x_trT"),
            sem("xo_full"), sem("xo_hi"), sem("xo_lo"))
        wr_hi, wr_lo, r_full, r_ready, r_exp = (
            sem("wr_hi"), sem("wr_lo"), sem("r_full"), sem("r_ready"), sem("r_exp"))
        m_silu, m_hid, m_hi, m_lo, d_free = sem("m_silu"), sem("m_hid"), sem("m_hi"), sem("m_lo"), sem("d_free")
        out_ready, out_stored = sem("out_ready"), sem("out_stored")

        N_IN = 0
        N_PA = N_IN + 2 * (IN_BLOCKS + 1)
        N_PB = N_PA + 4
        N_WO = N_PB + 4
        N_WQ = N_WO + 4

        def n_query(h):
            return N_WQ + max(0, 2 * h - 1)

        def n_scores(h):
            return N_WQ + min(2 * h + 2, 2 * PH - 1)

        N_MT = N_WQ + 2 * PH
        N_MV = N_MT + MIX_T
        N_K = N_MV + 4
        N_V = N_K + 4
        N_W2 = N_V + 4
        N_XQ = N_W2 + 4
        N_XO = N_XQ + 4
        SPLIT_U = U_IN

        GL0, V0 = QK_W, QK_W + GL_W

        def ada_bank(g):
            return 0 if g == 2 else 4

        def tr_place(t, k, first=0):
            if t == T_OA:
                return slice(0, 2), slice(0, S)
            per_tile = T_GROUPS[t] // TT
            tt, c = k // per_tile, first + 4 * (k % per_tile)
            return slice(c, c + 4), slice(tt * P, (tt + 1) * P)

        block = ctx.enter_context(nc.Block())

        @block.sync
        def _(sp):
            stream = io["stream"]
            for k in range(2):
                sp.dma_start(raw[:, k, :], stream[k, :, :]).then_inc(raw_loaded[k], 16)
            with sp.Fori(1, NU // 2) as i:
                for k in range(2):
                    sp.wait_ge(unit_split, 2 * i + (k - 1))
                    sp.dma_start(raw[:, k, :], stream[bass.ds(2 * i + k, 1), :, :].rearrange("a p n -> (a p) n")
                                 ).then_inc(raw_loaded[k], 16)
            for t in range(TT):
                sp.wait_ge(out_ready, t + 1)
                sp.dma_start(io["out"][t * P:(t + 1) * P, :], H[:, t, :]).then_inc(out_stored, 16)
            sp.wait_ge(out_stored, 16 * TT)

        @block.gpsimd
        def _(pool):
            nc.gpsimd.iota(iota[:, :], [[1, S]], base=0, channel_multiplier=0,
                           allow_small_or_imprecise_dtypes=True).then_inc(consts_ready, 1)
            nc.gpsimd.iota(pidx, [[0, 1]], base=0, channel_multiplier=1,
                           allow_small_or_imprecise_dtypes=True).then_inc(consts_ready, 1)
            nc.gpsimd.memset(ident[:, :], 0.0).then_inc(pool_chain, 1)
            pool.wait_ge(pool_chain, 1)
            nc.gpsimd.affine_select(out=ident[:, :], in_=ident[:, :], compare_op=ALU.not_equal, fill=1.0, base=0,
                                    pattern=[[-1, P]], channel_multiplier=1).then_inc(consts_ready, 1)

            def lo(u):
                pool.wait_ge(unit_hi, u - SPLIT_U + 1)
                nc.gpsimd.tensor_tensor(wlo[:, u % 2, :], raw[:, u % 2, :], whi[:, u % 2, :].bitcast(f32),
                                        ALU.subtract).then_inc(unit_split, 1)

            def load_gain(j):
                pool.dma_start(gain, io["gains"][j, :].partition_broadcast(P)).then_inc(gain_loaded, 16)

            load_gain(0)
            pool.wait_ge(unit_used, 2)
            pool.dma_start(b_gate, io["b_gate"].partition_broadcast(P)).then_inc(b_gate_loaded, 16)
            pool.dma_start(MOD[:, UW:ADA_GROUPS * UW], io["b_ada"][UW:ADA_GROUPS * UW].partition_broadcast(P)
                           ).then_inc(b_ada_late, 16)
            pool.wait_ge(b_gate_loaded, 16)
            pool.wait_ge(acc_free, 2 * -(-(QK_W + GL_W) // 512))
            for t in range(TT):
                nc.gpsimd.tensor_tensor(proj[:, t, GL0:GL0 + GL_W], proj[:, t, GL0:GL0 + GL_W], b_gate,
                                        ALU.add).then_inc(gate_biased, 1)
            pool.wait_ge(rope_done, TT)
            pool.wait_ge(rows_ready, ROWS[T_OB])
            load_gain(1)
            pool.wait_ge(rows_ready, ROWS[T_MIXED])
            pool.dma_start(keysT, io["keysT"].rearrange("p (b n) -> p b n", b=NHH)).then_inc(keys_loaded, 16)
            pool.wait_ge(rows_ready, ROWS[T_H2])
            for u in range(U_WQ + 2, U_PEER + NE + 2):
                if u == U_WQ + 2:
                    pool.wait_ge(unit_split, u)
                lo(u)
            for b in range(2):
                pool.wait_ge(g_spilled[b], 16 * (S // GC // 2))
            with pool.Fori(0, NB) as i:
                pool.wait_ge(w_done, i + 1)
                for j in range(2):
                    pool.dma_start(G[:, bass.ds(2 * i + j, 1), :].rearrange("p j (c t) -> p (j c) t", t=GC),
                                   g_spill[:, :, bass.ds(2 * i + j, 1), :].rearrange("c p j t -> p (c j) t")
                                   ).then_inc(g_loaded, 16)
            load_gain(2)
            pool.wait_ge(x_ready, 4)
            pool.dma_start(conv_w, io["conv_w"]).then_inc(mix_loaded, 16)
            pool.dma_start(lb2, io["hgrn_lb"]).then_inc(mix_loaded, 16)
            pool.dma_start(hnorm, io["hgrn_norm"].partition_broadcast(P)).then_inc(mix_loaded, 16)
            pool.dma_start(mem, io["mem"].rearrange("(t p) d -> p t d", p=P)).then_inc(mem_loaded, 16)
            pool.wait_ge(rows_ready, ROWS[T_MIX])
            load_gain(3)
            pool.wait_ge(rows_ready, ROWS[T_MEM])
            load_gain(4)
            pool.wait_ge(rows_ready, ROWS[T_HX])
            load_gain(5)
            pool.dma_start(wr[:, :, :], io["router"].rearrange("p (c n) -> p c n", c=DC)).then_inc(router_loaded, 16)
            pool.dma_start(r_bias, io["router_b"].partition_broadcast(P)).then_inc(router_loaded, 16)
            pool.wait_ge(rows_ready, ROWS[T_HF])
            load_gain(6)

        @block.scalar
        def _(act):
            chain = [0]

            def mark(ins):
                chain[0] += 1
                ins.then_inc(act_chain, 1)

            def settle():
                act.wait_ge(act_chain, chain[0])

            def hi(u, off=0, at=None, at_off=None):
                s = u - SPLIT_U
                at, at_off = (u, off) if at is None else (at, at_off)
                act.wait_ge(raw_loaded[u % 2], 16 * (at // 2 + 1) + 8 * at_off)
                if s >= 2:
                    act.wait_ge(unit_used, s - 1 + off)
                nc.scalar.activation(whi[:, u % 2, :], raw[:, u % 2, :], ACT.Copy).then_inc(unit_hi, 1)

            def used(u, off=0):
                act.wait_ge(unit_used, u - SPLIT_U + 1 + off)

            def evac(n, u, out, func=ACT.Copy, uoff=0, width=512):
                used(u, uoff)
                nc.scalar.activation(out, ps[:, n % 4, 0:width], func).then_inc(acc_free, 1)

            def norm(j, src, ready, counts):
                if j:
                    act.wait_ge(consts_ready, 3)
                    nc.scalar.activation(warm, pidx, ACT.Sqrt)
                for t in range(TT):
                    act.wait_ge(ready, counts[t])
                    nc.scalar.activation(H[:, t, :], src[:, t, :], ACT.Square,
                                         accum_out=sumsq[:, t:t + 1]).then_inc(norm_ss, 1)
                    act.wait_ge(norm_ms, TT * j + t + 1)
                    nc.scalar.activation(std[:, t:t + 1], meansq[:, t:t + 1], ACT.Sqrt).then_inc(norm_std, 1)

            def tr_high(t, first=0):
                for k in range(T_GROUPS[t]):
                    g = T_BASE[t] + k
                    chunks, tokens = tr_place(t, k, first)
                    act.wait_ge(tr_done, g + 1)
                    nc.scalar.activation(thi[:, chunks, tokens], ps[:, 4 + g % 2, :].rearrange(
                        "p (c t) -> p c t", t=tokens.stop - tokens.start), ACT.Copy).then_inc(tr_hi, 1)

            act.dma_start(cT, io["c"]).then_inc(c_loaded, 16)
            act.dma_start(X[:, :, :], io["x"].rearrange("(t p) d -> p t d", p=P)).then_inc(x_loaded, 16)
            act.wait_ge(ada_zeroed, 1)
            act.dma_start(ada_acc[0][0:1, :], io["b_ada"][0:UW].rearrange("(a n) -> a n", a=1)).then_inc(b_ada_loaded, 16)
            act.dma_start(lam_vec, io["lam"].partition_broadcast(P)).then_inc(rows_loaded, 16)
            act.dma_start(qk_gain, io["qk_gain"].partition_broadcast(P)).then_inc(rows_loaded, 16)
            act.dma_start(subln, io["subln"].partition_broadcast(P)).then_inc(rows_loaded, 16)
            act.dma_start(inv_freq, io["inv_freq"].partition_broadcast(P)).then_inc(rows_loaded, 16)
            act.dma_start(pos_i, io["positions"]).then_inc(rows_loaded, 16)

            act.wait_ge(c_loaded, 16)
            nc.scalar.activation(siluc, cT, ACT.Silu).then_inc(siluc_ready, 1)
            norm(0, X, x_loaded, (16, 16))
            hi(U_IN, 0, in_at(0), 0)
            hi(U_IN + 1, 0, in_at(1), 0)
            tr_high(T_H1)

            with act.Fori(0, 2) as i:
                for b in range(2):
                    hi(U_IN + 2 * b + 2, 4 * i, in_at(2 * b + 2), 4 * i)
                    hi(U_IN + 2 * b + 3, 4 * i, in_at(2 * b + 3), 4 * i)
                    for t in range(TT):
                        evac(2 * b + t, U_IN + 2 * b + 1, proj[:, t, bass.ds(1024 * i + 512 * b, 512)], uoff=4 * i)

            def in_high(k):
                if k < U_PA - U_IN:
                    hi(U_IN + k, 0, in_at(k), 0)

            def in_out(b):
                w = 512 if b < IN_BLOCKS else 256
                for t in range(TT):
                    evac(2 * b + t, min(U_IN + 2 * b + 1, U_PA - 1), proj[:, t, 512 * b:512 * b + w], width=w)

            def in_block(b):
                in_high(2 * b + 2)
                in_high(2 * b + 3)
                in_out(b)

            in_block(4)
            act.wait_ge(angles_ready, 1)
            nc.scalar.activation(sin, ang, ACT.Sin).then_inc(sincos_ready, 1)
            nc.scalar.activation(cos, atmp, ACT.Sin).then_inc(sincos_ready, 1)
            act.wait_ge(lam_dots, 1)
            nc.scalar.activation(lam2, lam2, ACT.Exp).then_inc(lam_exp, 1)
            in_block(5)
            in_block(6)
            act.wait_ge(acc_free, 2 * (QK_W // 512))

            def squares(t):
                nc.scalar.activation(rot, proj[:, t, 0:QK_W], ACT.Square).then_inc(qk_sq, 1)

            def roots(t):
                act.wait_ge(qk_ms, t + 1)
                nc.scalar.activation(qk_stat[:, t * QK_HEADS:(t + 1) * QK_HEADS],
                                     qk_stat[:, t * QK_HEADS:(t + 1) * QK_HEADS], ACT.Sqrt).then_inc(qk_std, 1)

            squares(0)
            roots(0)
            in_block(7)
            in_block(8)
            in_high(20)
            act.wait_ge(rope_done, 1)
            squares(1)
            in_high(21)
            in_out(9)
            roots(1)
            for b in range(10, 13):
                in_block(b)
            in_block(13)
            act.wait_ge(gate_biased, TT)
            for t in range(TT):
                nc.scalar.activation(proj[:, t, GL0:GL0 + GL_W], proj[:, t, GL0:GL0 + GL_W],
                                     ACT.Sigmoid).then_inc(gate_ready, 1)
            in_block(14)

            for g in range(0, NQK // 4 * TT, 2):
                act.wait_ge(qkT_done, g + 1)
                t, b4 = g % TT, g // TT
                nc.scalar.activation(qkT[:, 4 * b4:4 * b4 + 4, t * P:(t + 1) * P],
                                     ps[:, 4 + g % 4, :].rearrange("p (b t) -> p b t", b=4), ACT.Copy).then_inc(qkT_even, 1)

            def a_exp(i):
                act.wait_ge(a_masked, i + 1)
                nc.scalar.activation(a_s[i % 2], a_s[i % 2], ACT.Exp, bias=a_nmax[:, i % 2:i % 2 + 1],
                                     accum_out=a_sum[:, i % 2:i % 2 + 1]).then_inc(a_prob, 1)

            a_exp(0)
            for i in range(A_SLOTS * TT):
                if i + 1 < A_SLOTS * TT:
                    a_exp(i + 1)
                act.wait_ge(a_tr, i + 1)
                nc.scalar.activation(a_pT[i % 2], ps[:, 4:6, :].rearrange("p a n -> p (a n)")[:, 0:768], ACT.Copy
                                     ).then_inc(a_trT, 1)

            def b_copy(h):
                act.wait_ge(b_tr, h + 1)
                nc.scalar.activation(b_pT[h % 2], ps[:, 4 + h % 2, :], ACT.Copy).then_inc(b_trT, 1)

            def b_exp(h):
                act.wait_ge(b_bias, h + 1)
                if h >= 2:
                    act.wait_ge(b_tr, h - 1)
                for t in range(TT):
                    for m in range(2):
                        k = 4 * (h % 2) + 2 * m + t
                        nc.scalar.activation((b_p, b_p2)[m][h % 2][:, t * S:(t + 1) * S],
                                             ps[:, 2 * (h % 2) + m, t * S:(t + 1) * S], ACT.Exp,
                                             bias=b_max[:, k:k + 1], scale=HD ** -0.5,
                                             accum_out=b_sum[:, k:k + 1]).then_inc(b_prob, 1)

            b_exp(0)
            for h in range(B_HEADS):
                if h + 1 < B_HEADS:
                    b_exp(h + 1)
                b_copy(h)
            hi(U_PA)
            hi(U_PA + 1)
            act.wait_ge(b_out, B_HEADS)
            nc.scalar.activation(ob_sq, H[:, :, :].rearrange("p t n -> p (t n)"), ACT.Square).then_inc(ob_sqd, 1)
            tr_high(T_OA)
            act.wait_ge(ob_ms, 1)
            nc.scalar.activation(ob_stat, ob_stat, ACT.Sqrt).then_inc(ob_std, 1)

            hi(U_PA + 2)
            tr_high(T_OB)
            for u in range(U_PB, U_WO):
                hi(u + 2)
            tr_high(T_MIXED)
            for u in range(U_WO, U_WQ):
                hi(u + 2)

            norm(1, X, x_ready, (1, 2))
            tr_high(T_H2)
            def head_scores(h):
                act.wait_ge(keys_scored, h + 1)
                nc.scalar.activation(mid[:, 0:TT * 2048].rearrange("p (t n) -> p t n", t=TT)[:, :, 256 * h:256 * (h + 1)],
                                     ps[:, n_scores(h) % 4, :].rearrange("p (t n) -> p t n", t=TT), ACT.Copy
                                     ).then_inc(acc_free, 1)

            for h in range(PH):
                hi(U_WQ + h + 2)
                evac(n_query(h), U_WQ + h, qT[:, 2 * h:2 * h + 2, :].rearrange("p b t -> p (b t)"))
                if h:
                    head_scores(h - 1)
            head_scores(PH - 1)

            def kept_exp(t):
                act.wait_ge(gate_shift, t + 1)
                nc.scalar.activation(gate_e, gate_e, ACT.Exp).then_inc(gate_exp, 1)

            u0 = U_PEER
            for i in range(NE):
                hi(u0 + i + 2)
                used(u0 + i)
                nc.scalar.activation(early[i], ps[:, 4 + i % 2, :], ACT.Gelu).then_inc(gelu_done, 1)
                if i == NE // 2:
                    kept_exp(0)
            kept_exp(1)
            for q in range(3):
                act.wait_ge(route_tr, q + 1)
                nc.scalar.activation(routeT[:, q, :], ps[:, 4 + q % 2, 0:S], ACT.Copy).then_inc(route_in, 1)

            def gates_out(i, first):
                per = GC // GT
                for b in range(2):
                    for k in range(per):
                        n = b * per + k
                        act.wait_ge(g_full, 2 * per * i + (n + 1))
                        got = (ps[:, 4 + 2 * (n % 2):6 + 2 * (n % 2), :].rearrange("p a n -> p (a n)")
                               .rearrange("p (t j) -> p j t", j=N_KEYS))
                        nc.scalar.activation(G[:, :, bass.ds(2 * GC * i + n * GT, GT)], got[:, 0:2 * NB, :],
                                             ACT.Copy).then_inc(g_free, 1)
                        if k == 0 and not first:
                            act.wait_ge(g_spilled[b], 16 * i)
                        nc.scalar.activation(g_stage[b][:, :, k * GT:(k + 1) * GT], got[:, 2 * NB:, :],
                                             ACT.Copy).then_inc(g_free, 1)
                    act.wait_ge(g_free, 4 * per * i + 2 * per * (b + 1))
                    act.dma_start(g_spill[bass.ds(2 * i + b, 1), :, :, :].rearrange("c p j t -> (c p) j t"),
                                  g_stage[b]).then_inc(g_spilled[b], 16)

            gates_out(0, True)
            with act.Fori(1, S // (2 * GC)) as i:
                gates_out(i, False)
            def gated_high(i, off=0, source=None):
                act.wait_ge(w_done, i + 1 + off)
                nc.scalar.activation(phi[:, i % 2, :], act_w[i % 2] if source is None else source, ACT.Copy
                                     ).then_inc(w_hi, 1)

            def expert_act(i, off=0):
                used(u1 if i == NE else u1 + 2 * (i - NE) - 1, 2 * off)
                nc.scalar.activation(act_s[i % 2], ps[:, 4 + i % 2, :], ACT.Gelu).then_inc(gelu_done, 1)
                gated_high(i, off)

            for i in range(NE):
                if i >= 2:
                    hi(u0 + NE + i)
                gated_high(i, 0, early[i])
            u1 = u0 + 2 * NE
            hi(u1)
            hi(u1 + 1)
            hi(u1 + 2)
            expert_act(NE)
            hi(u1 + 3)
            expert_act(NE + 1)
            hi(u1 + 4)
            with act.Fori(0, (NP - NE - 2) // 2) as r:
                for k in (1, 2):
                    hi(u1 + 2 * k + 3, 4 * r)
                    expert_act(NE + k + 1, 2 * r)
                    hi(u1 + 2 * k + 4, 4 * r)
            hi(u0 + 2 * NP + 1)

            norm(2, X, x_ready, (3, 4))
            tr_high(T_MIX)
            act.wait_ge(lb_diff, 1)
            nc.scalar.activation(lb, lb, ACT.Exp).then_inc(lb_exp, 1)
            norm(3, mem, mem_loaded, (16, 16))
            for u in range(MIX_T):
                hi(U_MIX + u + 2)
                evac(N_MT + u, U_MIX + u, mixT[:, 2 * u:2 * u + 2, :].rearrange("p b t -> p (b t)"))
            act.wait_ge(acc_free, N_MT + MIX_T)
            nc.scalar.activation(sig, hz, ACT.Sigmoid).then_inc(z_sig, 1)
            nc.scalar.activation(rk, hz, ACT.Sigmoid, scale=-1.0).then_inc(z_sig, 1)
            hi(U_MIX + MIX_T + 2)
            act.wait_ge(f_ready, 1)
            nc.scalar.activation(dec, sig, ACT.Ln).then_inc(f_log, 1)
            hi(U_MIX + MIX_T + 3)
            for t in range(TT):
                evac(N_MV + t, U_MIX + MIX_T + 1, hv[:, t, :])
            hi(U_KV)
            hi(U_KV + 1)
            for t in range(TT):
                evac(N_MV + 2 + t, U_MIX + MIX_T + 3, hg[:, t, :], ACT.Silu)
            act.wait_ge(conv_ready, 1)
            nc.scalar.activation(conv_phi, conv_y, ACT.Copy).then_inc(conv_hi, 1)
            tr_high(T_MEM)

            def memory(u):
                if u < 4:
                    evac(N_K + u, U_KV + u, kT[:, 2 * u:2 * u + 2, :].rearrange("p b t -> p (b t)"))
                elif u % 2:
                    for t in range(TT):
                        b = (u - 4) // 2
                        evac(N_V + 2 * b + t, U_KV + u, vm[:, t, 512 * b:512 * (b + 1)])

            for l in range(1, LEVELS + 2):
                act.wait_ge(lev_d, l)
                mark(nc.scalar.activation(lev_e[l % 2], lev_e[l % 2], ACT.Abs))
                settle()
                nc.scalar.activation(lev_e[l % 2], lev_e[l % 2], ACT.Exp, scale=-1.0).then_inc(lev_exp, 1)
                if l >= 2:
                    memory(l - 2)
                    hi(U_KV + l)
            memory(LEVELS)
            hi(U_KV + LEVELS + 2)
            for t in range(TT):
                act.wait_ge(ro_full, t + 1)
                nc.scalar.activation(ro[:, t, :], ps[:, 4 + t, :], ACT.Copy).then_inc(ro_copied, 1)
            act.wait_ge(ro_copied, TT)
            nc.scalar.activation(lev_q.rearrange("p b t -> p (b t)"), ro.rearrange("p t n -> p (t n)"),
                                 ACT.Square).then_inc(ro_sq, 1)
            act.wait_ge(ro_ms, 1)
            nc.scalar.activation(r_stat[:, 0:TT * RH], r_stat[:, 0:TT * RH], ACT.Sqrt).then_inc(ro_std, 1)
            tr_high(T_YB, 4)
            for u in range(U_WO2, U_XQ):
                hi(u + 2)

            norm(4, X, acc_free, (N_W2 + 3, N_W2 + 4))
            tr_high(T_HX)
            for u in range(4):
                hi(U_XQ + u + 2)
                evac(N_XQ + u, U_XQ + u, xqT[:, 2 * u:2 * u + 2, :].rearrange("p b t -> p (b t)"))
            def x_exp(i):
                act.wait_ge(x_bias, i + 1)
                nc.scalar.activation(x_p[i % 2], ps[:, i % 2, 0:S], ACT.Exp, bias=x_max[:, i % 2:i % 2 + 1],
                                     scale=XD ** -0.5, accum_out=x_sum[:, i % 2:i % 2 + 1]).then_inc(x_prob, 1)

            def x_out(h):
                act.wait_ge(xo_full, h + 1)
                nc.scalar.activation(thi[:, 2 * h:2 * h + 2, :].rearrange("p c t -> p (c t)"),
                                     ps[:, 6 + h % 2, :], ACT.Copy).then_inc(xo_hi, 1)

            x_exp(0)
            for i in range(XH * TT):
                h, t = i // TT, i % TT
                if i + 1 < XH * TT:
                    x_exp(i + 1)
                act.wait_ge(x_tr, i + 1)
                nc.scalar.activation(x_pT[h % 2][:, :, t * P:(t + 1) * P],
                                     ps[:, 4 + i % 2, 0:S].rearrange("p (k t) -> p k t", k=TT),
                                     ACT.Copy).then_inc(x_trT, 1)
                if t == TT - 1 and h:
                    x_out(h - 1)
            x_out(XH - 1)
            for u in range(U_XO, U_MOE):
                hi(u + 2)

            act.wait_ge(router_loaded, 32)
            nc.scalar.activation(wrhi[:, :, :], wr, ACT.Copy).then_inc(wr_hi, 1)
            norm(5, X, acc_free, (N_XO + 3, N_XO + 4))
            tr_high(T_HF)
            act.wait_ge(r_ready, 1)
            nc.scalar.activation(r_prob, r_log, ACT.Exp).then_inc(r_exp, 1)

            def expert(u, off, uoff, last):
                for j in range(2):
                    used(u + 2 * j, uoff)
                    nc.scalar.activation(silu_g[j], ps[:, 4 + 2 * j, :], ACT.Silu).then_inc(m_silu, 1)
                    hi(u + 2 * j + 2, uoff)
                    hi(u + 2 * j + 3, uoff)
                    act.wait_ge(m_hid, j + 1 + 2 * off)
                    nc.scalar.activation(phi[:, j, :], hid[j], ACT.Copy).then_inc(m_hi, 1)
                if not last:
                    hi(u + 6, uoff)
                    hi(u + 7, uoff)

            with act.Fori(0, N_EXP - 1) as e:
                expert(U_MOE, e, 6 * e, False)
            expert(U_MOE + 6 * (N_EXP - 1), N_EXP - 1, 0, True)
            norm(6, X, d_free, (4 * N_EXP - 1, 4 * N_EXP))

        @block.vector
        def _(dve):
            chain = [0]

            def mark(ins):
                chain[0] += 1
                ins.then_inc(dve_chain, 1)

            def settle():
                dve.wait_ge(dve_chain, chain[0])

            def lo(u, off=0):
                s = u - SPLIT_U
                dve.wait_ge(unit_hi, s + 1 + off)
                nc.vector.tensor_tensor(wlo[:, u % 2, :], raw[:, u % 2, :], whi[:, u % 2, :].bitcast(f32),
                                        ALU.subtract).then_inc(unit_split, 1)

            def used(u, off=0):
                dve.wait_ge(unit_used, u - SPLIT_U + 1 + off)

            def tr_low(t, first=0):
                for k in range(T_GROUPS[t]):
                    g = T_BASE[t] + k
                    chunks, tokens = tr_place(t, k, first)
                    dve.wait_ge(tr_hi, g + 1)
                    nc.vector.tensor_tensor(tlo[:, chunks, tokens], ps[:, 4 + g % 2, :].rearrange(
                        "p (c t) -> p c t", t=tokens.stop - tokens.start), thi[:, chunks, tokens].bitcast(f32),
                        ALU.subtract).then_inc(tr_lo, 1)

            def norm(j, src, out_sem, scale=None, shift=None, meanwhile=None):
                for t in range(TT):
                    dve.wait_ge(norm_ss, TT * j + t + 1)
                    nc.vector.tensor_scalar(meansq[:, t:t + 1], sumsq[:, t:t + 1], 1.0 / D, EPS, ALU.mult,
                                            ALU.add).then_inc(norm_ms, 1)
                    dve.wait_ge(norm_std, TT * j + t + 1)
                    mark(nc.vector.reciprocal(rstd[:, t:t + 1], std[:, t:t + 1]))
                    dve.wait_ge(gain_loaded, 16 * (j + 1))
                    settle()
                    last = nc.vector.scalar_tensor_tensor(H[:, t, :], src[:, t, :], rstd[:, t:t + 1], gain,
                                                          ALU.mult, ALU.mult)
                    if scale is None:
                        last.then_inc(out_sem, 1)
                        continue
                    mark(last)
                    if meanwhile is None:
                        modulate(t, out_sem, scale, shift)
                if meanwhile is not None:
                    meanwhile()
                    for t in range(TT):
                        modulate(t, out_sem, scale, shift)

            def modulate(t, out_sem, scale, shift):
                settle()
                mark(nc.vector.tensor_tensor(H[:, t, :], H[:, t, :], scale, ALU.mult))
                settle()
                nc.vector.tensor_tensor(H[:, t, :], H[:, t, :], shift, ALU.add).then_inc(out_sem, 1)

            def root_mean(stat, width, ready, ms, rooted, count):
                dve.wait_ge(*ready)
                nc.vector.tensor_scalar(stat, stat, 1.0 / width, EPS, ALU.mult, ALU.add).then_inc(ms, 1)
                dve.wait_ge(rooted, count)
                mark(nc.vector.reciprocal(stat, stat))
                settle()

            nc.vector.memset(ada_acc[0], 0.0).then_inc(ada_zeroed, 1)
            nc.vector.memset(ones, 1.0).then_inc(ones_ready, 1)
            dve.wait_ge(siluc_ready, 1)
            dve.wait_ge(b_ada_loaded, 16)

            def ada_sum(u):
                g, c = u // DC, u % DC
                at = u if g == 0 else U_PA - ADA_LATE + u - DC
                dve.wait_ge(raw_loaded[at % 2], 16 * (at // 2 + 1))
                if c:
                    dve.wait_ge(unit_split, at)
                if g and c == 0:
                    last = nc.vector.tensor_scalar(ada_acc[g], raw[:, at % 2, :], siluc[:, 0:1], None, ALU.mult)
                else:
                    last = nc.vector.scalar_tensor_tensor(ada_acc[g], raw[:, at % 2, :], siluc[:, c:c + 1], ada_acc[g],
                                                          ALU.mult, ALU.add)
                last.then_inc(unit_split, 1)

            def ada_rows(g):
                dve.wait_ge(ada_full, g + 1)
                for m in range(4):
                    row = 4 * g + m
                    plus = 1.0 if row // 2 in (1, 4) else 0.0
                    got, out = ps[:, ada_bank(g) + m, :], MOD[:, row * 512:(row + 1) * 512]
                    if g == 0:
                        last = nc.vector.tensor_scalar(out, got, plus, None, ALU.add)
                    else:
                        last = nc.vector.scalar_tensor_tensor(out, got, plus, out, ALU.add, ALU.add)
                    last.then_inc(ada_free, 1)

            def first_rows():
                for u in range(3, DC):
                    ada_sum(u)
                ada_rows(0)
                dve.wait_ge(ada_free, 4)

            for u in range(3):
                ada_sum(u)
            norm(0, X, rows_ready, sc1, sh1, first_rows)
            lo(U_IN)
            lo(U_IN + 1)
            tr_low(T_H1)

            with dve.Fori(0, 2) as i:
                for k in range(4):
                    lo(U_IN + 2 + k, 4 * i)

            def in_block(b):
                for k in (2 * b + 2, 2 * b + 3):
                    if k < U_PA - U_IN:
                        lo(U_IN + k)

            in_block(4)
            dve.wait_ge(rows_loaded, 16 * 5)
            dve.wait_ge(rows_ready, ROWS[T_H1])
            dve.wait_ge(consts_ready, 3)
            mark(nc.vector.tensor_copy(pos, pos_i))
            mark(nc.vector.tensor_copy(pidx_i, pidx))
            mark(nc.vector.tensor_copy(key_i, iota[:, :]))
            settle()
            for t in range(TT):
                mark(nc.vector.tensor_scalar(ang[:, t, :], inv_freq, pos[:, t:t + 1], None, ALU.mult))
            settle()
            magic = 1.5 * 2.0 ** 23
            mark(nc.vector.tensor_scalar(atmp, ang, 1.0 / (2.0 * math.pi), magic, ALU.mult, ALU.add))
            settle()
            mark(nc.vector.tensor_scalar(atmp, atmp, magic, None, ALU.subtract))
            for part in (6.28125, 1.9350051879882812e-3, 3.0199159819566e-7):
                settle()
                mark(nc.vector.scalar_tensor_tensor(ang, atmp, -part, ang, ALU.mult, ALU.add))
            settle()
            mark(nc.vector.tensor_scalar(ang, ang, 3.1415925, -3.1415925, ALU.min, ALU.max))
            settle()
            mark(nc.vector.scalar_tensor_tensor(atmp, ang, -1.0, ang, ALU.mult, ALU.max))
            settle()
            nc.vector.tensor_scalar(atmp, atmp, -1.0, math.pi / 2, ALU.mult, ALU.add).then_inc(angles_ready, 1)
            lam_prod = mid[:, 6912:7040].rearrange("p (a d) -> p a d", a=2)
            mark(nc.vector.tensor_tensor(lam_prod, lam_vec[:, 0:4:2, :], lam_vec[:, 1:4:2, :], ALU.mult))
            settle()
            nc.vector.tensor_reduce(lam2, lam_prod, axis=AX.X, op=ALU.add).then_inc(lam_dots, 1)
            in_block(5)
            for t, at in ((0, 0), (1, 768)):
                band = masks[:, at:at + S]
                mark(nc.vector.tensor_scalar(band, iota[:, :], pidx, float(t * P), ALU.subtract, ALU.subtract))
                settle()
                mark(nc.vector.scalar_tensor_tensor(band, band, -1.0, band, ALU.mult, ALU.max))
                settle()
                mark(nc.vector.tensor_scalar(band, band, float(A_REACH), NEG, ALU.is_gt, ALU.mult))
            for g in (1, 2):
                mark(nc.vector.tensor_scalar(mtmp_i, key_i, pidx_i, A_DIL[g] - 1, ALU.bitwise_xor, ALU.bitwise_and))
                settle()
                mark(nc.vector.tensor_scalar(masks[:, g * S:(g + 1) * S], mtmp_i, 0.0, NEG, ALU.not_equal, ALU.mult))
                settle()
            in_block(6)
            dve.wait_ge(sincos_ready, 2)
            hf32 = HD // 2
            for t in range(TT):
                for k in range(4):
                    g_lo, g_hi = qk_gain[:, k, 0:hf32], qk_gain[:, k, hf32:HD]
                    mark(nc.vector.tensor_tensor(rope_c[:, t, k, 0:hf32], cos[:, t, :], g_lo, ALU.mult))
                    mark(nc.vector.tensor_tensor(rope_c[:, t, k, hf32:HD], cos[:, t, :], g_hi, ALU.mult))
                    mark(nc.vector.scalar_tensor_tensor(rope_s[:, t, k, 0:hf32], sin[:, t, :], -1.0, g_hi,
                                                        ALU.mult, ALU.mult))
                    mark(nc.vector.tensor_tensor(rope_s[:, t, k, hf32:HD], sin[:, t, :], g_lo, ALU.mult))
            dve.wait_ge(lam_exp, 1)
            mark(nc.vector.tensor_scalar(lam, lam2[:, 0:1], lam2[:, 1:2], LAM_INIT, ALU.subtract, ALU.add))
            settle()
            mark(nc.vector.tensor_scalar(lam, lam, -1.0, None, ALU.mult))
            mark(nc.vector.tensor_scalar(subln, subln, 1.0 - LAM_INIT, None, ALU.mult))
            settle()
            kinds = ((0, 12), (12, 24), (24, 40), (40, 56))
            for t in range(TT):
                stat = qk_stat[:, t * QK_HEADS:(t + 1) * QK_HEADS]
                rows = proj[:, t, 0:QK_W].rearrange("p (h d) -> p h d", d=HD)
                rots = rot.rearrange("p (h d) -> p h d", d=HD)
                dve.wait_ge(qk_sq, t + 1)
                nc.vector.tensor_reduce(stat, rots, axis=AX.X, op=ALU.add).then_inc(qk_summed, 1)
                if t:
                    lo(U_IN + 21)
                root_mean(stat, HD, (qk_summed, t + 1), qk_ms, qk_std, t + 1)
                mark(nc.vector.tensor_tensor(rows, rows, stat.unsqueeze(2).broadcast_to([P, QK_HEADS, HD]), ALU.mult))
                in_block((7, 10)[t])
                settle()
                for k, (a, b) in enumerate(kinds):
                    for out_h, in_h in ((0, hf32), (hf32, 0)):
                        table = rope_s[:, t, k, out_h:out_h + hf32].unsqueeze(1).broadcast_to([P, b - a, hf32])
                        mark(nc.vector.tensor_tensor(rots[:, a:b, out_h:out_h + hf32], rows[:, a:b, in_h:in_h + hf32],
                                                     table, ALU.mult))
                in_block((8, 11)[t])
                settle()
                for k, (a, b) in enumerate(kinds):
                    table = rope_c[:, t, k, :].unsqueeze(1).broadcast_to([P, b - a, HD])
                    mark(nc.vector.tensor_tensor(rows[:, a:b, :], rows[:, a:b, :], table, ALU.mult))
                if t:
                    in_block(12)
                settle()
                nc.vector.tensor_tensor(rows, rows, rots, ALU.add).then_inc(rope_done, 1)
                if t == 0:
                    lo(U_IN + 20)
            in_block(13)
            in_block(14)
            dve.wait_ge(gate_biased, TT)

            for g in range(1, NQK // 4 * TT, 2):
                dve.wait_ge(qkT_done, g + 1)
                t, b4 = g % TT, g // TT
                nc.vector.tensor_copy(qkT[:, 4 * b4:4 * b4 + 4, t * P:(t + 1) * P],
                                      ps[:, 4 + g % 4, :].rearrange("p (b t) -> p b t", b=4)).then_inc(qkT_odd, 1)

            def a_mask(i):
                t, b = i // A_SLOTS, i % 2
                sc = ps[:, 2 * b:2 * b + 2, :].rearrange("p a n -> p (a n)")[:, 0:768]
                dve.wait_ge(a_scored, i + 1)
                mark(nc.vector.scalar_tensor_tensor(a_s[b], sc, HD ** -0.5, masks[:, t * S:t * S + 768],
                                                    ALU.mult, ALU.add))
                settle()
                mark(nc.vector.tensor_reduce(a_max[:, b:b + 1], a_s[b], axis=AX.X, op=ALU.max))
                settle()
                nc.vector.tensor_scalar(a_nmax[:, b:b + 1], a_max[:, b:b + 1], -1.0, None,
                                        ALU.mult).then_inc(a_masked, 1)

            def a_inverse(i):
                b = i % 2
                dve.wait_ge(a_tr, i + 1)
                if i >= 2:
                    dve.wait_ge(a_out, i - 1)
                mark(nc.vector.reciprocal(a_rec[:, b:b + 1], a_sum[:, b:b + 1]))

            def a_rows(i):
                t, h, b = i // A_SLOTS, i % A_SLOTS, i % 2
                dve.wait_ge(a_pv, i + 1)
                settle()
                nc.vector.tensor_scalar(oa[:, t, h * HD:(h + 1) * HD], ps[:, 6 + b, 0:HD], a_rec[:, b:b + 1], None,
                                        ALU.mult).then_inc(a_out, 1)

            n_a = A_SLOTS * TT
            a_mask(0)
            a_mask(1)
            for i in range(n_a):
                a_inverse(i)
                ada_sum(DC + i)
                if i + 2 < n_a:
                    a_mask(i + 2)
                if i:
                    a_rows(i - 1)
            a_rows(n_a - 1)

            def b_maxima(h):
                b = h % 2
                dve.wait_ge(b_scored, h + 1)
                mark(nc.vector.tensor_reduce(b_max[:, 4 * b:4 * b + 4],
                                             ps[:, 2 * b:2 * b + 2, :].rearrange("p m (t n) -> p (m t) n", t=TT),
                                             axis=AX.X, op=ALU.max))
                settle()
                nc.vector.tensor_scalar(b_max[:, 4 * b:4 * b + 4], b_max[:, 4 * b:4 * b + 4], -(HD ** -0.5), None,
                                        ALU.mult).then_inc(b_bias, 1)

            def b_weights(h):
                b = h % 2
                r = b_rec[:, 4 * b:4 * b + 4]
                dve.wait_ge(b_prob, 4 * (h + 1))
                mark(nc.vector.reciprocal(r, b_sum[:, 4 * b:4 * b + 4]))
                settle()
                mark(nc.vector.tensor_scalar(r[:, 2:4], r[:, 2:4], lam, None, ALU.mult))
                settle()
                for t in range(TT):
                    mark(nc.vector.tensor_scalar(b_p2[b][:, t * S:(t + 1) * S], b_p2[b][:, t * S:(t + 1) * S],
                                                 r[:, 2 + t:3 + t], None, ALU.mult))
                settle()
                for t in range(TT):
                    nc.vector.scalar_tensor_tensor(b_p[b][:, t * S:(t + 1) * S], b_p[b][:, t * S:(t + 1) * S],
                                                   r[:, t:t + 1], b_p2[b][:, t * S:(t + 1) * S],
                                                   ALU.mult, ALU.add).then_inc(b_mix, 1)

            def b_rows(h):
                dve.wait_ge(b_pv, h + 1)
                nc.vector.tensor_copy(H[:, :, h * P:(h + 1) * P],
                                      ps[:, 6 + h % 2, 0:TT * P].rearrange("p (t n) -> p t n", t=TT)).then_inc(b_out, 1)

            b_maxima(0)
            b_maxima(1)
            dve.wait_ge(b_ada_late, 16)
            ada_rows(1)
            for h in range(B_HEADS):
                b_weights(h)
                ada_sum(2 * DC + h)
                if h:
                    b_rows(h - 1)
                if h + 2 < B_HEADS:
                    b_maxima(h + 2)
            b_rows(B_HEADS - 1)
            lo(U_PA)
            lo(U_PA + 1)
            ada_rows(2)
            tr_low(T_OA)
            dve.wait_ge(ob_sqd, 1)
            mark(nc.vector.tensor_reduce(ob_stat, ob_sq.rearrange("p (h d) -> p h d", d=P), axis=AX.X, op=ALU.add))
            root_mean(ob_stat, P, (dve_chain, chain[0]), ob_ms, ob_std, 1)
            obv = H[:, :, :].rearrange("p t (h d) -> p (t h) d", d=P)
            mark(nc.vector.tensor_tensor(obv, obv, ob_stat.unsqueeze(2).broadcast_to([P, TT * B_HEADS, P]), ALU.mult))
            settle()
            for t in range(TT):
                rows = obv[:, t * B_HEADS:(t + 1) * B_HEADS, :]
                nc.vector.tensor_tensor(rows, rows, subln.unsqueeze(1).broadcast_to([P, B_HEADS, P]),
                                        ALU.mult).then_inc(rows_ready, 1)

            def group(n, u, t, h, mul, out, first, last_sem, total=None):
                used(u)
                cols = slice(h * 512, (h + 1) * 512)
                if first:
                    ins = nc.vector.tensor_tensor(out[:, t, cols], ps[:, n % 4, :], mul, ALU.mult)
                    ins.then_inc(acc_free, 1)
                    return
                settle()
                nc.vector.tensor_tensor(lin_tmp[n % 2], ps[:, n % 4, :], mul, ALU.mult).then_inc(acc_free, 1)
                dve.wait_ge(acc_free, n + 1)
                ins = nc.vector.tensor_tensor((out if total is None else total)[:, t, cols], out[:, t, cols], lin_tmp[n % 2],
                                              ALU.add)
                if last_sem is None:
                    mark(ins)
                else:
                    ins.then_inc(last_sem, 1)

            dve.wait_ge(ada_free, 4 * ADA_GROUPS)
            lo(U_PA + 2)
            dve.wait_ge(gate_ready, TT)
            for n in range(4):
                t, h = n // 2, n % 2
                group(N_PA + n, U_PA, t, h, proj[:, t, GL0 + h * 512:GL0 + (h + 1) * 512], mixed, True, None)
            tr_low(T_OB)
            for b in range(2):
                lo(U_PB + 2 * b + 2)
                for t in range(TT):
                    group(N_PB + 2 * b + t, U_PB + 2 * b + 1, t, b, proj[:, t, GL0 + D + b * 512:GL0 + D + (b + 1) * 512],
                          mixed, False, rows_ready if b == 1 else None, H)
                lo(U_PB + 2 * b + 3)
            tr_low(T_MIXED)
            for b in range(2):
                lo(U_WO + 2 * b + 2)
                for t in range(TT):
                    group(N_WO + 2 * b + t, U_WO + 2 * b + 1, t, b, g1[:, b * 512:(b + 1) * 512], X, False,
                          x_ready if b == 1 else None)
                lo(U_WO + 2 * b + 3)

            settle()
            dve.wait_ge(x_ready, TT)
            norm(1, X, rows_ready, sc2, sh2)
            tr_low(T_H2)
            low = -3.0e38

            def keep_16(rows, vals, idx, n):
                for half in range(2):
                    k8 = slice(8 * half, 8 * half + 8)
                    for b in range(n):
                        mark(nc.vector.max(vals(b)[:, k8], rows(b)))
                    settle()
                    for b in range(n):
                        mark(nc.vector.max_index(idx(b)[:, k8], vals(b)[:, k8], rows(b)))
                    if half == 0:
                        for b in range(n):
                            mark(nc.vector.match_replace(rows(b), vals(b)[:, k8], rows(b), low))
                        settle()

            def head_keys(h):
                dve.wait_ge(acc_free, n_scores(h) + 1)
                keep_16(lambda b: score[b // 2][:, (2 * h + b % 2) * N_KEYS:(2 * h + b % 2 + 1) * N_KEYS],
                        lambda b: top_v[b // 2][:, 2 * h + b % 2, :], lambda b: top_i[b // 2][:, 2 * h + b % 2, :],
                        2 * TT)

            for h in range(PH):
                head_keys(h)
            for t in range(TT):
                v4 = top_v[t].rearrange("p (h s) k -> p h s k", s=2)
                settle()
                at = 0
                for first, n, w in PAIR_BLOCKS:
                    mark(nc.vector.tensor_tensor(
                        cand[:, :, at:at + n * w].rearrange("p h (a b) -> p h a b", a=n),
                        v4[:, :, 0, first:first + n].unsqueeze(3).broadcast_to([P, PH, n, w]),
                        v4[:, :, 1, 0:w].unsqueeze(2).broadcast_to([P, PH, n, w]), ALU.add))
                    at += n * w
                settle()
                keep_16(lambda b: cand[:, b, :], lambda b: best_v[:, b, :], lambda b: best_i[:, b, :], PH)
                settle()
                mark(nc.vector.tensor_copy(top_f.rearrange("p h s k -> p (h s) k"), top_i[t]))
                best_flat = best_i.rearrange("p h k -> p (h k)")
                c, start, c8, c4 = pair_f
                mark(nc.vector.tensor_copy(c, best_flat))
                mark(nc.vector.tensor_scalar(half_i, best_flat, 3, None, ALU.logical_shift_right))
                mark(nc.vector.tensor_scalar(quarter_i, best_flat, 2, None, ALU.logical_shift_right))
                settle()
                mark(nc.vector.tensor_copy(c8, half_i))
                mark(nc.vector.tensor_copy(c4, quarter_i))
                settle()
                mark(nc.vector.tensor_scalar(c8, c8, -1.0, 0.0, ALU.add, ALU.max))
                settle()
                mark(nc.vector.scalar_tensor_tensor(c8, c4, -6.0, c8, ALU.add, ALU.max))
                settle()
                mark(nc.vector.scalar_tensor_tensor(half_f[0], c, -48.0, c8, ALU.add, ALU.max))
                settle()
                mark(nc.vector.tensor_scalar(start, half_f[0], 8.0, 8.0, ALU.mult, ALU.add))
                mark(nc.vector.tensor_scalar(c4, half_f[0], 4.0, 24.0, ALU.mult, ALU.add))
                settle()
                mark(nc.vector.scalar_tensor_tensor(start, half_f[0], 16.0, start, ALU.mult, ALU.min))
                mark(nc.vector.scalar_tensor_tensor(c4, half_f[0], 48.0, c4, ALU.add, ALU.min))
                settle()
                mark(nc.vector.tensor_tensor(start, start, c4, ALU.min))
                settle()
                mark(nc.vector.tensor_tensor(half_f[1], c, start, ALU.subtract))
                settle()
                for s in range(2):
                    pick = score[s].rearrange("p (k j) -> p k j", j=TOPK)
                    mark(nc.vector.tensor_tensor(pick, half_f[s].unsqueeze(2).broadcast_to([P, PH * TOPK, TOPK]),
                                                 iota[:, 0:TOPK].unsqueeze(1).broadcast_to([P, PH * TOPK, TOPK]),
                                                 ALU.is_equal))
                    settle()
                    pick4 = score[s].rearrange("p (h k j) -> p h k j", h=PH, k=TOPK)
                    mark(nc.vector.tensor_tensor(pick4, pick4,
                                                 top_f[:, :, s, :].unsqueeze(2).broadcast_to([P, PH, TOPK, TOPK]),
                                                 ALU.mult))
                    settle()
                    mark(nc.vector.tensor_reduce(route[:, t, s, :], pick, axis=AX.X, op=ALU.add))
                if t:
                    settle()
                nc.vector.tensor_tensor(gate_e, best_v, best_v[:, :, 0:1].broadcast_to([P, PH, TOPK]),
                                        ALU.subtract).then_inc(gate_shift, 1)
                dve.wait_ge(gate_exp, t + 1)
                mark(nc.vector.tensor_reduce(gate_s, gate_e, axis=AX.X, op=ALU.add))
                settle()
                mark(nc.vector.reciprocal(gate_r, gate_s))
                settle()
                nc.vector.tensor_tensor(route[:, t, 2, :].rearrange("p (h k) -> p h k", h=PH), gate_e,
                                        gate_r.unsqueeze(2).broadcast_to([P, PH, TOPK]), ALU.mult).then_inc(routed, 1)
            dve.wait_ge(routed, TT)

            dve.wait_ge(route_in, 3)

            def one_hots(i, first):
                for k in range(2):
                    if not first:
                        dve.wait_ge(g_full, 2 * i + (k - 1))
                    nc.vector.tensor_tensor(one_a[k], iota[:, 0:P].unsqueeze(1).broadcast_to([P, GT, P]),
                                            routeT[:, 0, bass.ds(2 * GT * i + GT * k, GT)].unsqueeze(2)
                                            .broadcast_to([P, GT, P]), ALU.is_equal).then_inc(oa_ready, 1)
                    for q in range(GT):
                        tok = bass.ds(2 * GT * i + (GT * k + q), 1)
                        last = nc.vector.tensor_scalar(one_b[k][:, q, :], iota[:, 0:P], routeT[:, 1, tok],
                                                       routeT[:, 2, tok], ALU.is_equal, ALU.mult)
                    last.then_inc(ob_ready, 1)

            one_hots(0, True)
            with dve.Fori(1, S // (2 * GT)) as i:
                one_hots(i, False)

            u0 = U_PEER
            dve.wait_ge(g_free, 2 * S // GT)

            def gated(i, off=0, place=None, buffers=None):
                place = 2 * (i if place is None else place)
                gelu, out = buffers or (act_s[i % 2], act_w[i % 2])
                dve.wait_ge(gelu_done, i + 1 + off)
                nc.vector.tensor_tensor(out.rearrange("p (j t) -> p j t", j=2), gelu.rearrange("p (j t) -> p j t", j=2),
                                        G[:, bass.ds(place + 2 * off, 2), :], ALU.mult).then_inc(w_done, 1)
                dve.wait_ge(w_hi, i + 1 + off)
                nc.vector.tensor_tensor(plo[:, i % 2, :], out, phi[:, i % 2, :].bitcast(f32),
                                        ALU.subtract).then_inc(w_lo, 1)

            dve.wait_ge(unit_split, u0 + NE + 2)
            for i in range(NE):
                if i >= 2:
                    lo(u0 + NE + i)
                gated(i, buffers=(early[i], early[i]))
            u1 = u0 + 2 * NE
            lo(u1)
            lo(u1 + 1)
            lo(u1 + 2)
            gated(NE)
            lo(u1 + 3)
            gated(NE + 1)
            lo(u1 + 4)
            for first, count, place in ((NE + 2, NB - NE - 2, NE + 2), (NB, NP - NB, 0)):
                if first == NB:
                    dve.wait_ge(g_loaded, 32 * NB)
                with dve.Fori(0, count // 2) as r:
                    for k in range(2):
                        i = first + k
                        lo(u1 + 2 * (i - NE) + 1, 4 * r)
                        gated(i, 2 * r, place + k)
                        lo(u1 + 2 * (i - NE) + 2, 4 * r)
            used(U_MIX - 1)
            for n in range(4):
                cols = slice(n % 2 * 512, (n % 2 + 1) * 512)
                mark(nc.vector.tensor_tensor(mid[:, n * 512:(n + 1) * 512], ps[:, n, :], g2[:, cols], ALU.mult))
                if n % 2:
                    t = n // 2
                    settle()
                    nc.vector.tensor_tensor(X[:, t, :], X[:, t, :], mid[:, t * D:(t + 1) * D], ALU.add
                                            ).then_inc(x_ready, 1)

            lo(U_MIX + 1)

            dve.wait_ge(x_ready, 2 * TT)
            norm(2, X, rows_ready)
            tr_low(T_MIX)
            mark(nc.vector.tensor_copy(lint, iota[:, 0:P]))
            mark(nc.vector.tensor_scalar(lup, iota[:, 0:P], pidx, None, ALU.is_gt))
            mark(nc.vector.tensor_copy(lmask[:, 7, :], ident[:, :]))
            mark(nc.vector.memset(keep, 1.0))
            settle()
            mark(nc.vector.memset(keep[:, 0:S:SEG], 0.0))
            mark(nc.vector.tensor_scalar(lint, lint, pidx_i, None, ALU.bitwise_xor))
            settle()
            for l in range(LEVELS):
                mark(nc.vector.tensor_scalar(lsh, lint, l, None, ALU.logical_shift_right))
                settle()
                mark(nc.vector.scalar_tensor_tensor(lmask[:, l, :], lsh, 1.0, lup, ALU.is_equal, ALU.mult))
                settle()
            dve.wait_ge(mix_loaded, 48)
            nc.vector.tensor_tensor(lb, lb2[:, RH:2 * RH], lb2[:, 0:RH], ALU.subtract).then_inc(lb_diff, 1)
            dve.wait_ge(lb_exp, 1)
            mark(nc.vector.tensor_scalar(lb, lb, 1.0, None, ALU.add))
            settle()
            mark(nc.vector.reciprocal(lb, lb))
            settle()
            mark(nc.vector.tensor_scalar(omlb, lb, -1.0, 1.0, ALU.mult, ALU.add))
            norm(3, mem, rows_ready)
            for u in range(MIX_T):
                lo(U_MIX + u + 2)
            dve.wait_ge(z_sig, 2)
            settle()
            for h in range(RH):
                last = nc.vector.tensor_scalar(sig[:, h, :], sig[:, h, :], omlb[:, h:h + 1], lb[:, h:h + 1],
                                               ALU.mult, ALU.add)
                if h < RH - 1:
                    mark(last)
            settle()
            last.then_inc(f_ready, 1)
            for h in range(RH):
                mark(nc.vector.tensor_scalar(rk[:, h, :], rk[:, h, :], omlb[:, h:h + 1], None, ALU.mult))
            lo(U_MIX + MIX_T + 2)
            dve.wait_ge(acc_free, N_MT + MIX_T)
            mark(nc.vector.tensor_tensor(conv_u, cc, cx, ALU.mult))
            settle()
            for j in (2, 1, 0):
                for b in range(4):
                    w = conv_w[:, 3 * b + j:3 * b + j + 1]
                    if j == 2:
                        mark(nc.vector.tensor_scalar(conv_y[:, b, :], conv_u[:, b, :], w, None, ALU.mult))
                    else:
                        d = 2 - j
                        mark(nc.vector.scalar_tensor_tensor(conv_y[:, b, d:S], conv_u[:, b, 0:S - d], w,
                                                            conv_y[:, b, d:S], ALU.mult, ALU.add))
                settle()
                if j == 2:
                    lo(U_MIX + MIX_T + 3)
            nc.vector.tensor_tensor(conv_y, conv_y, cb, ALU.mult).then_inc(conv_ready, 1)
            dve.wait_ge(f_log, 1)
            for h in range(RH):
                mark(nc.vector.tensor_tensor_scan(sig[:, h, :], keep, dec[:, h, :], 0.0, ALU.mult, ALU.add))
            settle()
            bsum = sig

            def exponents(l):
                e = lev_e[l % 2]
                if l >= 3:
                    dve.wait_ge(lev_qk, l - 2)
                if l <= 6:
                    c = 1 << (l - 1)
                    v = bsum.rearrange("p h (n s) -> p (h n) s", s=2 * c)
                    o = e.rearrange("p h (n s) -> p (h n) s", s=2 * c)
                    last = nc.vector.tensor_tensor(o, v, v[:, :, c - 1:c].broadcast_to([P, RH * S // (2 * c), 2 * c]),
                                                   ALU.subtract)
                else:
                    v = bsum.rearrange("p h (n s) -> p h n s", s=SEG)
                    o = e.rearrange("p h (n s) -> p h n s", s=SEG)
                    end = v[:, :, :, SEG - 1:SEG]
                    if l == 7:
                        left = slice(0, 4, 2)
                        right = slice(1, 4, 2)
                        mark(nc.vector.tensor_tensor(o[:, :, left, :], v[:, :, left, :],
                                                     end[:, :, left, :].broadcast_to([P, RH, 2, SEG]), ALU.subtract))
                        settle()
                        last = nc.vector.tensor_copy(o[:, :, right, :], v[:, :, right, :])
                    else:
                        left = slice(0, 2)
                        mark(nc.vector.tensor_tensor(o[:, :, left, :], v[:, :, left, :],
                                                     end[:, :, left, :].broadcast_to([P, RH, 2, SEG]), ALU.subtract))
                        mark(nc.vector.tensor_copy(o[:, :, 2, :], v[:, :, 2, :]))
                        mark(nc.vector.tensor_tensor(o[:, :, 3, :], v[:, :, 3, :],
                                                     end[:, :, 2, :].broadcast_to([P, RH, SEG]), ALU.add))
                        settle()
                        last = nc.vector.tensor_tensor(o[:, :, 0, :], o[:, :, 0, :],
                                                       end[:, :, 1, :].broadcast_to([P, RH, SEG]), ALU.subtract)
                last.then_inc(lev_d, 1)

            def decayed(l):
                dve.wait_ge(lev_exp, l)
                dve.wait_ge(lev_full, l)
                mark(nc.vector.tensor_tensor(lev_k, rk, lev_e[l % 2], ALU.mult))
                settle()
                nc.vector.tensor_tensor(lev_q, hq, lev_e[l % 2], ALU.mult).then_inc(lev_qk, 1)

            def collect(l):
                dve.wait_ge(lev_full, l + 1)
                bank = 4 + 2 * (l % 2)
                if l == LEVELS + 1:
                    nc.vector.tensor_copy(rsc_x, ps[:, bank, :].rearrange("p (h n) -> p h n", h=RH)
                                          ).then_inc(lev_free, 1)
                    return
                m = lmask[:, (l - 1) % 8, :].unsqueeze(1).broadcast_to([P, RH, P])
                if l:
                    dve.wait_ge(lev_free, TT * l)
                for t in range(TT):
                    got = ps[:, bank + t, :].rearrange("p (h n) -> p h n", h=RH)
                    if l == 0:
                        last = nc.vector.tensor_tensor(rsc[:, t, :, :], got, m, ALU.mult)
                    else:
                        last = nc.vector.copy_predicated(rsc[:, t, :, :], m.bitcast(u32), got)
                    last.then_inc(lev_free, 1)

            exponents(1)
            lo(U_KV)
            lo(U_KV + 1)
            tr_low(T_MEM)
            for l in range(1, LEVELS + 2):
                if l <= LEVELS:
                    exponents(l + 1)
                decayed(l)
                collect(l - 1)
                if l == 1:
                    dve.wait_ge(conv_hi, 1)
                    nc.vector.tensor_tensor(conv_plo, conv_y, conv_phi.bitcast(f32), ALU.subtract).then_inc(conv_lo, 1)
                else:
                    lo(U_KV + l)
            collect(LEVELS + 1)
            lo(U_KV + LEVELS + 2)
            dve.wait_ge(ro_sq, 1)
            rst = r_stat[:, 0:TT * RH]
            mark(nc.vector.tensor_reduce(rst, lev_q.rearrange("p b t -> p (b t)").rearrange("p (h d) -> p h d", d=P),
                                         axis=AX.X, op=ALU.add))
            mark(nc.vector.tensor_tensor(hg, hg, hnorm.unsqueeze(1).broadcast_to([P, TT, CW]), ALU.mult))
            root_mean(rst, P, (dve_chain, chain[0]), ro_ms, ro_std, 1)
            rov = ro.rearrange("p t (h d) -> p (t h) d", d=P)
            mark(nc.vector.tensor_tensor(rov, rov, rst.unsqueeze(2).broadcast_to([P, TT * RH, P]), ALU.mult))
            settle()
            for t in range(TT):
                nc.vector.tensor_tensor(H[:, t, 0:CW], ro[:, t, :], hg[:, t, :], ALU.mult).then_inc(rows_ready, 1)
            tr_low(T_YB, 4)

            def residual(n0, u0):
                for b in range(2):
                    lo(u0 + 2 * b + 2)
                    for t in range(TT):
                        n = n0 + 2 * b + t
                        used(u0 + 2 * b + 1)
                        cols = slice(b * 512, (b + 1) * 512)
                        nc.vector.tensor_tensor(X[:, t, cols], X[:, t, cols], ps[:, n % 4, :],
                                                ALU.add).then_inc(acc_free, 1)
                    lo(u0 + 2 * b + 3)

            residual(N_W2, U_WO2)

            norm(4, X, rows_ready)
            tr_low(T_HX)
            for u in range(4):
                lo(U_XQ + u + 2)
            def x_maxima(i):
                b = i % 2
                dve.wait_ge(x_scored, i + 1)
                mark(nc.vector.tensor_reduce(x_max[:, b:b + 1], ps[:, b, 0:S], axis=AX.X, op=ALU.max))
                settle()
                nc.vector.tensor_scalar(x_max[:, b:b + 1], x_max[:, b:b + 1], -(XD ** -0.5), None,
                                        ALU.mult).then_inc(x_bias, 1)

            def x_low(h):
                dve.wait_ge(xo_hi, h + 1)
                nc.vector.tensor_tensor(tlo[:, 2 * h:2 * h + 2, :],
                                        ps[:, 6 + h % 2, :].rearrange("p (c t) -> p c t", c=2),
                                        thi[:, 2 * h:2 * h + 2, :].bitcast(f32), ALU.subtract).then_inc(xo_lo, 1)

            x_maxima(0)
            for i in range(XH * TT):
                b, h, t = i % 2, i // TT, i % TT
                if i + 1 < XH * TT:
                    x_maxima(i + 1)
                dve.wait_ge(x_prob, i + 1)
                mark(nc.vector.reciprocal(x_rec[:, b:b + 1], x_sum[:, b:b + 1]))
                settle()
                nc.vector.tensor_scalar(x_p[b], x_p[b], x_rec[:, b:b + 1], None, ALU.mult).then_inc(x_norm, 1)
                if t == TT - 1 and h:
                    x_low(h - 1)
            x_low(XH - 1)
            residual(N_XO, U_XO)

            dve.wait_ge(wr_hi, 1)
            nc.vector.tensor_tensor(wrlo[:, :, :], wr, wrhi[:, :, :].bitcast(f32), ALU.subtract).then_inc(wr_lo, 1)
            norm(5, X, rows_ready)
            tr_low(T_HF)
            dve.wait_ge(r_full, 1)
            for t in range(TT):
                mark(nc.vector.tensor_tensor(r_log[:, t, :], ps[:, t, 0:20], r_bias, ALU.add))
            settle()
            NG5 = N_GRP + 1
            lv = r_log.rearrange("p t (g a) -> p (t g) a", a=4)
            pv5 = r_prob.rearrange("p t (g a) -> p (t g) a", a=4)
            st = big[:, 9216:9216 + TT * NG5]
            mark(nc.vector.tensor_reduce(st, lv, axis=AX.X, op=ALU.max))
            settle()
            nc.vector.tensor_tensor(lv, lv, st.unsqueeze(2).broadcast_to([P, TT * NG5, 4]),
                                    ALU.subtract).then_inc(r_ready, 1)
            for a in range(4):
                mark(nc.vector.tensor_scalar(r_low[:, a, :], iota[:, 0:4], float(a), None, ALU.is_lt))
            dve.wait_ge(r_exp, 1)
            mark(nc.vector.tensor_reduce(st, pv5, axis=AX.X, op=ALU.add))
            settle()
            mark(nc.vector.reciprocal(st, st))
            settle()
            mark(nc.vector.tensor_tensor(pv5, pv5, st.unsqueeze(2).broadcast_to([P, TT * NG5, 4]), ALU.mult))
            settle()
            cmp3 = r_cmp.rearrange("p t g a b -> p (t g) a b")
            tie3 = r_tie.rearrange("p t g a b -> p (t g) a b")
            own = pv5.unsqueeze(3).broadcast_to([P, TT * NG5, 4, 4])
            other = pv5.unsqueeze(2).broadcast_to([P, TT * NG5, 4, 4])
            mark(nc.vector.tensor_tensor(cmp3, other, own, ALU.is_gt))
            mark(nc.vector.tensor_tensor(tie3, other, own, ALU.is_equal))
            settle()
            mark(nc.vector.tensor_tensor(tie3, tie3, r_low.unsqueeze(1).broadcast_to([P, TT * NG5, 4, 4]), ALU.mult))
            settle()
            mark(nc.vector.tensor_tensor(cmp3, cmp3, tie3, ALU.add))
            settle()
            rank = r_rank.rearrange("p t (g a) -> p (t g) a", a=4)
            mark(nc.vector.tensor_reduce(rank, cmp3, axis=AX.X, op=ALU.add))
            settle()
            mark(nc.vector.scalar_tensor_tensor(r_sel[:, :, 0:4], r_rank[:, :, 0:4], 0.5, r_prob[:, :, 0:4],
                                                ALU.is_lt, ALU.mult))
            mark(nc.vector.scalar_tensor_tensor(r_sel[:, :, 4:20], r_rank[:, :, 4:20], 1.5, r_prob[:, :, 4:20],
                                                ALU.is_lt, ALU.mult))
            settle()
            for t in range(TT):
                es = r_sel[:, t, 4:20].rearrange("p (g a) -> p g a", a=4)
                esum = big[:, 9248 + 4 * t:9252 + 4 * t]
                mark(nc.vector.tensor_reduce(esum, es, axis=AX.X, op=ALU.add))
                settle()
                mark(nc.vector.reciprocal(esum, esum))
                settle()
                mark(nc.vector.tensor_tensor(esum, esum, r_sel[:, t, 0:4], ALU.mult))
                settle()
                mark(nc.vector.tensor_tensor(comb[:, t, :].rearrange("p (g a) -> p g a", a=4), es,
                                             esum.unsqueeze(2).broadcast_to([P, N_GRP, 4]), ALU.mult))
            settle()

            def expert(u, off, uoff, last, e):
                for j in range(2):
                    lo(u + 2 * j + 2, uoff)
                    dve.wait_ge(m_silu, j + 1 + 2 * off)
                    used(u + 2 * j + 1, uoff)
                    nc.vector.tensor_tensor(hid[j], silu_g[j], ps[:, 5 + 2 * j, :], ALU.mult).then_inc(m_hid, 1)
                    lo(u + 2 * j + 3, uoff)
                    dve.wait_ge(m_hi, j + 1 + 2 * off)
                    nc.vector.tensor_tensor(plo[:, j, :], hid[j], phi[:, j, :].bitcast(f32),
                                            ALU.subtract).then_inc(m_lo, 1)
                if not last:
                    lo(u + 6, uoff)
                used(u + 5, uoff)
                for h in range(2):
                    if h and not last:
                        lo(u + 7, uoff)
                    for t in range(TT):
                        cols = slice(h * 512, (h + 1) * 512)
                        nc.vector.scalar_tensor_tensor(X[:, t, cols], ps[:, 2 * h + t, :], comb[:, t, e], X[:, t, cols],
                                                       ALU.mult, ALU.add).then_inc(d_free, 1)

            with dve.Fori(0, N_EXP - 1) as e:
                expert(U_MOE, e, 6 * e, False, bass.ds(e, 1))
                dve.wait_ge(d_free, 4 * e + 4)
            expert(U_MOE + 6 * (N_EXP - 1), N_EXP - 1, 0, True, slice(N_EXP - 1, N_EXP))
            dve.wait_ge(d_free, 4 * N_EXP)
            norm(6, X, out_ready)

        @block.tensor
        def _(pe):
            def mm3(out, ahi, alo, bhi, blo, start, stop):
                nc.tensor.matmul(out, ahi, bhi, start=start, stop=False)
                nc.tensor.matmul(out, ahi, blo, start=False, stop=False)
                return nc.tensor.matmul(out, alo, bhi, start=False, stop=stop)

            def arrived(u, off=0):
                pe.wait_ge(unit_split, u + 1 + off)

            def free_bank(n, off=0):
                if n >= 4:
                    pe.wait_ge(acc_free, n - 3 + off)

            def transposes(t, src):
                if t == T_OA:
                    pe.wait_ge(a_out, A_SLOTS * TT)
                for k in range(T_GROUPS[t]):
                    g = T_BASE[t] + k
                    chunks, tokens = tr_place(t, k)
                    if t != T_OA:
                        pe.wait_ge(rows_ready, ROWS[t] - TT + tokens.start // P + 1)
                    if g >= 2:
                        pe.wait_ge(tr_lo, g - 1)
                    blocks = [(c, tt) for c in range(chunks.start, chunks.stop)
                              for tt in range(tokens.start // P, tokens.stop // P)]
                    for n, (c, tt) in enumerate(blocks):
                        last = nc.tensor.transpose(ps[:, 4 + g % 2, n * P:(n + 1) * P],
                                                   src[:, tt, c * P:(c + 1) * P], ident[:, :])
                    last.then_inc(tr_done, 1)

            def split_rows(t):
                pe.wait_ge(tr_lo, T_BASE[t + 1])

            def rows_of(c, rows):
                return thi[:, c, rows], tlo[:, c, rows]

            def block_rows(n, u, off=0, uoff=0, at=None, units=(0, 1), source=rows_of):
                for t in range(TT):
                    if 0 in units:
                        free_bank(n + t, off)
                for k in units:
                    arrived((u if at is None else at) + k, uoff)
                    s = (u + k) % 2
                    for t in range(TT):
                        for c in range(4):
                            rows = slice(t * P, (t + 1) * P)
                            cols = slice(c * 512, (c + 1) * 512)
                            ahi, alo = source(4 * k + c, rows)
                            last = mm3(ps[:, (n + t) % 4, :], ahi, alo, whi[:, s, cols], wlo[:, s, cols],
                                       k == 0 and c == 0, k == 1 and c == 3)
                    last.then_inc(unit_used, 1)

            def block_T(out, u, uoff=0):
                arrived(u, uoff)
                s = u % 2
                for fb in range(2):
                    for c in range(DC):
                        cols = slice(c * 256 + fb * P, c * 256 + (fb + 1) * P)
                        last = mm3(out[:, fb * S:(fb + 1) * S], whi[:, s, cols], wlo[:, s, cols],
                                   thi[:, c, :], tlo[:, c, :], c == 0, c == DC - 1)
                last.then_inc(unit_used, 1)

            def group_T(n, u):
                free_bank(n)
                block_T(ps[:, n % 4, :], u)

            def ada_sums(g, units):
                pe.wait_ge(unit_split, units)
                for m in range(4):
                    last = nc.tensor.matmul(ps[:, ada_bank(g) + m, :], ones, ada_acc[g][:, m * 512:(m + 1) * 512],
                                            start=True, stop=True)
                last.then_inc(ada_full, 1)

            pe.wait_ge(ones_ready, 1)
            ada_sums(0, DC)

            pe.wait_ge(consts_ready, 3)
            transposes(T_H1, H)
            split_rows(T_H1)
            for b in range(2):
                block_rows(2 * b, U_IN + 2 * b, at=in_at(2 * b))
            with pe.Fori(0, (IN_BLOCKS - 2) // 2) as i:
                for b in range(2, 4):
                    block_rows(2 * b, U_IN + 2 * b, 4 * i, 4 * i, in_at(2 * b))
            u = U_PA - 1
            arrived(in_at(u - U_IN))
            for t in range(TT):
                n = N_PA - 2 + t
                free_bank(n)
                for c in range(DC):
                    rows = slice(t * P, (t + 1) * P)
                    cols = slice(c * 256, (c + 1) * 256)
                    last = mm3(ps[:, n % 4, 0:256], thi[:, c, rows], tlo[:, c, rows], whi[:, u % 2, cols],
                               wlo[:, u % 2, cols], c == 0, c == DC - 1)
            last.then_inc(unit_used, 1)

            pe.wait_ge(rope_done, TT)
            pe.wait_ge(gate_biased, TT)
            for g in range(NQK // 4 * TT):
                t, b4 = g % TT, g // TT
                if g >= 4:
                    pe.wait_ge(qkT_odd if g % 2 else qkT_even, g // 2 - 1)
                for b in range(4):
                    last = nc.tensor.transpose(ps[:, 4 + g % 4, b * P:(b + 1) * P],
                                               proj[:, t, (4 * b4 + b) * P:(4 * b4 + b + 1) * P], ident[:, :])
                last.then_inc(qkT_done, 1)
            pe.wait_ge(qkT_even, NQK // 4 * TT // 2)
            pe.wait_ge(qkT_odd, NQK // 4 * TT // 2)

            def a_groups(t):
                return (0, 1, 2) if t == 0 else (1, 2, 0)

            def a_scores(i):
                t, h, b = i // A_SLOTS, i % A_SLOTS, i % 2
                if i >= 2:
                    pe.wait_ge(a_masked, i - 1)
                sc = ps[:, 2 * b:2 * b + 2, :].rearrange("p a n -> p (a n)")
                for k, g in enumerate(a_groups(t)):
                    hd = g * A_SLOTS + h
                    part = slice(HD * (hd % 2), HD * (hd % 2) + HD)
                    last = nc.tensor.matmul(sc[:, k * S:(k + 1) * S], qkT[part, hd // 2, t * P:(t + 1) * P],
                                            qkT[part, 6 + hd // 2, :], start=True, stop=True)
                last.then_inc(a_scored, 1)

            def a_transposes(i):
                b = i % 2
                pe.wait_ge(a_prob, i + 1)
                if i:
                    pe.wait_ge(a_trT, i)
                trp = ps[:, 4:6, :].rearrange("p a n -> p (a n)")
                for k in range(6):
                    last = nc.tensor.transpose(trp[:, k * P:(k + 1) * P], a_s[b][:, k * P:(k + 1) * P], ident[:, :])
                last.then_inc(a_tr, 1)

            def a_values(i):
                t, h, b = i // A_SLOTS, i % A_SLOTS, i % 2
                if i >= 2:
                    pe.wait_ge(a_out, i - 1)
                pe.wait_ge(a_trT, i + 1)
                for k in range(6):
                    hd = a_groups(t)[k // 2] * A_SLOTS + h
                    last = nc.tensor.matmul(ps[:, 6 + b, 0:HD], a_pT[b][:, k * P:(k + 1) * P],
                                            proj[:, k % 2, V0 + hd * HD:V0 + (hd + 1) * HD], start=k == 0, stop=k == 5)
                last.then_inc(a_pv, 1)

            n_a = A_SLOTS * TT
            a_scores(0)
            a_scores(1)
            for i in range(n_a):
                a_transposes(i)
                if i + 2 < n_a:
                    a_scores(i + 2)
                if i:
                    a_values(i - 1)
            a_values(n_a - 1)

            def b_scores(h):
                if h >= 2:
                    pe.wait_ge(b_prob, 4 * (h - 1))
                elif h == 0:
                    pe.wait_ge(a_masked, n_a)
                for m in range(2):
                    part = slice(HD * m, HD * m + HD)
                    for t in range(TT):
                        last = nc.tensor.matmul(ps[:, 2 * (h % 2) + m, t * S:(t + 1) * S],
                                                qkT[part, 12 + h, t * P:(t + 1) * P],
                                                qkT[part, 20 + h, :], start=True, stop=True)
                last.then_inc(b_scored, 1)

            def b_transposes(h):
                pe.wait_ge(b_mix, TT * (h + 1))
                if h >= 2:
                    pe.wait_ge(b_trT, h - 1)
                elif h == 0:
                    pe.wait_ge(a_trT, n_a)
                for t in range(TT):
                    for k in range(2):
                        last = nc.tensor.transpose(ps[:, 4 + h % 2, (2 * t + k) * P:(2 * t + k + 1) * P],
                                                   b_p[h % 2][:, t * S + k * P:t * S + (k + 1) * P], ident[:, :])
                last.then_inc(b_tr, 1)

            def b_values(h):
                if h >= 2:
                    pe.wait_ge(b_out, h - 1)
                elif h == 0:
                    pe.wait_ge(a_out, n_a)
                pe.wait_ge(b_trT, h + 1)
                for t in range(TT):
                    for k in range(2):
                        last = nc.tensor.matmul(ps[:, 6 + h % 2, t * P:(t + 1) * P],
                                                b_pT[h % 2][:, (2 * t + k) * P:(2 * t + k + 1) * P],
                                                proj[:, k, V0 + A_W + h * P:V0 + A_W + (h + 1) * P],
                                                start=k == 0, stop=k == 1)
                last.then_inc(b_pv, 1)

            b_scores(0)
            b_scores(1)
            pe.wait_ge(a_trT, n_a)
            pe.wait_ge(a_out, n_a)
            ada_sums(1, U_PA - DC)
            pe.wait_ge(ada_free, 4 * 2)
            for h in range(B_HEADS):
                b_transposes(h)
                if h:
                    b_values(h - 1)
                if h + 2 < B_HEADS:
                    b_scores(h + 2)
            b_values(B_HEADS - 1)

            ada_sums(2, U_PA)

            pe.wait_ge(ada_free, 4 * ADA_GROUPS)
            pe.wait_ge(b_trT, B_HEADS)
            transposes(T_OA, oa)
            split_rows(T_OA)
            arrived(U_PA)
            for n in range(4):
                t, h = n // 2, n % 2
                free_bank(N_PA + n)
                for c in range(2):
                    cols = slice(c * D + h * 512, c * D + (h + 1) * 512)
                    rows = slice(t * P, (t + 1) * P)
                    last = mm3(ps[:, (N_PA + n) % 4, :], thi[:, c, rows], tlo[:, c, rows], whi[:, U_PA % 2, cols],
                               wlo[:, U_PA % 2, cols], c == 0, c == 1)
            last.then_inc(unit_used, 1)
            transposes(T_OB, H)
            split_rows(T_OB)
            for b in range(2):
                block_rows(N_PB + 2 * b, U_PB + 2 * b)
            transposes(T_MIXED, H)
            split_rows(T_MIXED)
            for b in range(2):
                block_rows(N_WO + 2 * b, U_WO + 2 * b)

            transposes(T_H2, H)
            split_rows(T_H2)
            def head_scores(h):
                if h == 0:
                    pe.wait_ge(keys_loaded, 16)
                pe.wait_ge(acc_free, n_query(h) + 1)
                free_bank(n_scores(h))
                for t in range(TT):
                    for k in range(2):
                        last = nc.tensor.matmul(ps[:, n_scores(h) % 4, (2 * t + k) * P:(2 * t + k + 1) * P],
                                                qT[:, 2 * h + k, t * P:(t + 1) * P], keysT[:, 2 * h + k, :],
                                                start=True, stop=True)
                last.then_inc(keys_scored, 1)

            for h in range(PH):
                group_T(n_query(h), U_WQ + h)
                if h:
                    head_scores(h - 1)
            head_scores(PH - 1)

            u0 = U_PEER

            def scores_of(i, u, off=0, uoff=0):
                if i >= 2:
                    pe.wait_ge(gelu_done, i - 1 + off)
                block_T(ps[:, 4 + i % 2, :], u, uoff)

            for i in range(NE):
                scores_of(i, u0 + i)
            pe.wait_ge(gelu_done, NE)
            pe.wait_ge(routed, TT)
            for q in range(3):
                if q == 2:
                    pe.wait_ge(route_in, 1)
                for t in range(TT):
                    last = nc.tensor.transpose(ps[:, 4 + q % 2, t * P:(t + 1) * P], route[:, t, q, :], ident[:, :])
                last.then_inc(route_tr, 1)

            pe.wait_ge(route_in, 3)

            def gates(i, first):
                for k in range(2):
                    pe.wait_ge(oa_ready, 2 * i + (k + 1))
                    pe.wait_ge(ob_ready, 2 * i + (k + 1))
                    if not first:
                        pe.wait_ge(g_free, 4 * i + 2 * (k - 1))
                    out = ps[:, 4 + 2 * k:6 + 2 * k, :].rearrange("p a n -> p (a n)")
                    for q in range(GT):
                        last = nc.tensor.matmul(out[:, q * N_KEYS:(q + 1) * N_KEYS], one_a[k][:, q, :],
                                                one_b[k][:, q, :], start=True, stop=True)
                    last.then_inc(g_full, 1)

            gates(0, True)
            with pe.Fori(1, S // (2 * GT)) as i:
                gates(i, False)

            pe.wait_ge(g_free, 2 * S // GT)

            def values_of(i, u, off=0, uoff=0):
                arrived(u, uoff)
                pe.wait_ge(w_lo, i + 1 + off)
                for j in range(2):
                    for t in range(TT):
                        for h in range(2):
                            rows = slice(j * S + t * P, j * S + (t + 1) * P)
                            cols = slice(j * D + h * 512, j * D + (h + 1) * 512)
                            last = mm3(ps[:, 2 * t + h, :], phi[:, i % 2, rows], plo[:, i % 2, rows],
                                       whi[:, u % 2, cols], wlo[:, u % 2, cols],
                                       i == 0 and j == 0, i == NP - 1 and j == 1)
                last.then_inc(unit_used, 1)

            for i in range(NE):
                values_of(i, u0 + NE + i)
            u1 = u0 + 2 * NE
            scores_of(NE, u1)
            scores_of(NE + 1, u1 + 1)
            values_of(NE, u1 + 2)
            with pe.Fori(0, (NP - NE - 2) // 2) as r:
                for k in (1, 2):
                    scores_of(NE + k + 1, u1 + 2 * k + 1, 2 * r, 4 * r)
                    values_of(NE + k, u1 + 2 * k + 2, 2 * r, 4 * r)
            values_of(NP - 1, u0 + 2 * NP - 1)

            transposes(T_MIX, H)
            split_rows(T_MIX)
            for u in range(MIX_T):
                group_T(N_MT + u, U_MIX + u)
            for b in range(2):
                block_rows(N_MV + 2 * b, U_MIX + MIX_T + 2 * b)
            transposes(T_MEM, H)
            split_rows(T_MEM)
            for l in range(LEVELS + 2):
                qs, ks = (hq, rk) if l == 0 else (lev_q, lev_k)
                if l == 0:
                    pe.wait_ge(acc_free, N_K)
                    pe.wait_ge(conv_ready, 1)
                else:
                    pe.wait_ge(lev_qk, l)
                    if l >= 2:
                        pe.wait_ge(lev_free, TT * (l - 1))
                for t in range(1 if l == LEVELS + 1 else TT):
                    for h in range(RH):
                        kt, qt = (0, 1) if l == LEVELS + 1 else (t, t)
                        last = nc.tensor.matmul(ps[:, 4 + 2 * (l % 2) + t, h * P:(h + 1) * P],
                                                ks[:, h, kt * P:(kt + 1) * P], qs[:, h, qt * P:(qt + 1) * P],
                                                start=True, stop=True)
                last.then_inc(lev_full, 1)
                if l < 4:
                    group_T(N_K + l, U_KV + l)
                elif l < 8:
                    b = (l - 4) // 2
                    block_rows(N_V + 2 * b, U_KV + 4 + 2 * b, units=(l % 2,))
            pe.wait_ge(lev_free, TT * (LEVELS + 1) + 1)
            for t in range(TT):
                for h in range(RH):
                    cols = slice(h * P, (h + 1) * P)
                    if t:
                        nc.tensor.matmul(ps[:, 4 + t, cols], rsc_x[:, h, :], hv[:, 0, cols], start=True, stop=False)
                    last = nc.tensor.matmul(ps[:, 4 + t, cols], rsc[:, t, h, :], hv[:, t, cols], start=t == 0, stop=True)
                last.then_inc(ro_full, 1)

            def mixed_rows(c, rows):
                at = slice((c % 2) * S + rows.start, (c % 2) * S + rows.stop)
                return (phi[:, c // 2, at], plo[:, c // 2, at]) if c < 4 else rows_of(c, rows)

            pe.wait_ge(conv_lo, 1)
            transposes(T_YB, H)
            split_rows(T_YB)
            for b in range(2):
                block_rows(N_W2 + 2 * b, U_WO2 + 2 * b, source=mixed_rows)

            transposes(T_HX, H)
            split_rows(T_HX)
            for u in range(4):
                group_T(N_XQ + u, U_XQ + u)
            pe.wait_ge(acc_free, N_XO)

            def x_scores(i):
                h, t = i // TT, i % TT
                if i >= 2:
                    pe.wait_ge(x_prob, i - 1)
                for c in range(2):
                    last = nc.tensor.matmul(ps[:, i % 2, 0:S], xqT[:, 2 * h + c, t * P:(t + 1) * P], kT[:, 2 * h + c, :],
                                            start=c == 0, stop=c == 1)
                last.then_inc(x_scored, 1)

            def x_values(h):
                pe.wait_ge(x_trT, TT * (h + 1))
                if h >= 2:
                    pe.wait_ge(xo_lo, h - 1)
                for c in range(2):
                    for k in range(TT):
                        cols = slice(h * XD + c * P, h * XD + (c + 1) * P)
                        last = nc.tensor.matmul(ps[:, 6 + h % 2, c * S:(c + 1) * S], vm[:, k, cols],
                                                x_pT[h % 2][:, k, :], start=k == 0, stop=k == TT - 1)
                last.then_inc(xo_full, 1)

            x_scores(0)
            x_scores(1)
            for i in range(XH * TT):
                h, t = i // TT, i % TT
                pe.wait_ge(x_norm, i + 1)
                if i >= 2:
                    pe.wait_ge(x_trT, i - 1)
                for k in range(TT):
                    last = nc.tensor.transpose(ps[:, 4 + i % 2, k * P:(k + 1) * P], x_p[i % 2][:, k * P:(k + 1) * P],
                                               ident[:, :])
                last.then_inc(x_tr, 1)
                if i + 2 < XH * TT:
                    x_scores(i + 2)
                if t == TT - 1 and h:
                    x_values(h - 1)
            x_values(XH - 1)
            pe.wait_ge(xo_lo, XH)
            for b in range(2):
                block_rows(N_XO + 2 * b, U_XO + 2 * b)

            transposes(T_HF, H)
            split_rows(T_HF)
            pe.wait_ge(wr_lo, 1)
            pe.wait_ge(acc_free, N_XO + 4)
            for t in range(TT):
                for c in range(DC):
                    rows = slice(t * P, (t + 1) * P)
                    last = mm3(ps[:, t, 0:20], thi[:, c, rows], tlo[:, c, rows], wrhi[:, c, :], wrlo[:, c, :],
                               c == 0, c == DC - 1)
            last.then_inc(r_full, 1)

            def expert(u, off, uoff, first):
                for j in range(2):
                    for k in range(2):
                        block_T(ps[:, 4 + 2 * j + k, :], u + 2 * j + k, uoff)
                if not first:
                    pe.wait_ge(d_free, 4 * off)
                for j in range(2):
                    s = (u + 4 + j) % 2
                    arrived(u + 4 + j, uoff)
                    pe.wait_ge(m_lo, j + 1 + 2 * off)
                    for c in range(2):
                        for t in range(TT):
                            for h in range(2):
                                rows = slice(c * S + t * P, c * S + (t + 1) * P)
                                cols = slice(c * D + h * 512, c * D + (h + 1) * 512)
                                last = mm3(ps[:, 2 * h + t, :], phi[:, j, rows], plo[:, j, rows], whi[:, s, cols],
                                           wlo[:, s, cols], j == 0 and c == 0, j == 1 and c == 1)
                    last.then_inc(unit_used, 1)

            pe.wait_ge(r_ready, 1)
            expert(U_MOE, 0, 0, True)
            with pe.Fori(1, N_EXP) as e:
                expert(U_MOE, e, 6 * e, False)


def _stream(i):
    import numpy as np

    def rows(w):
        k, n = w.shape
        return w.reshape(2, 4, P, n // 512, 512).transpose(3, 0, 2, 1, 4).reshape(-1, P, UW)

    def cols(w):
        return w.reshape(DC, P, w.shape[1] // 256, 256).transpose(2, 1, 0, 3).reshape(-1, P, UW)

    ada = i["w_ada"][0].reshape(DC, P, ADA_GROUPS, UW).transpose(2, 0, 1, 3).reshape(-1, P, UW)
    w = i["w_in"][0]
    qa_ka, va = w[:, 0:2 * A_W], w[:, 2 * A_W:3 * A_W]
    b0 = 3 * A_W
    qb_kb, vb, gl = w[:, b0:b0 + 2 * D], w[:, b0 + 2 * D:b0 + 3 * D], w[:, b0 + 3 * D:]
    w = np.concatenate([qa_ka, qb_kb, gl, va, vb], axis=1)
    full = 512 * IN_BLOCKS
    pa = i["w_proj_a"][0].reshape(2, P, D).transpose(1, 0, 2).reshape(1, P, UW)
    eu = i["expert_u"][0].reshape(P, NP, 2, DC, P).transpose(1, 4, 3, 2, 0).reshape(NP, P, UW)
    ev = i["expert_v"][0].reshape(P, NP, 2, D).transpose(1, 0, 2, 3).reshape(NP, P, UW)
    peer = [eu[:NE], ev[:NE], eu[NE:NE + 1], np.stack([eu[NE + 1:], ev[NE:-1]], axis=1).reshape(-1, P, UW), ev[-1:]]
    w2 = i["w_in_2"][0]
    wkv = i["w_kv_2"][0]
    moe = []
    for e in range(N_EXP):
        g, u = cols(i["w_gate_2"][0, e]), cols(i["w_up_2"][0, e])
        d = i["w_down_2"][0, e].reshape(2, 2, P, D).transpose(0, 2, 1, 3).reshape(2, P, UW)
        moe += [g[:1], u[:1], g[1:], u[1:], d]
    w_in = np.concatenate([rows(w[:, :full]), cols(w[:, full:])], axis=0)
    return np.concatenate([
        ada[:DC], w_in, ada[DC:], pa, rows(i["w_proj_b"][0]), rows(i["w_out"][0]),
        cols(i["w_query"][0]), *peer, cols(w2[:, :5 * CW]), rows(w2[:, 5 * CW:]),
        cols(wkv[:, :D]), rows(wkv[:, D:]), rows(i["w_out_2"][0]), cols(i["w_q_2"][0]), rows(i["w_o_2"][0]), *moe], axis=0)


def kernel(**inputs):
    import numpy as np
    import concourse.bacc as _bacc
    from concourse import mybir as _mybir
    from concourse.bass_utils import run_bass_kernel_spmd as _run

    i = {k: np.asarray(v) for k, v in inputs.items()}
    arrays = {
        "stream": _stream(i),
        "x": i["x"][0], "c": i["c"][0].reshape(DC, P).T,
        "positions": i["positions"][0].reshape(TT, P).T, "b_ada": i["b_ada"][0],
        "gains": np.concatenate([i["norm1_g"], i["norm2_g"], i["mix_norm_2"], i["mem_norm_2"], i["xattn_norm_2"],
                                 i["ffn_norm_2"], i["final_norm_2"][None]], axis=0),
        "lam": np.concatenate([i["lam_q1"], i["lam_k1"], i["lam_q2"], i["lam_k2"]], axis=0),
        "qk_gain": np.concatenate([i["qn_a"], i["kn_a"], i["qn_b"], i["kn_b"]], axis=0),
        "subln": i["subln_g"][0], "b_gate": i["b_gate"][0],
        "inv_freq": (1.0 / (10000.0 ** (np.arange(0, HD, 2, dtype=np.float32) / HD))).astype(np.float32),
        "keysT": i["sub_keys"][0].transpose(3, 0, 1, 2).reshape(P, NHH * N_KEYS),
        "conv_w": i["conv_w_2"][0].reshape(3, 4, P).transpose(2, 1, 0).reshape(P, 12),
        "hgrn_lb": i["hgrn_lb_2"].reshape(2, RH, P).transpose(2, 0, 1).reshape(P, 2 * RH),
        "hgrn_norm": i["hgrn_norm_2"][0], "mem": i["mem_2"][0],
        "router": np.concatenate([i["w_group_2"][0], i["w_expert_2"][0]], axis=1).reshape(DC, P, 20)
                    .transpose(1, 0, 2).reshape(P, DC * 20),
        "router_b": np.concatenate([i["b_group_2"][0], i["b_expert_2"][0]], axis=0),
    }
    nc = _bacc.Bacc("TRN2", target_bir_lowering=False, num_devices=1)
    io, feeds = {}, {}
    for name, a in arrays.items():
        feeds[f"in_{name}_dram"] = np.ascontiguousarray(a)
        io[name] = nc.dram_tensor(f"in_{name}_dram", a.shape, _mybir.dt.from_np(a.dtype), kind="ExternalInput").ap()
    io["out"] = nc.dram_tensor("out_dram", (S, D), _mybir.dt.float32, kind="ExternalOutput").ap()
    hybrid_block_then_mixer_memory_moe_kernel(nc, io)
    r = _run(nc, [feeds], core_ids=[0])
    return r.results[0]["out_dram"].reshape(1, S, D)
```
